# Optimizing a Trainium2 kernel written in Bass

```python
import math
import jax, jax.numpy as jnp
from jax import lax
import numpy as np
import jax
import jax.numpy as jnp

D_MODEL = 1024
BATCH = 1
SEQ = 512
DEPTH = 2

GRID_W = 64
D_MIX = D_MODEL
ATTN_WIDTH = D_MIX // 2
SSD_WIDTH = D_MIX - ATTN_WIDTH
HEAD_DIM = 64
N_Q_HEADS = ATTN_WIDTH // HEAD_DIM
N_KV_HEADS = 2
KV_WIDTH = N_KV_HEADS * HEAD_DIM
Q_BLOCK = 128
ROPE_THETA = 10000.0
ROPE_AXIS_DIM = HEAD_DIM // 2
SSD_HEAD_DIM = 64
SSD_HEADS = SSD_WIDTH // SSD_HEAD_DIM
SSD_GROUPS = 2
D_STATE = 128
D_CONV = 5
CONV_PAD = D_CONV // 2
CHUNK = 128
CONV_CH = SSD_WIDTH + 2 * SSD_GROUPS * D_STATE
DT_MIN = 0.001
DT_MAX = 0.1
D_IN_PROJ = ATTN_WIDTH + 2 * KV_WIDTH + SSD_WIDTH + CONV_CH + 2 * SSD_HEADS
D_FF = -(-8 * D_MODEL // (3 * 256)) * 256
EPS = 1e-6


def rms_norm(x, w):
    xf = x.astype(jnp.float32)
    y = xf * lax.rsqrt(jnp.mean(xf * xf, axis=-1, keepdims=True) + EPS)
    return (y * w.astype(jnp.float32)).astype(x.dtype)

def _rot_half(x, cos, sin):
    x1, x2 = jnp.split(x, 2, axis=-1)
    return jnp.concatenate([x1 * cos - x2 * sin, x2 * cos + x1 * sin], axis=-1)

def axial_rope(x, cos_r, sin_r, cos_c, sin_c):
    xr, xc = jnp.split(x, 2, axis=-1)
    return jnp.concatenate([_rot_half(xr, cos_r, sin_r), _rot_half(xc, cos_c, sin_c)], axis=-1)

def axial_rope_tables(seq_len):
    rows = seq_len // GRID_W
    row_idx, col_idx = jnp.meshgrid(jnp.arange(rows), jnp.arange(GRID_W), indexing="ij")
    row_idx = row_idx.reshape(-1).astype(jnp.float32)
    col_idx = col_idx.reshape(-1).astype(jnp.float32)
    half = ROPE_AXIS_DIM // 2
    inv_freq = ROPE_THETA ** (-(2.0 * jnp.arange(half, dtype=jnp.float32)) / ROPE_AXIS_DIM)
    ang_r = row_idx[:, None] * inv_freq[None, :]
    ang_c = col_idx[:, None] * inv_freq[None, :]
    return (jnp.cos(ang_r)[:, None], jnp.sin(ang_r)[:, None],
            jnp.cos(ang_c)[:, None], jnp.sin(ang_c)[:, None])

def blocked_gqa(q, k, v):
    b, l, hq, d = q.shape
    r = hq // N_KV_HEADS
    nb = l // Q_BLOCK
    qb = (q * (1.0 / math.sqrt(d))).reshape(b, nb, Q_BLOCK, N_KV_HEADS, r, d)
    qb = jnp.moveaxis(qb, 1, 0)

    def one_block(qi):
        s = jnp.einsum("bqgrd,bkgd->bgrqk", qi, k)
        p = jax.nn.softmax(s, axis=-1)
        return jnp.einsum("bgrqk,bkgd->bqgrd", p, v)

    out = lax.map(one_block, qb)
    return jnp.moveaxis(out, 0, 1).reshape(b, l, hq * d)

def depthwise_conv_centred(x, w, bias):
    y = lax.conv_general_dilated(
        x, w[:, None, :].astype(x.dtype), window_strides=(1,), padding=[(CONV_PAD, CONV_PAD)],
        dimension_numbers=("NWC", "WIO", "NWC"), feature_group_count=x.shape[-1])
    return y + bias.astype(x.dtype)

def ssd_chunked(x, dt, a, bm, cm):
    b, l, h, p = x.shape
    g, n = bm.shape[2], bm.shape[3]
    r = h // g
    nc = l // CHUNK
    xc = (x * dt[..., None]).reshape(b, nc, CHUNK, g, r, p)
    ac = (dt * a).reshape(b, nc, CHUNK, g, r)
    bc = bm.reshape(b, nc, CHUNK, g, n)
    cc = cm.reshape(b, nc, CHUNK, g, n)
    a_cs = jnp.cumsum(ac, axis=2)
    diff = a_cs[:, :, :, None] - a_cs[:, :, None, :]
    mask = jnp.tril(jnp.ones((CHUNK, CHUNK), dtype=bool))[:, :, None, None]
    decay = jnp.exp(jnp.where(mask, diff, -jnp.inf))
    scores = jnp.einsum("bclgn,bcsgn->bclsg", cc, bc)
    y_diag = jnp.einsum("bclsgr,bcsgrp->bclgrp", scores[..., None] * decay, xc)
    decay_to_end = jnp.exp(a_cs[:, :, -1:] - a_cs)
    states = jnp.einsum("bclgn,bclgrp->bcgrpn", bc, xc * decay_to_end[..., None])
    chunk_decay = jnp.exp(a_cs[:, :, -1])

    def step(hs, inp):
        dec, st = inp
        return hs * dec[..., None, None] + st, hs

    h0 = jnp.zeros((b, g, r, p, n), dtype=states.dtype)
    _, states_in = lax.scan(step, h0, (jnp.moveaxis(chunk_decay, 1, 0), jnp.moveaxis(states, 1, 0)))
    states_in = jnp.moveaxis(states_in, 0, 1)
    y_off = jnp.einsum("bclgn,bcgrpn->bclgrp", cc, states_in) * jnp.exp(a_cs)[..., None]
    return (y_diag + y_off).reshape(b, l, h, p)

def ssd_mixer(z, xbc_raw, dt_raw, conv_w, conv_b, dt_bias, a_log, d_skip, norm_w):
    b, l, _ = z.shape
    xbc = jax.nn.silu(depthwise_conv_centred(xbc_raw, conv_w, conv_b)).astype(jnp.float32)
    xs, bm, cm = jnp.split(xbc, [SSD_WIDTH, SSD_WIDTH + SSD_GROUPS * D_STATE], axis=-1)
    xs = xs.reshape(b, l, SSD_HEADS, SSD_HEAD_DIM)
    bm = bm.reshape(b, l, SSD_GROUPS, D_STATE)
    cm = cm.reshape(b, l, SSD_GROUPS, D_STATE)
    dt = jax.nn.softplus(dt_raw.astype(jnp.float32).reshape(b, l, 2, SSD_HEADS)
                         + dt_bias.astype(jnp.float32))
    a = -jnp.exp(a_log.astype(jnp.float32))
    y_fwd = ssd_chunked(xs, dt[:, :, 0], a[0], bm, cm)
    flip = lambda t: jnp.flip(t, axis=1)
    y_bwd = flip(ssd_chunked(flip(xs), flip(dt[:, :, 1]), a[1], flip(bm), flip(cm)))
    y = y_fwd + y_bwd + xs * d_skip.astype(jnp.float32)[:, None]
    y = y.reshape(b, l, SSD_WIDTH) * jax.nn.silu(z.astype(jnp.float32))
    yg = y.reshape(b, l, SSD_GROUPS, SSD_WIDTH // SSD_GROUPS)
    yg = yg * lax.rsqrt(jnp.mean(yg * yg, axis=-1, keepdims=True) + EPS)
    return (yg.reshape(b, l, SSD_WIDTH) * norm_w.astype(jnp.float32)).astype(z.dtype)

def first_inputs(seed: int = 0) -> dict:
    key = jax.random.key(seed)
    ks = jax.random.split(key, 20)
    f32 = jnp.float32
    nrm = lambda k, shape, s: jax.random.normal(k, shape, f32) * s
    dt0 = jnp.exp(jax.random.uniform(ks[7], (DEPTH, 2, SSD_HEADS), f32,
                                     math.log(DT_MIN), math.log(DT_MAX)))
    return {
        "x": jax.random.normal(ks[0], (BATCH, SEQ, D_MODEL), f32),
        "norm_mix_w": 1.0 + nrm(ks[1], (DEPTH, D_MODEL), 0.02),
        "w_in": nrm(ks[2], (DEPTH, D_MODEL, D_IN_PROJ), D_MODEL ** -0.5),
        "q_norm_w": 1.0 + nrm(ks[3], (DEPTH, HEAD_DIM), 0.02),
        "k_norm_w": 1.0 + nrm(ks[4], (DEPTH, HEAD_DIM), 0.02),
        "conv_w": nrm(ks[5], (DEPTH, D_CONV, CONV_CH), D_CONV ** -0.5),
        "conv_b": nrm(ks[6], (DEPTH, CONV_CH), 0.01),
        "dt_bias": dt0 + jnp.log(-jnp.expm1(-dt0)),
        "a_log": jnp.log(jax.random.uniform(ks[8], (DEPTH, 2, SSD_HEADS), f32, 1.0, 16.0)),
        "d_skip": 1.0 + nrm(ks[9], (DEPTH, SSD_HEADS), 0.1),
        "ssd_norm_w": 1.0 + nrm(ks[10], (DEPTH, SSD_WIDTH), 0.02),
        "w_out": nrm(ks[11], (DEPTH, D_MIX, D_MODEL), D_MIX ** -0.5),
        "norm_ffn_w": 1.0 + nrm(ks[12], (DEPTH, D_MODEL), 0.02),
        "w_gate": nrm(ks[13], (DEPTH, D_MODEL, D_FF), D_MODEL ** -0.5),
        "w_up": nrm(ks[14], (DEPTH, D_MODEL, D_FF), D_MODEL ** -0.5),
        "w_down": nrm(ks[15], (DEPTH, D_FF, D_MODEL), D_FF ** -0.5),
        "final_norm_w": 1.0 + nrm(ks[16], (D_MODEL,), 0.02),
    }

def first_block(x, norm_mix_w, w_in, q_norm_w, k_norm_w, conv_w, conv_b, dt_bias, a_log, d_skip,
              ssd_norm_w, w_out, norm_ffn_w, w_gate, w_up, w_down, final_norm_w):
    b, l, _ = x.shape
    cos_r, sin_r, cos_c, sin_c = axial_rope_tables(l)
    split_at = np.cumsum([ATTN_WIDTH, KV_WIDTH, KV_WIDTH, SSD_WIDTH, CONV_CH]).tolist()
    for i in range(DEPTH):
        h = rms_norm(x, norm_mix_w[i])
        proj = jnp.einsum("bld,de->ble", h, w_in[i])
        q, k, v, z, xbc_raw, dt_raw = jnp.split(proj, split_at, axis=-1)
        q = rms_norm(q.reshape(b, l, N_Q_HEADS, HEAD_DIM), q_norm_w[i]).astype(jnp.float32)
        k = rms_norm(k.reshape(b, l, N_KV_HEADS, HEAD_DIM), k_norm_w[i]).astype(jnp.float32)
        v = v.reshape(b, l, N_KV_HEADS, HEAD_DIM).astype(jnp.float32)
        q = axial_rope(q, cos_r, sin_r, cos_c, sin_c)
        k = axial_rope(k, cos_r, sin_r, cos_c, sin_c)
        attn_out = blocked_gqa(q, k, v).astype(x.dtype)
        ssd_out = ssd_mixer(z, xbc_raw, dt_raw, conv_w[i], conv_b[i], dt_bias[i], a_log[i],
                            d_skip[i], ssd_norm_w[i])
        mixed = jnp.concatenate([attn_out, ssd_out], axis=-1)
        x = x + jnp.einsum("ble,ed->bld", mixed, w_out[i])
        h = rms_norm(x, norm_ffn_w[i])
        g = jnp.einsum("bld,df->blf", h, w_gate[i])
        u = jnp.einsum("bld,df->blf", h, w_up[i])
        x = x + jnp.einsum("blf,fd->bld", jax.nn.silu(g) * u, w_down[i])
    return rms_norm(x, final_norm_w)


CTX_LEN = 256
RMS_EPS = 1e-6
N_MOD = 6
SHORT_W = 3

HY_WIDTH = 512
HY_EMB = 33
HY_FF = 64
HY_FAST = 0.3
HY_SLOW = 1.5
HY_TARGET = 1e-2
HY_SHIFT = 0.05

ML_HEADS = 4
ML_HEAD_DIM = 128
ML_WIDTH = ML_HEADS * ML_HEAD_DIM
ML_CHUNK = 64
IN0_COLS = 3 * HY_WIDTH + 4 * ML_WIDTH + 4 * ML_HEADS

MLA_HEADS = 8
MLA_NOPE = 128
MLA_ROPE = 64
MLA_V = 128
MLA_Q_RANK = 384
MLA_KV_RANK = 256
MLA_SCALE = (MLA_NOPE + MLA_ROPE) ** -0.5
ROPE_AXIS = MLA_ROPE // 2
ROPE_BASE = 10000.0

D_FF_2 = 2816


F32 = jnp.float32

def rmsnorm(x, g):
    xf = x.astype(F32)
    y = xf * lax.rsqrt(jnp.mean(xf * xf, axis=-1, keepdims=True) + RMS_EPS)
    return (y * g.astype(F32)).astype(x.dtype)

def ada_mod(cv, w, b):
    m = jax.nn.silu(cv) @ w + b
    return jnp.split(m, N_MOD, axis=-1)

def dwconv(x, w):
    k = w.shape[0]
    return lax.conv_general_dilated(x, w[:, None, :].astype(x.dtype), (1,), [(k // 2, k // 2)],
                                    dimension_numbers=('NWC', 'WIO', 'NWC'),
                                    feature_group_count=x.shape[-1])

def hyena_filters(L, fw1, fb1, fw2, fb2, fw3, freq):
    pos = jnp.arange(L, dtype=F32)
    t = (pos / (L - 1))[:, None]
    bands = (HY_EMB - 1) // 2
    f = jnp.linspace(1e-4, bands - 1, bands, dtype=F32)
    ang = (2.0 * math.pi / L) * pos[:, None] * f[None, :]
    z = jnp.concatenate([t, jnp.cos(ang), -jnp.sin(ang)], axis=-1)
    fq = freq.astype(F32)
    h = jnp.sin(fq * (z @ fw1.astype(F32) + fb1.astype(F32)))
    h = jnp.sin(fq * (h @ fw2.astype(F32) + fb2.astype(F32)))
    h = h @ fw3.astype(F32)
    deltas = jnp.linspace(math.log(HY_TARGET) / HY_FAST, math.log(HY_TARGET) / HY_SLOW, HY_WIDTH, dtype=F32)
    decay = jnp.exp(-t * jnp.abs(jnp.tile(deltas, 2))[None, :])
    return h * (decay + HY_SHIFT)

def hyena_mix(u, conv_w, conv_b, filt, bias):
    u = dwconv(u, conv_w) + conv_b
    x0, x1, v = jnp.split(u, 3, axis=-1)
    L = u.shape[1]
    g = (v * x1).astype(F32)
    h = hyena_filters(L, *filt)
    hf, hb = h[:, :HY_WIDTH], h[:, HY_WIDTH:]
    k2 = jnp.concatenate([hf, jnp.zeros((1, HY_WIDTH), F32), hb[:0:-1]], axis=0)
    n = 2 * L
    y = jnp.fft.irfft(jnp.fft.rfft(g, n=n, axis=1) * jnp.fft.rfft(k2, axis=0)[None], n=n, axis=1)[:, :L]
    y = y + g * bias.astype(F32)
    return y.astype(u.dtype) * x0

def mlstm_chunkwise(q, k, v, ig, lf, state):
    B, H, T, d = q.shape
    nc = T // ML_CHUNK

    def chunks(a):
        return jnp.moveaxis(a.reshape((B, H, nc, ML_CHUNK) + a.shape[3:]), 2, 0)

    causal = jnp.tril(jnp.ones((ML_CHUNK, ML_CHUNK), dtype=bool))

    def step(carry, inp):
        C, nv, m = carry
        qc, kc, vc, ic, fc = inp
        b = jnp.cumsum(fc, axis=-1)
        dlog = jnp.where(causal, b[..., :, None] - b[..., None, :] + ic[..., None, :], -jnp.inf)
        inter = b + m[..., None]
        m_t = jnp.maximum(inter, jnp.max(dlog, axis=-1))
        w_in = jnp.exp(dlog - m_t[..., None])
        w_st = jnp.exp(inter - m_t)
        s = jnp.einsum('bhtd,bhsd->bhts', qc, kc) * w_in
        num = jnp.einsum('bhts,bhsd->bhtd', s, vc) + w_st[..., None] * jnp.einsum('bhve,bhte->bhtv', C, qc)
        den = jnp.sum(s, axis=-1) + w_st * jnp.einsum('bhe,bhte->bht', nv, qc)
        h = num / jnp.maximum(jnp.abs(den), jnp.exp(-m_t))[..., None]
        bl = b[..., -1]
        gs = bl[..., None] - b + ic
        m_new = jnp.maximum(bl + m, jnp.max(gs, axis=-1))
        a = jnp.exp(bl + m - m_new)
        ws = jnp.exp(gs - m_new[..., None])
        C_new = a[..., None, None] * C + jnp.einsum('bhs,bhsv,bhse->bhve', ws, vc, kc)
        n_new = a[..., None] * nv + jnp.einsum('bhs,bhse->bhe', ws, kc)
        return (C_new, n_new, m_new), h

    state, hs = lax.scan(step, state, (chunks(q), chunks(k), chunks(v), chunks(ig), chunks(lf)))
    return jnp.moveaxis(hs, 0, 2).reshape(B, H, T, d), state

def mlstm_direction(q, k, v, ig, f_pre, state, reverse):
    lf = jax.nn.log_sigmoid(f_pre)
    if reverse:
        q, k, v = jnp.flip(q, 2), jnp.flip(k, 2), jnp.flip(v, 2)
        ig, lf = jnp.flip(ig, -1), jnp.flip(lf, -1)
    h, state = mlstm_chunkwise(q, k, v, ig, lf, state)
    if reverse:
        h = jnp.flip(h, 2)
    return h, state

def mlstm_inputs(u, conv_w, gate_b):
    B, L, _ = u.shape
    off = 3 * HY_WIDTH
    qk = jax.nn.silu(dwconv(u[..., off:off + 2 * ML_WIDTH], conv_w))
    q, k = jnp.split(qk, 2, axis=-1)
    v = u[..., off + 2 * ML_WIDTH:off + 3 * ML_WIDTH]
    og = u[..., off + 3 * ML_WIDTH:off + 4 * ML_WIDTH]
    gates = u[..., off + 4 * ML_WIDTH:].astype(F32) + gate_b.astype(F32)
    gates = jnp.transpose(gates.reshape(B, L, 4, ML_HEADS), (2, 0, 3, 1))

    def heads(a):
        return jnp.transpose(a.reshape(B, L, ML_HEADS, ML_HEAD_DIM), (0, 2, 1, 3)).astype(F32)

    return heads(q) * ML_HEAD_DIM ** -0.5, heads(k), heads(v), og, gates

def mlstm_out(h, og, norm_g):
    B, H, L, d = h.shape
    t = jnp.swapaxes(h, 1, 2)
    t = t * lax.rsqrt(jnp.mean(t * t, axis=-1, keepdims=True) + RMS_EPS)
    t = t.reshape(B, L, H * d) * norm_g.astype(F32)
    return (t * jax.nn.sigmoid(og.astype(F32))).astype(og.dtype)

def mlstm_mix(u_ctx, u_lat, conv_w, gate_b, norm_g):
    qc, kc, vc, oc, gc = mlstm_inputs(u_ctx, conv_w, gate_b)
    ql, kl, vl, ol, gl = mlstm_inputs(u_lat, conv_w, gate_b)
    B = u_ctx.shape[0]
    zero = (jnp.zeros((B, ML_HEADS, ML_HEAD_DIM, ML_HEAD_DIM), F32),
            jnp.zeros((B, ML_HEADS, ML_HEAD_DIM), F32),
            jnp.zeros((B, ML_HEADS), F32))
    hc_f, st_f = mlstm_direction(qc, kc, vc, gc[0], gc[1], zero, False)
    hl_f, _ = mlstm_direction(ql, kl, vl, gl[0], gl[1], st_f, False)
    hc_b, st_b = mlstm_direction(qc, kc, vc, gc[2], gc[3], zero, True)
    hl_b, _ = mlstm_direction(ql, kl, vl, gl[2], gl[3], st_b, True)
    return mlstm_out(hc_f + hc_b, oc, norm_g), mlstm_out(hl_f + hl_b, ol, norm_g)

def hyena_mlstm_mixer(h_ctx, h_lat, w_in, hy_conv_w, hy_conv_b, hy_filter, hy_bias,
                      ml_conv_w, ml_gate_b, ml_norm_g, w_out):
    u_ctx = h_ctx @ w_in
    u_lat = h_lat @ w_in
    hy_c = hyena_mix(u_ctx[..., :3 * HY_WIDTH], hy_conv_w, hy_conv_b, hy_filter, hy_bias)
    hy_l = hyena_mix(u_lat[..., :3 * HY_WIDTH], hy_conv_w, hy_conv_b, hy_filter, hy_bias)
    ml_c, ml_l = mlstm_mix(u_ctx, u_lat, ml_conv_w, ml_gate_b, ml_norm_g)
    y_ctx = jnp.concatenate([hy_c, ml_c], axis=-1) @ w_out
    y_lat = jnp.concatenate([hy_l, ml_l], axis=-1) @ w_out
    return y_ctx, y_lat

def rope_tables(T):
    n_rows = T // GRID_W
    row = jnp.repeat(jnp.arange(n_rows, dtype=F32), GRID_W)
    col = jnp.tile(jnp.arange(GRID_W, dtype=F32), n_rows)
    inv = ROPE_BASE ** (-jnp.arange(0, ROPE_AXIS, 2, dtype=F32) / ROPE_AXIS)
    ang = jnp.stack([row[:, None] * inv, col[:, None] * inv], axis=1)
    return jnp.cos(ang), jnp.sin(ang)

def apply_rope2d(x, cos, sin):
    xa = x.reshape(x.shape[:-1] + (2, ROPE_AXIS))
    x1, x2 = jnp.split(xa, 2, axis=-1)
    c = cos[None, :, None].astype(x.dtype)
    s = sin[None, :, None].astype(x.dtype)
    return jnp.concatenate([x1 * c - x2 * s, x2 * c + x1 * s], axis=-1).reshape(x.shape)

def mla_down(h, w_down):
    return jnp.split(h @ w_down, [MLA_Q_RANK, MLA_Q_RANK + MLA_KV_RANK], axis=-1)

def mla_q(q_a, q_norm, w_uq, rope):
    B, L, _ = q_a.shape
    q = (rmsnorm(q_a, q_norm) @ w_uq).reshape(B, L, MLA_HEADS, MLA_NOPE + MLA_ROPE)
    if rope is None:
        return q
    q_n, q_r = jnp.split(q, [MLA_NOPE], axis=-1)
    return jnp.concatenate([q_n, apply_rope2d(q_r, *rope)], axis=-1)

def mla_kv(kv_a, k_r, kv_norm, w_ukv, rope):
    B, L, _ = kv_a.shape
    kv = (rmsnorm(kv_a, kv_norm) @ w_ukv).reshape(B, L, MLA_HEADS, MLA_NOPE + MLA_V)
    k_n, v = jnp.split(kv, [MLA_NOPE], axis=-1)
    k_r = k_r[:, :, None, :]
    if rope is not None:
        k_r = apply_rope2d(k_r, *rope)
    k = jnp.concatenate([k_n, jnp.broadcast_to(k_r, (B, L, MLA_HEADS, MLA_ROPE))], axis=-1)
    return k, v

def attend(q, k, v):
    s = jnp.einsum('bqhd,bkhd->bhqk', q, k).astype(F32) * MLA_SCALE
    p = jax.nn.softmax(s, axis=-1).astype(v.dtype)
    return jnp.einsum('bhqk,bkhd->bqhd', p, v)

def mla_mixer(h_ctx, h_lat, ctx_queries, w_down, q_norm, kv_norm, w_uq, w_ukv, w_o):
    B, S, _ = h_lat.shape
    rope = rope_tables(S)
    qa_c, kva_c, kr_c = mla_down(h_ctx, w_down)
    qa_l, kva_l, kr_l = mla_down(h_lat, w_down)
    k_c, v_c = mla_kv(kva_c, kr_c, kv_norm, w_ukv, None)
    k_l, v_l = mla_kv(kva_l, kr_l, kv_norm, w_ukv, rope)
    q_l = mla_q(qa_l, q_norm, w_uq, rope)
    k_all = jnp.concatenate([k_c, k_l], axis=1)
    v_all = jnp.concatenate([v_c, v_l], axis=1)
    nb = S // Q_BLOCK
    qb = jnp.moveaxis(q_l.reshape(B, nb, Q_BLOCK, MLA_HEADS, MLA_NOPE + MLA_ROPE), 1, 0)
    o_l = lax.map(lambda blk: attend(blk, k_all, v_all), qb)
    y_lat = jnp.moveaxis(o_l, 0, 1).reshape(B, S, MLA_HEADS * MLA_V) @ w_o
    y_ctx = None
    if ctx_queries:
        q_c = mla_q(qa_c, q_norm, w_uq, None)
        y_ctx = attend(q_c, k_c, v_c).reshape(B, h_ctx.shape[1], MLA_HEADS * MLA_V) @ w_o
    return y_ctx, y_lat

def conv_ffn(h, w_up, conv_w, conv_b, w_down):
    g, u = jnp.split(h @ w_up, 2, axis=-1)
    g = dwconv(g, conv_w) + conv_b
    return (jax.nn.silu(g) * u) @ w_down

def second_inputs(seed: int = 0) -> dict:
    key = jax.random.key(seed)
    keys = iter(jax.random.split(key, 64))

    def nrm(shape, scale):
        return jax.random.normal(next(keys), shape, F32) * scale

    def gain(n):
        return 1.0 + nrm((n,), 0.02)

    def ffn():
        return (nrm((D_MODEL, 2 * D_FF_2), D_MODEL ** -0.5), nrm((SHORT_W, D_FF_2), SHORT_W ** -0.5),
                nrm((D_FF_2,), 0.02), nrm((D_FF_2, D_MODEL), D_FF_2 ** -0.5))

    x = nrm((BATCH, SEQ, D_MODEL), 1.0)
    c = nrm((BATCH, D_MODEL), 1.0)
    ctx = nrm((BATCH, CTX_LEN, D_MODEL), 1.0)
    c_ctx = nrm((D_MODEL,), 1.0)
    forget_b = jnp.linspace(3.0, 6.0, ML_HEADS, dtype=F32)
    ml_gate_b = jnp.concatenate([nrm((ML_HEADS,), 0.1), forget_b + nrm((ML_HEADS,), 0.01),
                                 nrm((ML_HEADS,), 0.1), forget_b + nrm((ML_HEADS,), 0.01)])
    f0 = ffn()
    f1 = ffn()
    mix_w = HY_WIDTH + ML_WIDTH
    return {
        'x': x, 'c': c, 'ctx': ctx, 'c_ctx': c_ctx,
        'ada_w_0': nrm((D_MODEL, N_MOD * D_MODEL), 0.5 * D_MODEL ** -0.5),
        'ada_b_0': nrm((N_MOD * D_MODEL,), 0.02),
        'norm_mix_0': gain(D_MODEL), 'norm_ffn_0': gain(D_MODEL),
        'w_in_0': nrm((D_MODEL, IN0_COLS), D_MODEL ** -0.5),
        'hy_conv_w': nrm((SHORT_W, 3 * HY_WIDTH), SHORT_W ** -0.5),
        'hy_conv_b': nrm((3 * HY_WIDTH,), 0.02),
        'hy_fw1': nrm((HY_EMB, HY_FF), HY_EMB ** -0.5),
        'hy_fb1': nrm((HY_FF,), 0.02),
        'hy_fw2': nrm((HY_FF, HY_FF), HY_FF ** -0.5),
        'hy_fb2': nrm((HY_FF,), 0.02),
        'hy_fw3': nrm((HY_FF, 2 * HY_WIDTH), 0.05 * HY_FF ** -0.5),
        'hy_freq': gain(HY_FF),
        'hy_bias': nrm((HY_WIDTH,), 0.1),
        'ml_conv_w': nrm((SHORT_W, 2 * ML_WIDTH), SHORT_W ** -0.5),
        'ml_gate_b': ml_gate_b,
        'ml_norm_g': gain(ML_WIDTH),
        'w_out_0': nrm((mix_w, D_MODEL), mix_w ** -0.5),
        'ffn_up_0': f0[0], 'ffn_conv_w_0': f0[1], 'ffn_conv_b_0': f0[2], 'ffn_down_0': f0[3],
        'ada_w_1': nrm((D_MODEL, N_MOD * D_MODEL), 0.5 * D_MODEL ** -0.5),
        'ada_b_1': nrm((N_MOD * D_MODEL,), 0.02),
        'norm_mix_1': gain(D_MODEL), 'norm_ffn_1': gain(D_MODEL),
        'mla_w_down': nrm((D_MODEL, MLA_Q_RANK + MLA_KV_RANK + MLA_ROPE), D_MODEL ** -0.5),
        'mla_q_norm': gain(MLA_Q_RANK), 'mla_kv_norm': gain(MLA_KV_RANK),
        'mla_w_uq': nrm((MLA_Q_RANK, MLA_HEADS * (MLA_NOPE + MLA_ROPE)), MLA_Q_RANK ** -0.5),
        'mla_w_ukv': nrm((MLA_KV_RANK, MLA_HEADS * (MLA_NOPE + MLA_V)), MLA_KV_RANK ** -0.5),
        'mla_w_o': nrm((MLA_HEADS * MLA_V, D_MODEL), (MLA_HEADS * MLA_V) ** -0.5),
        'ffn_up_1': f1[0], 'ffn_conv_w_1': f1[1], 'ffn_conv_b_1': f1[2], 'ffn_down_1': f1[3],
        'final_norm': gain(D_MODEL),
    }

def second_block(x, c, ctx, c_ctx, ada_w_0, ada_b_0, norm_mix_0, norm_ffn_0, w_in_0, hy_conv_w, hy_conv_b,
              hy_fw1, hy_fb1, hy_fw2, hy_fb2, hy_fw3, hy_freq, hy_bias, ml_conv_w, ml_gate_b, ml_norm_g,
              w_out_0, ffn_up_0, ffn_conv_w_0, ffn_conv_b_0, ffn_down_0, ada_w_1, ada_b_1, norm_mix_1,
              norm_ffn_1, mla_w_down, mla_q_norm, mla_kv_norm, mla_w_uq, mla_w_ukv, mla_w_o, ffn_up_1,
              ffn_conv_w_1, ffn_conv_b_1, ffn_down_1, final_norm):
    ada_w = (ada_w_0, ada_w_1)
    ada_b = (ada_b_0, ada_b_1)
    norm_mix = (norm_mix_0, norm_mix_1)
    norm_ffn = (norm_ffn_0, norm_ffn_1)
    ffn_p = ((ffn_up_0, ffn_conv_w_0, ffn_conv_b_0, ffn_down_0),
             (ffn_up_1, ffn_conv_w_1, ffn_conv_b_1, ffn_down_1))
    hy_filter = (hy_fw1, hy_fb1, hy_fw2, hy_fb2, hy_fw3, hy_freq)
    x_lat, x_ctx = x, ctx
    for layer in range(DEPTH):
        last = layer == DEPTH - 1
        sh1, sc1, g1, sh2, sc2, g2 = ada_mod(c[:, None, :], ada_w[layer], ada_b[layer])
        csh1, csc1, cg1, csh2, csc2, cg2 = ada_mod(c_ctx, ada_w[layer], ada_b[layer])
        h_lat = rmsnorm(x_lat, norm_mix[layer]) * (1 + sc1) + sh1
        h_ctx = rmsnorm(x_ctx, norm_mix[layer]) * (1 + csc1) + csh1
        if layer % 2 == 0:
            y_ctx, y_lat = hyena_mlstm_mixer(h_ctx, h_lat, w_in_0, hy_conv_w, hy_conv_b, hy_filter, hy_bias,
                                             ml_conv_w, ml_gate_b, ml_norm_g, w_out_0)
        else:
            y_ctx, y_lat = mla_mixer(h_ctx, h_lat, not last, mla_w_down, mla_q_norm, mla_kv_norm,
                                     mla_w_uq, mla_w_ukv, mla_w_o)
        x_lat = x_lat + g1 * y_lat
        x_lat = x_lat + g2 * conv_ffn(rmsnorm(x_lat, norm_ffn[layer]) * (1 + sc2) + sh2, *ffn_p[layer])
        if not last:
            x_ctx = x_ctx + cg1 * y_ctx
            x_ctx = x_ctx + cg2 * conv_ffn(rmsnorm(x_ctx, norm_ffn[layer]) * (1 + csc2) + csh2, *ffn_p[layer])
    return rmsnorm(x_lat, final_norm)


def setup_inputs(seed=0):
    out = dict(first_inputs(seed))
    for name, value in second_inputs(seed + 1).items():
        if name != "x":
            out[name + "_2"] = value
    return out


def reference(
    x, norm_mix_w, w_in, q_norm_w, k_norm_w, conv_w, conv_b, dt_bias, a_log, d_skip, ssd_norm_w,
    w_out, norm_ffn_w, w_gate, w_up, w_down, final_norm_w, c_2, ctx_2, c_ctx_2, ada_w_0_2,
    ada_b_0_2, norm_mix_0_2, norm_ffn_0_2, w_in_0_2, hy_conv_w_2, hy_conv_b_2, hy_fw1_2,
    hy_fb1_2, hy_fw2_2, hy_fb2_2, hy_fw3_2, hy_freq_2, hy_bias_2, ml_conv_w_2, ml_gate_b_2,
    ml_norm_g_2, w_out_0_2, ffn_up_0_2, ffn_conv_w_0_2, ffn_conv_b_0_2, ffn_down_0_2, ada_w_1_2,
    ada_b_1_2, norm_mix_1_2, norm_ffn_1_2, mla_w_down_2, mla_q_norm_2, mla_kv_norm_2,
    mla_w_uq_2, mla_w_ukv_2, mla_w_o_2, ffn_up_1_2, ffn_conv_w_1_2, ffn_conv_b_1_2,
    ffn_down_1_2, final_norm_2,
):
    x = first_block(
        x, norm_mix_w, w_in, q_norm_w, k_norm_w, conv_w, conv_b, dt_bias, a_log, d_skip,
        ssd_norm_w, w_out, norm_ffn_w, w_gate, w_up, w_down, final_norm_w,
    )
    return second_block(
        x, c_2, ctx_2, c_ctx_2, ada_w_0_2, ada_b_0_2, norm_mix_0_2, norm_ffn_0_2, w_in_0_2,
        hy_conv_w_2, hy_conv_b_2, hy_fw1_2, hy_fb1_2, hy_fw2_2, hy_fb2_2, hy_fw3_2, hy_freq_2,
        hy_bias_2, ml_conv_w_2, ml_gate_b_2, ml_norm_g_2, w_out_0_2, ffn_up_0_2, ffn_conv_w_0_2,
        ffn_conv_b_0_2, ffn_down_0_2, ada_w_1_2, ada_b_1_2, norm_mix_1_2, norm_ffn_1_2,
        mla_w_down_2, mla_q_norm_2, mla_kv_norm_2, mla_w_uq_2, mla_w_ukv_2, mla_w_o_2,
        ffn_up_1_2, ffn_conv_w_1_2, ffn_conv_b_1_2, ffn_down_1_2, final_norm_2,
    )


_drawn_inputs = setup_inputs


def setup_inputs(seed=0):
    import zlib

    import numpy as np

    out = dict(_drawn_inputs(seed))
    spreads = {}
    factors = {'q_norm_w': 8.0,
     'k_norm_w': 8.0,
     'conv_b': 3.528,
     'ssd_norm_w': 3.073,
     'norm_ffn_w': 3.036,
     'final_norm_w': 2.734,
     'ctx_2': 2.999,
     'ada_b_0_2': 2.719,
     'norm_mix_0_2': 8.0,
     'norm_ffn_0_2': 31.701,
     'hy_conv_b_2': 8.0,
     'hy_fb1_2': 8.0,
     'hy_fb2_2': 8.0,
     'hy_freq_2': 8.0,
     'ml_norm_g_2': 200.0,
     'ffn_conv_b_0_2': 49.492,
     'ada_b_1_2': 3.098,
     'norm_mix_1_2': 38.583,
     'norm_ffn_1_2': 48.178,
     'mla_q_norm_2': 47.778,
     'mla_kv_norm_2': 59.402,
     'ffn_conv_b_1_2': 64.0,
     'final_norm_2': 24.664,
     'ml_conv_w_2': 8.0,
     'ml_gate_b_2': 3.432}
    for name, (base, spread) in spreads.items():
        noise = np.random.default_rng([zlib.crc32(name.encode()), seed]).standard_normal(out[name].shape)
        drawn = base * np.exp(spread * noise) if base else spread * noise
        out[name] = jnp.asarray(drawn.astype(out[name].dtype))
    for name, factor in factors.items():
        out[name] = (out[name] * factor).astype(out[name].dtype)
    return out
```

```python
from contextlib import ExitStack, contextmanager
from itertools import count

import numpy as np

import concourse.bass as bass
from concourse import mybir

F32 = mybir.dt.float32
ALU = mybir.AluOpType
ACT = mybir.ActivationFunctionType
AX = mybir.AxisListType

P = 128
D = 1024
KT = D // P
CTX, SEQ = 256, 512
TOK = CTX + SEQ
LAT = slice(CTX, TOK)
LT = SEQ // P
FF = 2816
FT = FF // P
EPS = 1e-6
NEG = -1e30
FIRST_SEMAPHORE = 120
SEGS = [(0, CTX), (CTX, SEQ)]
PADDED = 1 + CTX + 1 + SEQ + 1
PSEG = [(1, CTX), (2 + CTX, SEQ)]



NAMES = count()


def unique(name):
    return f"{name}_{next(NAMES)}"

@contextmanager
def stage(nc, *names):
    first = FIRST_SEMAPHORE
    with ExitStack() as ctx:
        sems = [ctx.enter_context(nc.semaphore(n, num=first + k)) for k, n in enumerate(names)]
        with nc.Block() as block:
            yield (block, *sems)
        nc.multi_engine_barrier(mybir.ALL_ENGINES, sems_to_clear=range(first, first + len(names)))


class Chain:

    def __init__(self, eng, sem):
        self.eng, self.sem, self.n = eng, sem, 0

    def step(self, ins):
        self.n += 1
        ins.then_inc(self.sem, 1)
        self.eng.wait_ge(self.sem, self.n)


def in_pairs(eng, tiles, step):
    for j in range(min(2, tiles)):
        step(j, 0)
    if tiles >= 4:
        with eng.Fori(1, tiles // 2) as i:
            step(0, i)
            step(1, i)
    if tiles % 2 and tiles > 2:
        step(0, tiles // 2)


def later(i):
    return not isinstance(i, int) or i > 0


def stream_weights(sp, weights, slots, arrived, used, tiles):
    def load(j, i):
        if later(i):
            sp.wait_ge(used, 2 * i + j - 1)
        sp.dma_start(slots[j], weights[2 * i + j]).then_inc(arrived[j], 16)
    in_pairs(sp, tiles, load)


def project(pe, slots, kt, rhs, banks, arrived, drained, done, tiles):
    def tile(j, i):
        pe.wait_ge(arrived[j], 16 * (i + 1))
        if later(i):
            pe.wait_ge(drained, 2 * i + j - 1)
        for k in range(kt):
            for out, x in zip(banks(j), rhs(k)):
                mm = pe.matmul(out, slots[j][:, k], x, start=k == 0, stop=k == kt - 1)
        mm.then_inc(done, 1)
    in_pairs(pe, tiles, tile)



def rms_norm(nc, K, src, dst, segs, tiles, size, gain, shift=None):
    with ExitStack() as ctx:
        ps = ctx.enter_context(nc.psum_tensor(unique("sums"), [P, 2, 512], F32))
        rs = ctx.enter_context(nc.sbuf_tensor(unique("rstd"), [P, TOK], F32))
        with stage(nc, "squares_ready", "sums_ready", "root_ready", "rstd_ready", "scaled") as (
                block, squares_ready, sums_ready, root_ready, rstd_ready, scaled):
            @block.scalar
            def _(act):
                for k in range(tiles):
                    act.activation(dst(k), src(k), ACT.Square).then_inc(squares_ready, 1)
                act.wait_ge(sums_ready, 1)
                for n, (a, w) in enumerate(segs):
                    act.activation(rs[:, a:a + w], ps[:, n, 0:w], ACT.Sqrt, scale=1.0 / size,
                                   bias=K["eps"]).then_inc(root_ready, 1)
                if shift is not None:
                    for k in range(tiles):
                        for n, (a, w) in enumerate(segs):
                            act.wait_ge(scaled, len(segs) * k + n + 1)
                            act.activation(dst(k, n), dst(k, n), ACT.Identity, bias=shift(k, n))

            @block.tensor
            def _(pe):
                for k in range(tiles):
                    pe.wait_ge(squares_ready, k + 1)
                    for n, (a, w) in enumerate(segs):
                        mm = pe.matmul(ps[:, n, 0:w], K["ones"], dst(k, n), start=k == 0,
                                       stop=k == tiles - 1)
                mm.then_inc(sums_ready, 1)

            @block.vector
            def _(dve):
                for n, (a, w) in enumerate(segs):
                    dve.wait_ge(root_ready, n + 1)
                    dve.reciprocal(rs[:, a:a + w], rs[:, a:a + w]).then_inc(rstd_ready, 1)
                dve.wait_ge(rstd_ready, len(segs))
                for k in range(tiles):
                    for n, (a, w) in enumerate(segs):
                        dve.scalar_tensor_tensor(dst(k, n), src(k, n), gain(k, n), rs[:, a:a + w],
                                                 ALU.mult, ALU.mult).then_inc(scaled, 1)


def token_tiles(buf, segs):
    a0, total = segs[0][0], sum(w for _, w in segs)

    def at(k, n=None):
        if n is None:
            return buf[:, k, a0:a0 + total]
        return buf[:, k, segs[n][0]:segs[n][0] + segs[n][1]]
    return at


def project_residual(nc, weights, tiles, kt, rhs, x, segs, gate=None):
    with ExitStack() as ctx:
        W = ctx.enter_context(nc.sbuf_tensor(unique("weights"), [P, 2, kt, P], F32))
        ps = ctx.enter_context(nc.psum_tensor(unique("sum"), [P, 2, 2, 512], F32))
        with stage(nc, "even_arrived", "odd_arrived", "sum_ready", "added") as (
                block, even_arrived, odd_arrived, sum_ready, added):
            arrived = (even_arrived, odd_arrived)

            @block.sync
            def _(sp):
                stream_weights(sp, weights, [W[:, j].rearrange("p k m -> p (k m)") for j in (0, 1)],
                               arrived, sum_ready, tiles)

            @block.tensor
            def _(pe):
                project(pe, [W[:, 0], W[:, 1]], kt, rhs,
                        lambda j: [ps[:, j, n, 0:w] for n, (_, w) in enumerate(segs)],
                        arrived, added, sum_ready, tiles)

            @block.vector
            def _(dve):
                def tile(j, i):
                    dve.wait_ge(sum_ready, 2 * i + j + 1)
                    for n, (a, w) in enumerate(segs):
                        t = x[:, 2 * i + j, a:a + w]
                        if gate is None:
                            last = dve.tensor_tensor(t, ps[:, j, n, 0:w], t, ALU.add)
                        else:
                            last = dve.scalar_tensor_tensor(t, ps[:, j, n, 0:w], gate(2 * i + j, n), t,
                                                            ALU.mult, ALU.add)
                    last.then_inc(added, 1)
                in_pairs(dve, tiles, tile)



Q_T, K_T, V_T, Z_T, X_T = 0, 4, 5, 6, 10
IN_TILES = 18
PAD5 = SEQ + 4


def mix_projection(nc, K, c, layer, w_in, w_dt, h, proj, conv, dt_rows):
    HEAD = X_T
    with ExitStack() as ctx:
        W = ctx.enter_context(nc.sbuf_tensor(unique("w_in"), [P, 2, KT, P], F32))
        Wd = ctx.enter_context(nc.sbuf_tensor(unique("w_dt"), [P, KT, 16], F32))
        raw = ctx.enter_context(nc.sbuf_tensor(unique("conv_raw"), [P, 2, PAD5], F32))
        acc = ctx.enter_context(nc.sbuf_tensor(unique("conv_acc"), [P, 2, SEQ], F32))
        ps = ctx.enter_context(nc.psum_tensor(unique("proj_ps"), [P, 2, 512], F32))
        pd = ctx.enter_context(nc.psum_tensor(unique("dt_ps"), [P, 512], F32))
        with stage(nc, "even_arrived", "odd_arrived", "product_ready", "copied", "dt_arrived", "dt_ready") as (
                block, even_arrived, odd_arrived, product_ready, copied, dt_arrived, dt_ready):
            arrived = (even_arrived, odd_arrived)

            @block.sync
            def _(sp):
                sp.dma_start(Wd[:].rearrange("p k m -> p (k m)"), w_dt).then_inc(dt_arrived, 16)
                stream_weights(sp, w_in[0:HEAD], [W[:, j].rearrange("p k m -> p (k m)") for j in (0, 1)],
                               arrived, product_ready, HEAD)

            @block.tensor
            def _(pe):
                project(pe, [W[:, 0], W[:, 1]], KT, lambda k: [h[:, k, LAT]], lambda j: [ps[:, j]],
                        arrived, copied, product_ready, HEAD)
                pe.wait_ge(dt_arrived, 16)
                for k in range(KT):
                    mm = pe.matmul(pd[0:16, :], Wd[:, k], h[:, k, LAT], start=k == 0, stop=k == KT - 1)
                mm.then_inc(dt_ready, 1)

            @block.scalar
            def _(act):
                def tile(j, i):
                    act.wait_ge(product_ready, 2 * i + j + 1)
                    act.activation(proj[:, 2 * i + j], ps[:, j], ACT.Copy).then_inc(copied, 1)
                in_pairs(act, HEAD, tile)
                act.wait_ge(dt_ready, 1)
                act.activation(dt_rows, pd[0:16, :], ACT.Identity, bias=c("dt_bias", layer)[0:16])
        with stage(nc, "even_arrived", "odd_arrived", "product_ready", "raw_ready", "pads_zero",
                   "conv_step", "conv_ready", "silu_done") as (
                block, even_arrived, odd_arrived, product_ready, raw_ready, pads_zero,
                conv_step, conv_ready, silu_done):
            arrived = (even_arrived, odd_arrived)
            tiles = IN_TILES - HEAD
            cw = c("conv_w", layer).rearrange("p (n w) -> p n w", w=5)
            cb = c("conv_b", layer).rearrange("p (n w) -> p n w", w=1)

            @block.sync
            def _(sp):
                stream_weights(sp, w_in[HEAD:IN_TILES], [W[:, j].rearrange("p k m -> p (k m)") for j in (0, 1)],
                               arrived, product_ready, tiles)

            @block.tensor
            def _(pe):
                project(pe, [W[:, 0], W[:, 1]], KT, lambda k: [h[:, k, LAT]], lambda j: [ps[:, j]],
                        arrived, raw_ready, product_ready, tiles)

            @block.scalar
            def _(act):
                act.wait_ge(pads_zero, 2)

                def tile(j, i):
                    act.wait_ge(product_ready, 2 * i + j + 1)
                    if later(i):
                        act.wait_ge(conv_ready, 2 * i + j - 1)
                    act.activation(raw[:, j, 2:2 + SEQ], ps[:, j], ACT.Copy).then_inc(raw_ready, 1)
                    if j == 1:
                        for jj in (0, 1):
                            act.wait_ge(conv_ready, 2 * i + jj + 1)
                            act.activation(conv[:, 2 * i + jj], acc[:, jj], ACT.Silu).then_inc(silu_done, 1)
                in_pairs(act, tiles, tile)
                for n in range(4):
                    act.activation(proj[:, Z_T + n], proj[:, Z_T + n], ACT.Silu)

            @block.vector
            def _(dve):
                for side in (0, 2 + SEQ):
                    dve.memset(raw[:, :, side:side + 2], 0.0).then_inc(pads_zero, 1)

                def tile(j, i):
                    n = 2 * i + j
                    dve.wait_ge(raw_ready, n + 1)
                    if later(i):
                        dve.wait_ge(silu_done, n - 1)
                    dve.tensor_scalar(acc[:, j], raw[:, j, 0:SEQ], cw[:, n, 0:1], cb[:, n, 0:1],
                                      ALU.mult, ALU.add).then_inc(conv_step, 1)
                    for w in range(1, 5):
                        dve.wait_ge(conv_step, 4 * n + w)
                        last = dve.scalar_tensor_tensor(acc[:, j], raw[:, j, w:w + SEQ], cw[:, n, w:w + 1],
                                                        acc[:, j], ALU.mult, ALU.add)
                        last.then_inc(conv_step if w < 4 else conv_ready, 1)
                in_pairs(dve, tiles, tile)


def head_norm_rope(nc, K, tiles, a, w):
    with ExitStack() as ctx:
        sq = ctx.enter_context(nc.sbuf_tensor(unique("squares"), [P, 2, SEQ], F32))
        rs = ctx.enter_context(nc.sbuf_tensor(unique("rstd"), [P, 2, SEQ], F32))
        t2 = ctx.enter_context(nc.sbuf_tensor(unique("turned"), [P, 2, SEQ], F32))
        pn = ctx.enter_context(nc.psum_tensor(unique("norm_ps"), [P, 2, 512], F32))
        pr = ctx.enter_context(nc.psum_tensor(unique("rope_ps"), [P, 2, 512], F32))
        with stage(nc, "squares_ready", "sums_ready", "root_ready", "normed", "swapped", "dve_step", "done") as (
                block, squares_ready, sums_ready, root_ready, normed, swapped, dve_step, done):
            N = len(tiles)

            @block.scalar
            def _(act):
                for n, (x, g) in enumerate(tiles):
                    if g is None:
                        continue
                    if n >= 2:
                        act.wait_ge(sums_ready, n - 1)
                        act.wait_ge(normed, n - 1)
                    act.activation(sq[:, n % 2], x, ACT.Square).then_inc(squares_ready, 1)
                    act.wait_ge(sums_ready, n + 1)
                    act.activation(rs[:, n % 2], pn[:, n % 2], ACT.Sqrt, scale=1.0 / 64,
                                   bias=K["eps"]).then_inc(root_ready, 1)

            @block.tensor
            def _(pe):
                def sums(n):
                    if tiles[n][1] is not None:
                        pe.wait_ge(squares_ready, n + 1)
                        if n >= 2:
                            pe.wait_ge(root_ready, n - 1)
                        pe.matmul(pn[:, n % 2], K["ones64"], sq[:, n % 2], start=True,
                                  stop=True).then_inc(sums_ready, 1)

                def swap(n):
                    pe.wait_ge(normed, n + 1)
                    if n >= 2:
                        pe.wait_ge(done, n - 1)
                    pe.matmul(pr[:, n % 2], K["swap"], tiles[n][0], start=True,
                              stop=True).then_inc(swapped, 1)
                sums(0)
                for n in range(N):
                    if n + 1 < N:
                        sums(n + 1)
                    swap(n)

            @block.vector
            def _(dve):
                chain = Chain(dve, dve_step)

                def norm(n):
                    x, g = tiles[n]
                    if g is None:
                        dve.nop().then_inc(normed, 1)
                        return
                    dve.wait_ge(root_ready, n + 1)
                    chain.step(dve.reciprocal(rs[:, n % 2], rs[:, n % 2]))
                    dve.scalar_tensor_tensor(x, x, g, rs[:, n % 2], ALU.mult, ALU.mult).then_inc(normed, 1)
                    dve.wait_ge(normed, n + 1)

                def rotate(n):
                    x = tiles[n][0]
                    dve.wait_ge(swapped, n + 1)
                    chain.step(dve.tensor_tensor(t2[:, n % 2], pr[:, n % 2], K["rope_sin"], ALU.mult))
                    chain.step(dve.tensor_tensor(x, x, K["rope_cos"], ALU.mult))
                    dve.tensor_tensor(x, x, t2[:, n % 2], ALU.add).then_inc(done, 1)
                norm(0)
                for n in range(N):
                    if n + 1 < N:
                        norm(n + 1)
                    rotate(n)
                dve.wait_ge(done, N)


def attention(nc, K, heads, keys, scale, score_parts, values, vrows, out):
    kt = keys // P
    cuts = [(0, 512)] if keys == 512 else [(0, 384), (384, 384)]
    nb = len(cuts)
    with ExitStack() as ctx:
        pr = ctx.enter_context(nc.sbuf_tensor(unique("probs"), [P, 2, keys], F32))
        pt = ctx.enter_context(nc.sbuf_tensor(unique("probs_t"), [P, 2, kt, SEQ], F32))
        sm = ctx.enter_context(nc.sbuf_tensor(unique("rows"), [P, 2, 4], F32))
        ps = ctx.enter_context(nc.psum_tensor(unique("scores"), [P, 2, nb, 512], F32))
        pT = ctx.enter_context(nc.psum_tensor(unique("turned"), [P, nb, 4, P], F32))
        po = ctx.enter_context(nc.psum_tensor(unique("mixed"), [P, 2, 512], F32))
        NQ = 4 * heads
        with stage(nc, "scores_ready", "max_ready", "exp_done", "probs_ready", "turned", "turned_copied",
                   "mixed_ready", "mixed_copied", "dve_step") as (
                block, scores_ready, max_ready, exp_done, probs_ready, turned, turned_copied,
                mixed_ready, mixed_copied, dve_step):

            @block.tensor
            def _(pe):
                def scores(n):
                    if n >= 2:
                        pe.wait_ge(exp_done, n - 1)
                    for b, (a, w) in enumerate(cuts):
                        parts = score_parts(n // 4, (n % 4) * P)
                        for m, (q, k) in enumerate(parts):
                            mm = pe.matmul(ps[:, n % 2, b, 0:w], q, k(a, w), start=m == 0,
                                           stop=m == len(parts) - 1)
                    mm.then_inc(scores_ready, 1)

                def turn(n):
                    pe.wait_ge(probs_ready, n + 1)
                    if n:
                        pe.wait_ge(turned_copied, n)
                    for t in range(kt):
                        mm = pe.transpose(pT[:, t // 4, t % 4], pr[:, n % 2, t * P:(t + 1) * P], K["ident"])
                    mm.then_inc(turned, 1)

                def mix(h):
                    pe.wait_ge(turned_copied, 4 * h + 4)
                    if h >= 2:
                        pe.wait_ge(mixed_copied, h - 1)
                    row = 64 * (h % 2) if vrows == 64 else 0
                    for t in range(kt):
                        mm = pe.matmul(po[row:row + vrows, h % 2], values(h, t), pt[:, h % 2, t],
                                       start=t == 0, stop=t == kt - 1)
                    mm.then_inc(mixed_ready, 1)
                scores(0)
                for n in range(NQ):
                    if n + 1 < NQ:
                        scores(n + 1)
                    turn(n)
                    if n % 4 == 0 and n:
                        mix(n // 4 - 1)
                mix(heads - 1)

            def evac(dve, h):
                row = 64 * (h % 2) if vrows == 64 else 0
                dve.wait_ge(mixed_ready, h + 1)
                dve.tensor_copy(out(h), po[row:row + vrows, h % 2]).then_inc(mixed_copied, 1)

            @block.vector
            def _(dve):
                chain = Chain(dve, dve_step)
                for n in range(NQ):
                    dve.wait_ge(scores_ready, n + 1)
                    if n >= 2:
                        dve.wait_ge(exp_done, n - 1)
                    s = sm[:, n % 2]
                    src = ps[:, n % 2, 0, 0:512] if nb == 1 else ps[:, n % 2, :, 0:384]
                    chain.step(dve.tensor_reduce(s[:, 0:1], src, AX.X if nb == 1 else AX.XY, ALU.max))
                    dve.tensor_scalar(s[:, 1:2], s[:, 0:1], -scale, None, ALU.mult).then_inc(max_ready, 1)
                    dve.wait_ge(exp_done, n + 1)
                    chain.step(dve.reciprocal(s[:, 3:4], s[:, 2:3]))
                    dve.tensor_scalar(pr[:, n % 2], pr[:, n % 2], s[:, 3:4], None,
                                      ALU.mult).then_inc(probs_ready, 1)
                    if n % 4 == 1 and n > 4:
                        evac(dve, n // 4 - 1)
                evac(dve, heads - 1)

            @block.scalar
            def _(act):
                def copy(n):
                    act.wait_ge(turned, n + 1)
                    h = n // 4
                    if h >= 2:
                        act.wait_ge(mixed_ready, h - 1)
                    q0 = (n % 4) * P
                    for b in range(nb):
                        c0, c1 = 4 * b, min(4 * b + 4, kt)
                        last = act.activation(pt[:, h % 2, c0:c1, q0:q0 + P], pT[:, b, 0:c1 - c0], ACT.Copy)
                    last.then_inc(turned_copied, 1)
                for n in range(NQ):
                    act.wait_ge(max_ready, n + 1)
                    if n >= 2:
                        act.wait_ge(turned, n - 1)
                    src = ps[:, n % 2, 0, 0:512] if nb == 1 else ps[:, n % 2, :, 0:384]
                    dst = pr[:, n % 2] if nb == 1 else pr[:, n % 2].rearrange("p (b w) -> p b w", b=nb)
                    act.activation(dst, src, ACT.Exp, bias=sm[:, n % 2, 1:2], scale=scale,
                                   accum_out=sm[:, n % 2, 2:3]).then_inc(exp_done, 1)
                    if n:
                        copy(n - 1)
                copy(NQ - 1)


def turn_tiles(nc, K, pairs, group=4):
    with ExitStack() as ctx:
        ps = ctx.enter_context(nc.psum_tensor(unique("turn_ps"), [P, 2, 4, P], F32))
        with stage(nc, "turned", "copied") as (block, turned, copied):
            @block.tensor
            def _(pe):
                for n, (ins, _) in enumerate(pairs):
                    if n >= 2:
                        pe.wait_ge(copied, n - 1)
                    for m, x in enumerate(ins):
                        mm = pe.transpose(ps[:, n % 2, m], x, K["ident"])
                    mm.then_inc(turned, 1)

            @block.vector
            def _(dve):
                for n, (ins, out) in enumerate(pairs):
                    dve.wait_ge(turned, n + 1)
                    dve.tensor_copy(out, ps[:, n % 2, 0:len(ins)]).then_inc(copied, 1)


def ssd(nc, K, c, layer, proj, conv, dt_rows, mixed):
    with ExitStack() as ctx:
        def sb(name, shape):
            return ctx.enter_context(nc.sbuf_tensor(unique(name), shape, F32))

        rows = sb("dt_rows", [64, SEQ])
        tmp = sb("softplus", [48, SEQ])
        acol = sb("a_log", [P, 2])
        cols = sb("dt_cols", [P, LT, 2, 16])
        csl = sb("local_sums", [P, LT, 16])
        gap = sb("between", [P, 2, LT, LT, 8])
        xt = sb("x_tokens", [P, LT, 4 * P])
        sc = sb("scores", [P, 2, LT, SEQ])
        xd = mixed
        PAIRS = [(0, j, i) for j in range(LT) for i in range(j + 1, LT)] + \
                [(1, j, i) for j in range(LT) for i in range(j)]
        with ExitStack() as c2:
            pt = c2.enter_context(nc.psum_tensor(unique("turn_ps"), [P, 2, 4, P], F32))
            pc = c2.enter_context(nc.psum_tensor(unique("col_ps"), [P, 4, P], F32))
            pb = c2.enter_context(nc.psum_tensor(unique("sum_ps"), [P, 512], F32))
            psc = c2.enter_context(nc.psum_tensor(unique("score_ps"), [P, 2, 512], F32))
            with stage(nc, "act_step", "dve_step", "abs_ready", "log_ready", "rows_ready", "cols_turned", "cols_copied",
                       "sums_ready", "sums_copied", "turned", "x_copied", "scores_ready", "scores_copied") as (
                    block, act_step, dve_step, abs_ready, log_ready, rows_ready, cols_turned, cols_copied,
                    sums_ready, sums_copied, turned, x_copied, scores_ready, scores_copied):
                @block.vector
                def _(dve):
                    chain = Chain(dve, dve_step)
                    chain.step(dve.memset(rows[:], 0.0))
                    chain.step(dve.scalar_tensor_tensor(tmp[0:16], dt_rows, -1.0, dt_rows, ALU.mult, ALU.max))
                    dve.nop().then_inc(abs_ready, 1)
                    for n in range(LT):
                        dve.wait_ge(turned, n + 1)
                        dve.tensor_copy(xt[:, n].rearrange("p (m c) -> p m c", m=4),
                                        pt[:, n % 2]).then_inc(x_copied, 1)
                    dve.wait_ge(log_ready, 2)
                    chain.step(dve.scalar_tensor_tensor(rows[0:16], dt_rows, 0.0, tmp[0:16], ALU.max, ALU.add))
                    chain.step(dve.tensor_scalar(rows[32:48], rows[0:16], acol[0:16, 0:1], -1.0,
                                                 ALU.mult, ALU.mult))
                    dve.nop().then_inc(rows_ready, 1)
                    dve.wait_ge(cols_turned, 1)
                    chain.step(dve.tensor_copy(cols[:, :, 0], pc[:, 0:LT, 0:16]))
                    dve.tensor_copy(cols[:, :, 1], pc[:, 0:LT, 32:48]).then_inc(cols_copied, 1)
                    dve.wait_ge(sums_copied, 1)
                    for n, (d, j, i) in enumerate(PAIRS):
                        dve.tensor_tensor(gap[:, d, j, i], gap[:, d, j, i], cols[:, j, 0, 8 * d:8 * d + 8],
                                          ALU.mult)

                @block.scalar
                def _(act):
                    chain = Chain(act, act_step)
                    act.activation(acol[0:16, 0:1], c("a_log", layer)[0:16], ACT.Exp).then_inc(log_ready, 1)
                    act.wait_ge(abs_ready, 1)
                    chain.step(act.activation(tmp[0:16], tmp[0:16], ACT.Exp, scale=-1.0))
                    act.activation(tmp[0:16], tmp[0:16], ACT.Ln, bias=1.0).then_inc(log_ready, 1)
                    for n in range(2 * LT):
                        act.wait_ge(scores_ready, n + 1)
                        act.activation(sc[:, n // LT, n % LT], psc[:, n % 2], ACT.Copy).then_inc(scores_copied, 1)
                    act.wait_ge(sums_ready, 1)
                    act.activation(csl[:].rearrange("p a b -> p (a b)"), pb[:, 0:64], ACT.Copy)
                    for n, (d, j, i) in enumerate(PAIRS):
                        last = act.activation(gap[:, d, j, i], pb[:, 64 + 8 * n:72 + 8 * n], ACT.Exp)
                    last.then_inc(sums_copied, 1)

                @block.tensor
                def _(pe):
                    for n in range(LT):
                        if n >= 2:
                            pe.wait_ge(x_copied, n - 1)
                        for m in range(4):
                            mm = pe.transpose(pt[:, n % 2, m], conv[:, m, n * P:(n + 1) * P], K["ident"])
                        mm.then_inc(turned, 1)
                    for n in range(2 * LT):
                        if n >= 2:
                            pe.wait_ge(scores_copied, n - 1)
                        g, j = n // LT, n % LT
                        pe.matmul(psc[:, n % 2], conv[:, 4 + g, j * P:(j + 1) * P], conv[:, 6 + g],
                                  start=True, stop=True).then_inc(scores_ready, 1)
                    pe.wait_ge(rows_ready, 1)
                    for n in range(LT):
                        mm = pe.transpose(pc[:, n, 0:64], rows[:, n * P:(n + 1) * P], K["ident"][0:64, 0:64])
                    mm.then_inc(cols_turned, 1)
                    pe.wait_ge(cols_copied, 1)
                    for j in range(LT):
                        pe.matmul(pb[:, 16 * j:16 * j + 8], K["le"], cols[:, j, 1, 0:8], start=True, stop=True)
                        pe.matmul(pb[:, 16 * j + 8:16 * j + 16], K["ge"], cols[:, j, 1, 8:16], start=True, stop=True)
                    for n, (d, j, i) in enumerate(PAIRS):
                        between = list(range(j + 1, i)) if d == 0 else list(range(i + 1, j))
                        o = pb[:, 64 + 8 * n:72 + 8 * n]
                        mm = pe.matmul(o, K["gt"] if d == 0 else K["lt"], cols[:, j, 1, 8 * d:8 * d + 8],
                                       start=True, stop=not between)
                        for m in between:
                            mm = pe.matmul(o, K["ones"], cols[:, m, 1, 8 * d:8 * d + 8], start=False,
                                           stop=m == between[-1])
                    mm.then_inc(sums_ready, 1)

        W = sb("weights_st", [P, 2, LT, SEQ])
        E = sb("decay_t", [P, 2, 2, SEQ])
        Dg = sb("decay_diag", [P, 2, 2, LT, P])
        pe_ps = ctx.enter_context(nc.psum_tensor(unique("decay_ps"), [P, 2, 2, 512], F32))
        py = ctx.enter_context(nc.psum_tensor(unique("y_ps"), [P, 2, 512], F32))
        with stage(nc, "sums_ready", "decays_ready", "diag_ready", "diag_exp", "weights_ready", "y_ready", "y_copied", "dve_step") as (
                block, sums_ready, decays_ready, diag_ready, diag_exp, weights_ready, y_ready, y_copied, dve_step):
            @block.tensor
            def _(pe):
                def decays(h):
                    if h >= 2:
                        pe.wait_ge(diag_ready, h - 1)
                        pe.wait_ge(decays_ready, h - 1)
                    for d in range(2):
                        for i in range(LT):
                            a = cols[:, i, 1, 8 * d + h:8 * d + h + 1].broadcast_to([P, P])
                            mm = pe.matmul(pe_ps[:, h % 2, d, i * P:(i + 1) * P], a,
                                           K["le"] if d == 0 else K["ge"], start=True, stop=True)
                    mm.then_inc(sums_ready, 1)
                decays(0)
                for h in range(8):
                    if h + 1 < 8:
                        decays(h + 1)
                    pe.wait_ge(weights_ready, h + 1)
                    if h >= 2:
                        pe.wait_ge(y_copied, h - 1)
                    r = 64 * (h % 2)
                    for j in range(LT):
                        mm = pe.matmul(py[r:r + 64, h % 2], xt[:, j, 64 * h:64 * h + 64], W[:, h % 2, j],
                                       start=j == 0, stop=j == LT - 1)
                    mm.then_inc(y_ready, 1)

            @block.scalar
            def _(act):
                for h in range(8):
                    act.wait_ge(sums_ready, h + 1)
                    if h >= 2:
                        act.wait_ge(weights_ready, h - 1)
                    act.activation(E[:, h % 2], pe_ps[:, h % 2], ACT.Exp).then_inc(decays_ready, 1)
                    act.wait_ge(diag_ready, h + 1)
                    act.activation(Dg[:, h % 2], Dg[:, h % 2], ACT.Exp).then_inc(diag_exp, 1)

            def skip(dve, h):
                r, n = 64 * (h % 2), h // 2
                dve.wait_ge(y_ready, h + 1)
                dve.scalar_tensor_tensor(mixed[r:r + 64, 4 + n, LAT], conv[r:r + 64, n],
                                         c("d_skip", layer)[r:r + 64, n:n + 1], py[r:r + 64, h % 2],
                                         ALU.mult, ALU.add).then_inc(y_copied, 1)

            @block.vector
            def _(dve):
                chain = Chain(dve, dve_step)

                def diag(h):
                    dve.wait_ge(decays_ready, h + 1)
                    dg = Dg[:, h % 2]
                    cs = csl[:].rearrange("p j (d h) -> p d j h", d=2)[:, :, :, h:h + 1].broadcast_to([P, 2, LT, P])
                    chain.step(dve.tensor_tensor(dg, pe_ps[:, h % 2].rearrange("p d (j t) -> p d j t", j=LT), cs,
                                                 ALU.subtract))
                    mask = K["masks"].unsqueeze(2).broadcast_to([P, 2, LT, P])
                    dve.tensor_tensor(dg, dg, mask, ALU.add).then_inc(diag_ready, 1)
                    dve.wait_ge(diag_ready, h + 1)
                diag(0)
                for h in range(8):
                    if h + 1 < 8:
                        diag(h + 1)
                    g = h // 4
                    w = W[:, h % 2]
                    dg = Dg[:, h % 2]
                    if h >= 2:
                        dve.wait_ge(y_ready, h - 1)
                    for d, j, i in PAIRS:
                        dve.scalar_tensor_tensor(w[:, j, i * P:(i + 1) * P], E[:, h % 2, d, i * P:(i + 1) * P],
                                                 gap[:, d, j, i, h:h + 1], sc[:, g, j, i * P:(i + 1) * P],
                                                 ALU.mult, ALU.mult)
                    dve.wait_ge(diag_exp, h + 1)
                    dt = cols[:, :, 0].rearrange("p j (d h) -> p d j h", d=2)[:, :, :, h:h + 1].broadcast_to([P, 2, LT, P])
                    chain.step(dve.tensor_tensor(dg, dg, dt, ALU.mult))
                    chain.step(dve.tensor_tensor(dg[:, 0], dg[:, 0], dg[:, 1], ALU.add))
                    for j in range(LT):
                        last = dve.tensor_tensor(w[:, j, j * P:(j + 1) * P], dg[:, 0, j],
                                                 sc[:, g, j, j * P:(j + 1) * P], ALU.mult)
                    last.then_inc(weights_ready, 1)
                    if h:
                        skip(dve, h - 1)
                skip(dve, 7)
                dve.wait_ge(y_copied, 8)
                for n in range(4):
                    dve.tensor_tensor(mixed[:, 4 + n, LAT], mixed[:, 4 + n, LAT], proj[:, Z_T + n], ALU.mult)


def gated_up(nc, K, weights, h, hid, segs, conv=None):
    total = sum(w for _, w in segs)
    a0 = segs[0][0]
    with ExitStack() as ctx:
        W = ctx.enter_context(nc.sbuf_tensor(unique("w_up"), [P, 2, 2, KT, P], F32))
        gs = ctx.enter_context(nc.sbuf_tensor(unique("gate"), [P, 2, TOK], F32))
        raw = acc = None
        if conv:
            raw = ctx.enter_context(nc.sbuf_tensor(unique("gate_raw"), [P, 2, PADDED], F32))
            acc = ctx.enter_context(nc.sbuf_tensor(unique("gate_conv"), [P, 2, PADDED], F32))
        ps = ctx.enter_context(nc.psum_tensor(unique("gate_up"), [P, 2, 2, 2, 512], F32))
        with stage(nc, "even_arrived", "odd_arrived", "product_ready", "raw_ready", "conv_step", "conv_ready",
                   "gate_ready", "hidden_ready", "pads_zero") as (
                block, even_arrived, odd_arrived, product_ready, raw_ready, conv_step, conv_ready,
                gate_ready, hidden_ready, pads_zero):
            arrived = (even_arrived, odd_arrived)

            @block.sync
            def _(sp):
                stream_weights(sp, weights, [W[:, j].rearrange("p g k m -> p (g k m)") for j in (0, 1)],
                               arrived, product_ready, FT)

            @block.tensor
            def _(pe):
                def tile(j, i):
                    pe.wait_ge(arrived[j], 16 * (i + 1))
                    if later(i):
                        pe.wait_ge(hidden_ready, 2 * i + j - 1)
                    for g in range(2):
                        for k in range(KT):
                            for n, (a, w) in enumerate(segs):
                                mm = pe.matmul(ps[:, j, g, n, 0:w], W[:, j, g, k], h[:, k, a:a + w],
                                               start=k == 0, stop=k == KT - 1)
                    mm.then_inc(product_ready, 1)
                in_pairs(pe, FT, tile)

            pseg = PSEG if len(segs) == 2 else PSEG[1:]
            lo = pseg[0][0]
            span = pseg[-1][0] + pseg[-1][1] - lo

            @block.scalar
            def _(act):
                if conv:
                    act.wait_ge(pads_zero, 1)

                def tile(j, i):
                    act.wait_ge(product_ready, 2 * i + j + 1)
                    if later(i):
                        act.wait_ge(hidden_ready, 2 * i + j - 1)
                    if conv:
                        for n, (_, w) in enumerate(segs):
                            p0 = pseg[n][0]
                            last = act.activation(raw[:, j, p0:p0 + w], ps[:, j, 0, n, 0:w], ACT.Copy)
                        last.then_inc(raw_ready, 1)
                        act.wait_ge(conv_ready, 2 * i + j + 1)
                    for n, (a, w) in enumerate(segs):
                        p0 = pseg[n][0]
                        src = acc[:, j, p0:p0 + w] if conv else ps[:, j, 0, n, 0:w]
                        last = act.activation(gs[:, j, a:a + w], src, ACT.Silu)
                    last.then_inc(gate_ready, 1)
                in_pairs(act, FT, tile)

            @block.vector
            def _(dve):
                if conv:
                    taps = conv[0].rearrange("p (n w) -> p n w", w=3)
                    bias = conv[1].rearrange("p (n w) -> p n w", w=1)
                    dve.memset(raw[:], 0.0).then_inc(pads_zero, 1)

                def tile(j, i):
                    f = 2 * i + j
                    if conv:
                        dve.wait_ge(raw_ready, f + 1)
                        if later(i):
                            dve.wait_ge(gate_ready, f - 1)
                        o = acc[:, j, lo:lo + span]
                        dve.tensor_scalar(o, raw[:, j, lo:lo + span], taps[:, f, 1:2], bias[:, f, 0:1],
                                          ALU.mult, ALU.add).then_inc(conv_step, 1)
                        dve.wait_ge(conv_step, 2 * f + 1)
                        dve.scalar_tensor_tensor(o, raw[:, j, lo - 1:lo - 1 + span], taps[:, f, 0:1], o,
                                                 ALU.mult, ALU.add).then_inc(conv_step, 1)
                        dve.wait_ge(conv_step, 2 * f + 2)
                        dve.scalar_tensor_tensor(o, raw[:, j, lo + 1:lo + 1 + span], taps[:, f, 2:3], o,
                                                 ALU.mult, ALU.add).then_inc(conv_ready, 1)
                    dve.wait_ge(gate_ready, f + 1)
                    for n, (a, w) in enumerate(segs):
                        last = dve.tensor_tensor(hid[:, f, a:a + w], gs[:, j, a:a + w], ps[:, j, 1, n, 0:w],
                                                 ALU.mult)
                    last.then_inc(hidden_ready, 1)
                in_pairs(dve, FT, tile)


def feed_forward(nc, K, X, H, w_up, w_down, segs, conv=None, gate=None):
    with ExitStack() as ctx:
        hid = ctx.enter_context(nc.sbuf_tensor(unique("hidden"), [P, FT, TOK], F32))
        gated_up(nc, K, w_up, H, hid, segs, conv)
        project_residual(nc, w_down, KT, FT, lambda k: [hid[:, k, a:a + w] for a, w in segs], X, segs, gate)


def first_block(nc, K, c, X, dram):
    segs = SEGS[1:]
    for layer in range(2):
        with ExitStack() as ctx:
            def sb(name, shape):
                return ctx.enter_context(nc.sbuf_tensor(unique(name), shape, F32))

            H = sb("normed", [P, KT, TOK])
            rms_norm(nc, K, token_tiles(X, segs), token_tiles(H, segs), segs, KT, D,
                     lambda k, n: c("norm_mix_w", layer)[:, k:k + 1])
            with ExitStack() as mx:
                def sb(name, shape):
                    return mx.enter_context(nc.sbuf_tensor(unique(name), shape, F32))

                proj = sb("proj", [P, X_T, SEQ])
                conv = sb("conv", [P, 8, SEQ])
                dt_rows = sb("dt_raw", [16, SEQ])
                mix_projection(nc, K, c, layer, dram[f"w_in{layer}"], dram[f"w_dt{layer}"], H, proj, conv,
                               dt_rows[:])
                mixed = H
                ssd(nc, K, c, layer, proj, conv, dt_rows[:], mixed)
                group = lambda g: (lambda k, n=None: mixed[:, 4 + 2 * g + k, LAT])
                with nc.sbuf_tensor(unique("ssd_out"), [P, 2, TOK], F32) as sq:
                    for g in range(2):
                        rms_norm(nc, K, group(g), token_tiles(sq, segs), segs, 2, 2 * P,
                                 lambda k, n: c("ssd_norm_w", layer)[:, 2 * g + k:2 * g + k + 1])
                        copy_tiles(nc, [(mixed[:, 4 + 2 * g:6 + 2 * g, LAT], sq[:, :, LAT])])
                tiles = [(proj[:, Q_T + n], c("q_norm_w", layer)) for n in range(4)]
                head_norm_rope(nc, K, tiles + [(proj[:, K_T], c("k_norm_w", layer))], 0, SEQ)
                vt = sb("v_tokens", [P, LT, P])
                turn_tiles(nc, K, [([proj[:, V_T, t * P:(t + 1) * P] for t in range(LT)], vt[:])])

                def parts(h, q0):
                    r = 64 * (h % 2)
                    return [(proj[r:r + 64, Q_T + h // 2, q0:q0 + P],
                             lambda a, w: proj[r:r + 64, K_T, a:a + w])]
                attention(nc, K, 8, SEQ, 64 ** -0.5, parts,
                          lambda h, t: vt[:, t, 64 * (h % 2):64 * (h % 2) + 64], 64,
                          lambda h: mixed[64 * (h % 2):64 * (h % 2) + 64, h // 2, LAT])
                project_residual(nc, dram[f"w_out{layer}"], KT, KT,
                                 lambda k: [mixed[:, k, LAT]], X, segs)
            if K["stop"] == f"mix{layer}":
                return
            rms_norm(nc, K, token_tiles(X, segs), token_tiles(H, segs), segs, KT, D,
                     lambda k, n: c("norm_ffn_w", layer)[:, k:k + 1])
            feed_forward(nc, K, X, H, dram[f"w_up{layer}"], dram[f"w_down{layer}"], segs)
            if K["stop"] == f"ffn{layer}":
                return
    with nc.sbuf_tensor(unique("normed"), [P, KT, TOK], F32) as H:
        rms_norm(nc, K, token_tiles(X, segs), token_tiles(H, segs), segs, KT, D,
                 lambda k, n: c("final_norm_w")[:, k:k + 1])
        copy_tiles(nc, [(X[:, :, LAT], H[:, :, LAT])])


def copy_tiles(nc, pairs):
    with stage(nc, "copied") as (block, copied):
        @block.vector
        def _(dve):
            for dst, src in pairs:
                dve.tensor_copy(dst, src)



HY_T, OG_T, MQ_T, MK_T, MV_T = 0, 12, 16, 20, 24
IN2_TILES = 28
ML_HEADS = 4


def modulation(nc, K, c, layer, weights, mod, gains):
    G = 4
    groups = 6 * KT // G
    with ExitStack() as ctx:
        W = ctx.enter_context(nc.sbuf_tensor(unique("ada_w"), [P, 2, G, KT, P], F32))
        cv = ctx.enter_context(nc.sbuf_tensor(unique("silu_c"), [P, KT, 2], F32))
        ps = ctx.enter_context(nc.psum_tensor(unique("ada_ps"), [P, 2, 512], F32))
        with stage(nc, "even_arrived", "odd_arrived", "product_ready", "silu_ready", "biased", "scales") as (
                block, even_arrived, odd_arrived, product_ready, silu_ready, biased, scales):
            arrived = (even_arrived, odd_arrived)

            @block.sync
            def _(sp):
                stream_weights(sp, weights, [W[:, j].rearrange("p g k m -> p (g k m)") for j in (0, 1)],
                               arrived, product_ready, groups)

            @block.scalar
            def _(act):
                act.activation(cv[:].rearrange("p k v -> p (k v)"), c("conditions"), ACT.Silu).then_inc(silu_ready, 1)

            @block.tensor
            def _(pe):
                pe.wait_ge(silu_ready, 1)

                def group(j, i):
                    pe.wait_ge(arrived[j], 16 * (i + 1))
                    if later(i):
                        pe.wait_ge(biased, 2 * i + j - 1)
                    for g in range(G):
                        for k in range(KT):
                            mm = pe.matmul(ps[:, j, 2 * g:2 * g + 2], W[:, j, g, k], cv[:, k],
                                           start=k == 0, stop=k == KT - 1)
                    mm.then_inc(product_ready, 1)
                in_pairs(pe, groups, group)

            @block.vector
            def _(dve):
                m = mod[:].rearrange("p (n g) v -> p n g v", g=G)
                b = c("ada_b", layer).rearrange("p (n g v) -> p n g v", g=G, v=1)

                def group(j, i):
                    dve.wait_ge(product_ready, 2 * i + j + 1)
                    for v in range(2):
                        last = dve.tensor_tensor(m[:, 2 * i + j, :, v], ps[:, j, v:2 * G:2],
                                                 b[:, 2 * i + j, :, 0], ALU.add)
                    last.then_inc(biased, 1)
                in_pairs(dve, groups, group)
                dve.wait_ge(biased, groups)
                chain = Chain(dve, scales)
                for s, name in ((1, "norm_mix2"), (4, "norm_ffn2")):
                    for v in range(2):
                        o = gains[:, s // 4, :, v]
                        chain.step(dve.tensor_scalar(o, mod[:, s * KT:s * KT + KT, v], 1.0, None, ALU.add))
                        chain.step(dve.tensor_tensor(o, o, c(name, layer), ALU.mult))


def in2_projection(nc, K, c, w_in, w_gates, H, pc, og, hy, qk, v, G):
    with ExitStack() as ctx:
        W = ctx.enter_context(nc.sbuf_tensor(unique("w_in"), [P, 2, KT, P], F32))
        raw = ctx.enter_context(nc.sbuf_tensor(unique("raw"), [P, 2, PADDED], F32))
        acc = ctx.enter_context(nc.sbuf_tensor(unique("acc"), [P, 2, PADDED], F32))
        ps = ctx.enter_context(nc.psum_tensor(unique("proj_ps"), [P, 2, 2, 512], F32))
        rhs = lambda k: [H[:, k, a:a + w] for a, w in SEGS]
        banks = lambda j: [ps[:, j, n, 0:w] for n, (_, w) in enumerate(SEGS)]
        slots = [W[:, j].rearrange("p k m -> p (k m)") for j in (0, 1)]

        def convolved(first, tiles, out, silu):
            with stage(nc, "even_arrived", "odd_arrived", "product_ready", "raw_ready", "conv_step",
                       "conv_ready", "stored", "pads_zero") as (
                    block, even_arrived, odd_arrived, product_ready, raw_ready, conv_step, conv_ready,
                    stored, pads_zero):
                arrived = (even_arrived, odd_arrived)
                taps = c("conv2_w").rearrange("p (n w) -> p n w", w=3)[:, pc[first]:pc[first] + tiles]
                bias = c("conv2_b").rearrange("p (n w) -> p n w", w=1)[:, pc[first]:pc[first] + tiles]

                @block.sync
                def _(sp):
                    stream_weights(sp, w_in[first:first + tiles], slots, arrived, product_ready, tiles)

                @block.tensor
                def _(pe):
                    project(pe, [W[:, 0], W[:, 1]], KT, rhs, banks, arrived, raw_ready, product_ready, tiles)

                @block.scalar
                def _(act):
                    act.wait_ge(pads_zero, 1)

                    def tile(j, i):
                        act.wait_ge(product_ready, 2 * i + j + 1)
                        if later(i):
                            act.wait_ge(conv_ready, 2 * i + j - 1)
                        for n, (p0, w) in enumerate(PSEG):
                            last = act.activation(raw[:, j, p0:p0 + w], ps[:, j, n, 0:w], ACT.Copy)
                        last.then_inc(raw_ready, 1)
                        act.wait_ge(conv_ready, 2 * i + j + 1)
                        for n, (a, w) in enumerate(SEGS):
                            p0 = PSEG[n][0]
                            last = act.activation(out[:, 2 * i + j, a:a + w], acc[:, j, p0:p0 + w],
                                                  ACT.Silu if silu else ACT.Copy)
                        last.then_inc(stored, 1)
                    in_pairs(act, tiles, tile)

                @block.vector
                def _(dve):
                    dve.memset(raw[:], 0.0).then_inc(pads_zero, 1)

                    def tile(j, i):
                        f = 2 * i + j
                        dve.wait_ge(raw_ready, f + 1)
                        if later(i):
                            dve.wait_ge(stored, f - 1)
                        o = acc[:, j, 1:PADDED - 1]
                        dve.tensor_scalar(o, raw[:, j, 1:PADDED - 1], taps[:, f, 1:2], bias[:, f, 0:1],
                                          ALU.mult, ALU.add).then_inc(conv_step, 1)
                        dve.wait_ge(conv_step, 2 * f + 1)
                        dve.scalar_tensor_tensor(o, raw[:, j, 0:PADDED - 2], taps[:, f, 0:1], o,
                                                 ALU.mult, ALU.add).then_inc(conv_step, 1)
                        dve.wait_ge(conv_step, 2 * f + 2)
                        dve.scalar_tensor_tensor(o, raw[:, j, 2:PADDED], taps[:, f, 2:3], o,
                                                 ALU.mult, ALU.add).then_inc(conv_ready, 1)
                    in_pairs(dve, tiles, tile)

        def plain(weights, tiles, out, func, bias=0.0):
            with stage(nc, "even_arrived", "odd_arrived", "product_ready", "stored") as (
                    block, even_arrived, odd_arrived, product_ready, stored):
                arrived = (even_arrived, odd_arrived)

                @block.sync
                def _(sp):
                    stream_weights(sp, weights, slots, arrived, product_ready, tiles)

                @block.tensor
                def _(pe):
                    project(pe, [W[:, 0], W[:, 1]], KT, rhs, banks, arrived, stored, product_ready, tiles)

                @block.scalar
                def _(act):
                    def tile(j, i):
                        act.wait_ge(product_ready, 2 * i + j + 1)
                        for n, (a, w) in enumerate(SEGS):
                            last = act.activation(out[:, 2 * i + j, a:a + w], ps[:, j, n, 0:w], func, bias=bias)
                        last.then_inc(stored, 1)
                    in_pairs(act, tiles, tile)

        convolved(HY_T, 12, hy, False)
        plain(w_in[OG_T:OG_T + 4], 4, og, ACT.Sigmoid)
        convolved(MQ_T, 8, qk, True)
        plain(w_in[MV_T:MV_T + 4], 4, v, ACT.Copy)
        plain(w_gates, 1, G, ACT.Identity, c("gate_b"))


def gate_sums(nc, K, G, rows, acol, t, one):
    with ExitStack() as ctx:
        ps = ctx.enter_context(nc.psum_tensor(unique("col_ps"), [P, 6, 64], F32))
        with stage(nc, "dve_step", "abs_ready", "log_ready", "cols_turned", "rows_ready", "act_step") as (
                block, dve_step, abs_ready, log_ready, cols_turned, rows_ready, act_step):
            b, a, M, em = (rows[:, n] for n in range(4))

            @block.vector
            def _(dve):
                chain = Chain(dve, dve_step)
                chain.step(dve.memset(one, 1.0))
                chain.step(dve.tensor_copy(t[:, 0], G[64:128, 0]))
                chain.step(dve.scalar_tensor_tensor(t[:, 1], t[:, 0], -1.0, t[:, 0], ALU.mult, ALU.max))
                dve.nop().then_inc(abs_ready, 1)
                dve.wait_ge(log_ready, 1)
                chain.step(dve.scalar_tensor_tensor(t[:, 0], t[:, 0], 0.0, t[:, 1], ALU.min, ALU.subtract))

                def scans(out, d0, d1, op0, op1):
                    chain.step(dve.tensor_tensor_scan(out[0:32], d0[0:32], d1[0:32], 0.0, op0, op1))
                    chain.step(dve.tensor_tensor_scan(out[32:64, CTX - 1::-1], d0[32:64, CTX - 1::-1],
                                                      d1[32:64, CTX - 1::-1], 0.0, op0, op1))
                    chain.step(dve.tensor_tensor_scan(out[32:64, TOK - 1:CTX - 1:-1],
                                                      d0[32:64, TOK - 1:CTX - 1:-1],
                                                      d1[32:64, TOK - 1:CTX - 1:-1], out[32:64, 0:1], op0, op1))
                scans(b, one, t[:, 0], ALU.mult, ALU.add)
                chain.step(dve.tensor_tensor(a, G[0:64, 0], b, ALU.subtract))
                scans(M, a, a, ALU.max, ALU.max)
                chain.step(dve.tensor_tensor(em, M, b, ALU.add))
                chain.step(dve.tensor_scalar(M, M, -1.0, None, ALU.mult))
                dve.nop().then_inc(rows_ready, 1)
                dve.wait_ge(cols_turned, 1)
                dve.tensor_copy(acol[:], ps[:])

            @block.scalar
            def _(act):
                chain = Chain(act, act_step)
                act.wait_ge(abs_ready, 1)
                chain.step(act.activation(t[:, 1], t[:, 1], ACT.Exp, scale=-1.0))
                act.activation(t[:, 1], t[:, 1], ACT.Ln, bias=1.0).then_inc(log_ready, 1)
                act.wait_ge(rows_ready, 1)
                act.activation(em, em, ACT.Exp, scale=-1.0)

            @block.tensor
            def _(pe):
                pe.wait_ge(rows_ready, 1)
                for n in range(6):
                    mm = pe.transpose(ps[:, n], a[:, n * P:(n + 1) * P], K["ident"][0:64, 0:64])
                mm.then_inc(cols_turned, 1)


def mlstm(nc, K, c, qkv, og, S, Dc, mixed):
    with ExitStack() as ctx:
        def sb(name, shape):
            return ctx.enter_context(nc.sbuf_tensor(unique(name), shape, F32))
        rows = sb("gate_rows", [64, 4, TOK])
        acol = sb("a_cols", [P, 6, 64])
        Pw = sb("weights_st", [P, 2, TOK])
        den = sb("den", [P, 2, TOK])
        gate_sums(nc, K, Dc, rows, acol, Pw[0:64], den[0:64, 0])
        vt = sb("v_tokens", [P, 6, 4, P])
        turn_tiles(nc, K, [([S[:, h, t * P:(t + 1) * P] for h in range(4)], vt[:, t]) for t in range(6)])
        Mb = sb("m_rows", [P, 2, 2, TOK])
        psb = ctx.enter_context(nc.psum_tensor(unique("row_ps"), [P, 2, 512], F32))
        pss = ctx.enter_context(nc.psum_tensor(unique("score_ps"), [P, 2, 512], F32))
        pn = ctx.enter_context(nc.psum_tensor(unique("num_ps"), [P, 2, 512], F32))
        pd = ctx.enter_context(nc.psum_tensor(unique("den_ps"), [P, 2, 512], F32))

        def spans(d, j):
            s0 = j * P
            if d == 0:
                return [(0, s0, CTX - s0), (1, CTX, SEQ)] if j < 2 else [(1, s0, TOK - s0)]
            return [(0, 0, s0 + P), (1, CTX, SEQ)] if j < 2 else [(1, CTX, s0 + P - CTX)]

        def off_diagonal(d, j):
            cut = [(a + P if d == 0 and a == j * P else a, w - P if a <= j * P < a + w else w)
                   for _, a, w in spans(d, j)]
            return [(a, w) for a, w in cut if w]
        ORDER = ((0, 1, 2, 3, 4, 5), (1, 0, 5, 4, 3, 2))
        RUNS = [(h, d) for h in range(4) for d in range(2)]
        STEPS = [(h, d, j) for h, d in RUNS for j in ORDER[d]]
        SCORES = [(h, j, seg) for h in range(4) for j in range(6) for seg in ((0, 1) if j < 2 else (1,))]
        PER_HEAD = len(SCORES) // 4

        with stage(nc, "rows_spread", "rows_copied", "scores_ready", "scores_copied", "masked", "decays_ready",
                   "weights_ready", "weights_used", "out_done", "dve_step") as (
                block, rows_spread, rows_copied, scores_ready, scores_copied, masked, decays_ready,
                weights_ready, weights_used, out_done, dve_step):

            @block.tensor
            def _(pe):
                def spread(n):
                    h, d = RUNS[n]
                    for m in range(2):
                        if 2 * n + m:
                            pe.wait_ge(rows_copied, 2 * n + m)
                        sel = K["ident"][0:64, 32 * d + h:32 * d + h + 1].broadcast_to([64, P])
                        for seg, (a, w) in enumerate(SEGS):
                            mm = pe.matmul(psb[:, seg, 0:w], sel, rows[:, 2 + m, a:a + w], start=True, stop=True)
                        mm.then_inc(rows_spread, 1)

                def scores(h):
                    for n in range(PER_HEAD * h, PER_HEAD * (h + 1)):
                        _, j, seg = SCORES[n]
                        if n >= 2:
                            pe.wait_ge(scores_copied, n - 1)
                        a, w = SEGS[seg]
                        pe.matmul(pss[:, n % 2, 0:w], qkv[:, 4 + h, j * P:(j + 1) * P], qkv[:, h, a:a + w],
                                  start=True, stop=True).then_inc(scores_ready, 1)
                spread(0)
                for n, (h, d) in enumerate(RUNS):
                    if d == 0:
                        scores(h)
                    if n + 1 < 8:
                        spread(n + 1)
                    if n:
                        pe.wait_ge(out_done, n)
                    begun = set()
                    for m, j in enumerate(ORDER[d]):
                        pe.wait_ge(weights_ready, 6 * n + m + 1)
                        for seg, a, w in spans(d, j):
                            o = a - SEGS[seg][0]
                            x = Pw[:, m % 2, a:a + w]
                            end = m == 5 or (seg == 0 and m == 1)
                            pe.matmul(pn[:, seg, o:o + w], vt[:, j, h], x, start=seg not in begun, stop=end)
                            mm = pe.matmul(pd[:, seg, o:o + w], K["ones"], x, start=seg not in begun, stop=end)
                            begun.add(seg)
                        mm.then_inc(weights_used, 1)

            @block.scalar
            def _(act):
                def copy_rows(n):
                    for m in range(2):
                        act.wait_ge(rows_spread, 2 * n + m + 1)
                        if n >= 2:
                            act.wait_ge(out_done, n - 1)
                        for seg, (a, w) in enumerate(SEGS):
                            last = act.activation(Mb[:, n % 2, m, a:a + w], psb[:, seg, 0:w], ACT.Copy)
                        last.then_inc(rows_copied, 1)

                def copy_scores(h):
                    for n in range(PER_HEAD * h, PER_HEAD * (h + 1)):
                        _, j, seg = SCORES[n]
                        act.wait_ge(scores_ready, n + 1)
                        if h:
                            act.wait_ge(weights_ready, 12 * h)
                        a, w = SEGS[seg]
                        act.activation(S[:, j, a:a + w], pss[:, n % 2, 0:w], ACT.Copy,
                                       scale=P ** -0.5).then_inc(scores_copied, 1)
                copy_rows(0)
                for n, (h, d) in enumerate(RUNS):
                    if d == 0:
                        copy_scores(h)
                    if n + 1 < 8:
                        copy_rows(n + 1)
                    act.wait_ge(rows_copied, 2 * n + 2)
                    for m, j in enumerate(ORDER[d]):
                        q = 6 * n + m
                        if q >= 2:
                            act.wait_ge(weights_ready, q - 1)
                        r = 32 * d + h
                        for a, w in off_diagonal(d, j):
                            act.activation(Dc[:, m % 2, a:a + w], Mb[:, n % 2, 0, a:a + w], ACT.Exp,
                                           bias=acol[:, j, r:r + 1])
                        act.wait_ge(masked, q + 1)
                        act.activation(Dc[:, m % 2, j * P:(j + 1) * P], den[:, 0, q % 2 * P:q % 2 * P + P],
                                       ACT.Exp).then_inc(decays_ready, 1)

            @block.vector
            def _(dve):
                chain = Chain(dve, dve_step)

                def mask(q):
                    h, d, j = STEPS[q]
                    n = q // 6
                    r = 32 * d + h
                    dve.wait_ge(rows_copied, 2 * n + 2)
                    if q >= 2:
                        dve.wait_ge(decays_ready, q - 1)
                    dve.scalar_tensor_tensor(den[:, 0, q % 2 * P:q % 2 * P + P],
                                             Mb[:, n % 2, 0, j * P:(j + 1) * P], acol[:, j, r:r + 1],
                                             K["mask_f"] if d == 0 else K["mask_b"],
                                             ALU.add, ALU.add).then_inc(masked, 1)
                mask(0)
                for n, (h, d) in enumerate(RUNS):
                    if d == 0:
                        dve.wait_ge(scores_copied, PER_HEAD * (h + 1))
                    for m, j in enumerate(ORDER[d]):
                        q = 6 * n + m
                        if q + 1 < 48 and m < 5:
                            mask(q + 1)
                        dve.wait_ge(decays_ready, q + 1)
                        if q >= 2:
                            dve.wait_ge(weights_used, q - 1)
                        for seg, a, w in spans(d, j):
                            last = dve.tensor_tensor(Pw[:, m % 2, a:a + w], Dc[:, m % 2, a:a + w],
                                                     S[:, j, a:a + w], ALU.mult)
                        last.then_inc(weights_ready, 1)
                    if n + 1 < 8:
                        mask(6 * n + 6)
                    dve.wait_ge(weights_used, 6 * n + 6)
                    for seg, (a, w) in enumerate(SEGS):
                        o = den[:, 1, a:a + w]
                        num, dn = pn[:, seg, 0:w], pd[:, seg, 0:w]
                        chain.step(dve.tensor_copy(o, dn))
                        chain.step(dve.scalar_tensor_tensor(o, o, -1.0, o, ALU.mult, ALU.max))
                        chain.step(dve.tensor_tensor(o, o, Mb[:, n % 2, 1, a:a + w], ALU.max))
                        chain.step(dve.reciprocal(o, o))
                        t = mixed[:, 4 + h, a:a + w]
                        if d == 0:
                            chain.step(dve.tensor_tensor(t, num, o, ALU.mult))
                        else:
                            chain.step(dve.tensor_tensor(o, num, o, ALU.mult))
                            chain.step(dve.tensor_tensor(t, t, o, ALU.add))
                    dve.nop().then_inc(out_done, 1)
    for h in range(4):
        one = lambda k, n=None: mixed[:, 4 + h] if n is None else mixed[:, 4 + h, SEGS[n][0]:SEGS[n][0] + SEGS[n][1]]
        dst = lambda k, n=None: qkv[:, h] if n is None else qkv[:, h, SEGS[n][0]:SEGS[n][0] + SEGS[n][1]]
        rms_norm(nc, K, one, dst, SEGS, 1, P, lambda k, n: c("ml_norm")[:, h:h + 1])
    with stage(nc, "gated") as (block, gated):
        @block.vector
        def _(dve):
            dve.tensor_tensor(mixed[:, 4:8], qkv[:, 0:4], og[:], ALU.mult)


def hyena(nc, K, c, hy, dram, mixed):
    with ExitStack() as ctx:
        def sb(name, shape):
            return ctx.enter_context(nc.sbuf_tensor(unique(name), shape, F32))
        fw = sb("filter_w", [64, 2 * SEQ + 64 + 64])
        z = sb("positions", [33, TOK])
        hid = sb("filter_hidden", [64, 2, TOK])
        with ExitStack() as c2:
            t = c2.enter_context(nc.sbuf_tensor(unique("turns"), [64, 2, TOK], F32))
            ps = c2.enter_context(nc.psum_tensor(unique("hid_ps"), [64, 2, 2, 512], F32))
            with stage(nc, "arrived", "product_ready", "angle_ready", "sine_ready", "dve_step", "g_done") as (
                    block, arrived, product_ready, angle_ready, sine_ready, dve_step, g_done):
                @block.sync
                def _(sp):
                    sp.dma_start(fw[:], dram["filter_w"]).then_inc(arrived, 16)
                    sp.dma_start(z[:], dram["positions"]).then_inc(arrived, 16)

                @block.tensor
                def _(pe):
                    pe.wait_ge(arrived, 32)
                    for n in range(2):
                        if n:
                            pe.wait_ge(sine_ready, 1)
                        for seg, (a, w) in enumerate(SEGS):
                            if n == 0:
                                mm = pe.matmul(ps[:, n, seg, 0:w], fw[0:33, 0:64], z[:, a:a + w],
                                               start=True, stop=True)
                            else:
                                mm = pe.matmul(ps[:, n, seg, 0:w], fw[:, 64:128], hid[:, 0, a:a + w],
                                               start=True, stop=True)
                        mm.then_inc(product_ready, 1)

                @block.vector
                def _(dve):
                    chain = Chain(dve, dve_step)
                    for m in range(4):
                        dve.tensor_tensor(hy[:, 8 + m], hy[:, 8 + m], hy[:, 4 + m], ALU.mult)
                    MAGIC, INV = 12582912.0, float(np.float32(1 / (2 * np.pi)))
                    HI = 6.28125
                    MID = float(np.float32(2 * np.pi - HI))
                    LO = float(2 * np.pi - HI - MID)
                    for n in range(2):
                        dve.wait_ge(product_ready, n + 1)
                        u, r = t[:, 0], t[:, 1]
                        for seg, (a, w) in enumerate(SEGS):
                            chain.step(dve.tensor_scalar(u[:, a:a + w], ps[:, n, seg, 0:w],
                                                         c("filter_b")[0:64, n:n + 1],
                                                         c("filter_freq")[0:64, 0:1], ALU.add, ALU.mult))
                        chain.step(dve.tensor_scalar(r, u, INV, MAGIC, ALU.mult, ALU.add))
                        chain.step(dve.tensor_scalar(r, r, MAGIC, None, ALU.subtract))
                        for part in (HI, MID, LO):
                            chain.step(dve.scalar_tensor_tensor(u, r, -part, u, ALU.mult, ALU.add))
                        chain.step(dve.tensor_scalar(u, u, 3.1415925, -3.1415925, ALU.min, ALU.max))
                        dve.nop().then_inc(angle_ready, 1)
                        if n == 0:
                            dve.wait_ge(sine_ready, 1)

                @block.scalar
                def _(act):
                    for n in range(2):
                        act.wait_ge(angle_ready, n + 1)
                        act.activation(hid[:, n], t[:, 0], ACT.Sin).then_inc(sine_ready, 1)

        gt = sb("g_tokens", [P, LT, SEQ])
        fl = sb("filters", [P, 2, LT, SEQ])
        dc = sb("filter_decay", [P, LT, SEQ])
        F = sb("dft", [P, 2, LT, SEQ])
        Y = sb("spectrum", [P, LT, 2, SEQ])
        gs = sb("g_spectrum", [P, 2, SEQ])
        t = sb("products", [P, 4, SEQ])
        for seg, (a0, L) in enumerate(SEGS):
            lt = L // P
            turn_tiles(nc, K, [([hy[:, 8 + m, a0 + s * P:a0 + (s + 1) * P] for m in range(4)],
                                gt[:, s].rearrange("p (m q) -> p m q", m=4)) for s in range(lt)])
            with ExitStack() as c2:
                ph = c2.enter_context(nc.psum_tensor(unique("filter_ps"), [P, 2, 2, 512], F32))
                with stage(nc, "arrived", "product_ready", "shaped", "zeroed", "summed", "dve_step") as (
                        block, arrived, product_ready, shaped, zeroed, summed, dve_step):
                    @block.sync
                    def _(sp):
                        sp.dma_start(dc[:, 0:lt], dram[f"decay{seg}"]).then_inc(arrived, 16)
                        for m in range(2):
                            sp.dma_start(F[:, m, 0:lt, 0:L], dram[f"dft{seg}"][m]).then_inc(arrived, 16)
                        sp.wait_ge(arrived, 48)

                    @block.tensor
                    def _(pe):
                        for s in range(lt):
                            if s >= 2:
                                pe.wait_ge(shaped, s - 1)
                            for m in range(2):
                                mm = pe.matmul(ph[:, s % 2, m], hid[:, 1, a0 + s * P:a0 + (s + 1) * P],
                                               fw[:, 128 + m * SEQ:128 + (m + 1) * SEQ], start=True, stop=True)
                            mm.then_inc(product_ready, 1)

                    @block.vector
                    def _(dve):
                        chain = Chain(dve, dve_step)
                        dve.wait_ge(arrived, 48)
                        for s in range(lt):
                            dve.wait_ge(product_ready, s + 1)
                            chain.step(dve.tensor_tensor(t[:, 0], ph[:, s % 2, 0], dc[:, s], ALU.mult))
                            dve.tensor_tensor(t[:, 1], ph[:, s % 2, 1], dc[:, s], ALU.mult).then_inc(shaped, 1)
                            dve.wait_ge(shaped, s + 1)
                            if s == 0:
                                chain.step(dve.memset(t[0:1, 1], 0.0))
                            chain.step(dve.tensor_tensor(fl[:, 0, s], t[:, 0], t[:, 1], ALU.add))
                            chain.step(dve.tensor_tensor(fl[:, 1, s], t[:, 1], t[:, 0], ALU.subtract))
                pf = c2.enter_context(nc.psum_tensor(unique("spec_ps"), [P, 4, 512], F32))
                with stage(nc, "spectra_ready", "g_copied", "product_step", "spectrum_done") as (
                        block, spectra_ready, g_copied, product_step, spectrum_done):
                    @block.tensor
                    def _(pe):
                        for k in range(lt):
                            if k:
                                pe.wait_ge(spectrum_done, k)
                            for q, (table, x) in enumerate(((0, gt), (1, gt), (0, fl[:, 0]), (1, fl[:, 1]))):
                                for s in range(lt):
                                    mm = pe.matmul(pf[:, q], F[:, table, s, k * P:(k + 1) * P], x[:, s],
                                                   start=s == 0, stop=s == lt - 1)
                            mm.then_inc(spectra_ready, 1)

                    @block.scalar
                    def _(act):
                        for k in range(lt):
                            act.wait_ge(spectra_ready, k + 1)
                            if k:
                                act.wait_ge(spectrum_done, k)
                            act.activation(gs[:], pf[:, 0:2], ACT.Copy).then_inc(g_copied, 1)

                    @block.vector
                    def _(dve):
                        for k in range(lt):
                            dve.wait_ge(g_copied, k + 1)
                            if k:
                                dve.wait_ge(spectrum_done, k)
                            for n, (g, f) in enumerate(((0, 2), (1, 3), (1, 2), (0, 3))):
                                dve.tensor_tensor(t[:, n], gs[:, g], pf[:, f], ALU.mult).then_inc(product_step, 1)
                            dve.wait_ge(product_step, 4 * k + 4)
                            dve.tensor_tensor(Y[:, k, 0], t[:, 0], t[:, 1], ALU.add)
                            dve.tensor_tensor(Y[:, k, 1], t[:, 2], t[:, 3], ALU.subtract).then_inc(spectrum_done, 1)
                with stage(nc, "even_arrived", "y_ready", "y_done", "dve_step") as (block, arrived, y_ready, y_done, dve_step):
                    @block.sync
                    def _(sp):
                        for m in range(2):
                            sp.dma_start(F[:, m, 0:lt, 0:L], dram[f"idft{seg}"][m]).then_inc(arrived, 16)

                    @block.tensor
                    def _(pe):
                        pe.wait_ge(arrived, 32)
                        for m in range(4):
                            for k in range(lt):
                                for q in range(2):
                                    mm = pe.matmul(pf[:, m, 0:L], Y[:, k, q, m * P:(m + 1) * P], F[:, q, k, 0:L],
                                                   start=k == 0 and q == 0, stop=k == lt - 1 and q == 1)
                            mm.then_inc(y_ready, 1)

                    @block.vector
                    def _(dve):
                        chain = Chain(dve, dve_step)
                        for m in range(4):
                            dve.wait_ge(y_ready, m + 1)
                            o = t[:, m, 0:L]
                            chain.step(dve.scalar_tensor_tensor(o, hy[:, 8 + m, a0:a0 + L], c("hy_bias")[:, m:m + 1],
                                                                pf[:, m, 0:L], ALU.mult, ALU.add))
                            dve.tensor_tensor(mixed[:, m, a0:a0 + L], o, hy[:, m, a0:a0 + L], ALU.mult)


def plain_projection(nc, weights, tiles, kt, rhs, out, segs):
    with ExitStack() as ctx:
        W = ctx.enter_context(nc.sbuf_tensor(unique("weights"), [P, 2, kt, P], F32))
        ps = ctx.enter_context(nc.psum_tensor(unique("product"), [P, 2, 2, 512], F32))
        with stage(nc, "even_arrived", "odd_arrived", "product_ready", "stored") as (
                block, even_arrived, odd_arrived, product_ready, stored):
            arrived = (even_arrived, odd_arrived)

            @block.sync
            def _(sp):
                stream_weights(sp, weights, [W[:, j].rearrange("p k m -> p (k m)") for j in (0, 1)],
                               arrived, product_ready, tiles)

            @block.tensor
            def _(pe):
                project(pe, [W[:, 0], W[:, 1]], kt, rhs,
                        lambda j: [ps[:, j, n, 0:w] for n, (_, w) in enumerate(segs)],
                        arrived, stored, product_ready, tiles)

            @block.scalar
            def _(act):
                def tile(j, i):
                    act.wait_ge(product_ready, 2 * i + j + 1)
                    for n, (a, w) in enumerate(segs):
                        last = act.activation(out[:, 2 * i + j, a:a + w], ps[:, j, n, 0:w], ACT.Copy)
                    last.then_inc(stored, 1)
                in_pairs(act, tiles, tile)


def mla(nc, K, c, H, dram, mixed):
    with ExitStack() as ctx:
        def sb(name, shape):
            return ctx.enter_context(nc.sbuf_tensor(unique(name), shape, F32))
        down = sb("latent", [P, 6, TOK])
        plain_projection(nc, dram["mla_down"], 6, KT, lambda k: [H[:, k, a:a + w] for a, w in SEGS], down, SEGS)
        lat = sb("latent_normed", [P, 5, TOK])
        lseg = SEGS[1:]
        part = lambda buf, n0, segs: (lambda k, n=None: token_tiles(buf, segs)(n0 + k, n))
        rms_norm(nc, K, part(down, 0, lseg), part(lat, 0, lseg), lseg, 3, 3 * P,
                 lambda k, n: c("mla_q_norm")[:, k:k + 1])
        rms_norm(nc, K, part(down, 3, SEGS), part(lat, 3, SEGS), SEGS, 2, 2 * P,
                 lambda k, n: c("mla_kv_norm")[:, k:k + 1])
        q = sb("queries", [P, 12, SEQ])
        plain_projection(nc, dram["mla_uq"], 12, 3, lambda k: [lat[:, k, LAT]], q, [(0, SEQ)])
        head_norm_rope(nc, K, [(q[:, 8 + n], None) for n in range(4)] + [(down[:, 5, LAT], None)], 0, SEQ)
        kn = sb("keys", [P, 8, TOK])
        plain_projection(nc, dram["mla_uk"], 8, 2, lambda k: [lat[:, 3 + k, a:a + w] for a, w in SEGS], kn, SEGS)
        vt = sb("v_tokens", [P, 6, D])
        with ExitStack() as c2:
            W = c2.enter_context(nc.sbuf_tensor(unique("w_v"), [P, 2, D], F32))
            ps = c2.enter_context(nc.psum_tensor(unique("v_ps"), [P, 2, 2, 512], F32))
            with stage(nc, "arrived", "v_ready", "v_copied") as (block, arrived, v_ready, v_copied):
                @block.sync
                def _(sp):
                    sp.dma_start(W[:], dram["mla_uv"]).then_inc(arrived, 16)

                @block.tensor
                def _(pe):
                    pe.wait_ge(arrived, 16)
                    for t in range(6):
                        if t >= 2:
                            pe.wait_ge(v_copied, t - 1)
                        for k in range(2):
                            for n in range(2):
                                mm = pe.matmul(ps[:, t % 2, n], lat[:, 3 + k, t * P:(t + 1) * P],
                                               W[:, k, n * 512:(n + 1) * 512], start=k == 0, stop=k == 1)
                        mm.then_inc(v_ready, 1)

                @block.scalar
                def _(act):
                    for t in range(6):
                        act.wait_ge(v_ready, t + 1)
                        act.activation(vt[:, t].rearrange("p (n w) -> p n w", n=2), ps[:, t % 2],
                                       ACT.Copy).then_inc(v_copied, 1)

        def parts(h, q0):
            r = 64 * (h % 2)
            return [(q[:, h, q0:q0 + P], lambda a, w: kn[:, h, a:a + w]),
                    (q[r:r + 64, 8 + h // 2, q0:q0 + P], lambda a, w: down[r:r + 64, 5, a:a + w])]
        attention(nc, K, 8, TOK, 192 ** -0.5, parts, lambda h, t: vt[:, t, h * P:(h + 1) * P], P,
                  lambda h: mixed[:, h, LAT])


def second_block(nc, K, c, X, dram):
    mod = [dram.pop("mod0"), dram.pop("mod1")]
    for layer in range(2):
        segs = SEGS if layer == 0 else SEGS[1:]
        n0 = len(SEGS) - len(segs)
        m, gains = mod[layer]
        modulation(nc, K, c, layer, dram[f"ada{layer}"], m, gains)
        gain = lambda which, seg0=0: (lambda k, n: gains[:, which, k, 1 - n - seg0:2 - n - seg0])
        vec = lambda which, seg0=0: (lambda k, n: m[:, which * KT:which * KT + KT][:, k, 1 - n - seg0:2 - n - seg0])
        with ExitStack() as ctx:
            def sb(name, shape):
                return ctx.enter_context(nc.sbuf_tensor(unique(name), shape, F32))
            H = sb("normed", [P, KT, TOK])
            rms_norm(nc, K, token_tiles(X, SEGS), token_tiles(H, SEGS), SEGS, KT, D, gain(0), vec(0))
            if layer == 0:
                with ExitStack() as hx:
                    hy = hx.enter_context(nc.sbuf_tensor(unique("hyena_in"), [P, 12, TOK], F32))
                    with ExitStack() as mx:
                        og = mx.enter_context(nc.sbuf_tensor(unique("out_gate"), [P, 4, TOK], F32))
                        qk = mx.enter_context(nc.sbuf_tensor(unique("qk"), [P, 8, TOK], F32))
                        S = mx.enter_context(nc.sbuf_tensor(unique("scores"), [P, 6, TOK], F32))
                        Dc = mx.enter_context(nc.sbuf_tensor(unique("decays"), [P, 2, TOK], F32))
                        in2_projection(nc, K, c, dram["w_in2"], dram["w_gates"], H, {HY_T: 0, MQ_T: 12},
                                       og, hy, qk, S[:, 0:4], Dc)
                        mlstm(nc, K, c, qk, og, S, Dc, H)
                    if K["stop"] == "ml":
                        return H
                    hyena(nc, K, c, hy, dram, H)
                    if K["stop"] == "hy":
                        return H
            else:
                mla(nc, K, c, H, dram, H)
                if K["stop"] == "mla":
                    return H
            project_residual(nc, dram[f"w_out2{layer}"], KT, KT,
                             lambda k: [H[:, k, a:a + w] for a, w in segs], X, segs, lambda k, n: vec(2, n0)(k, n))
            if K["stop"] == f"mix2{layer}":
                return X
            rms_norm(nc, K, token_tiles(X, segs), token_tiles(H, segs), segs, KT, D, gain(1, n0), vec(3, n0))
            feed_forward(nc, K, X, H, dram[f"w_up2{layer}"], dram[f"w_down2{layer}"], segs,
                         (c("ffn_conv_w", layer), c("ffn_conv_b", layer)), vec(5, n0))
            if K["stop"] == f"ffn2{layer}":
                return X



CONSTS = ["ident", "ones", "ones64", "swap", "le", "ge", "gt", "lt", "mask_f", "mask_b"]


def build(nc, ins, places, out, stop=None):
    K = {"stop": stop}
    with ExitStack() as ctx:
        def sb(name, shape):
            return ctx.enter_context(nc.sbuf_tensor(name, shape, F32))
        X = sb("x", [P, KT, TOK])
        C = sb("consts", [P, len(CONSTS), P])
        R = sb("rope", [P, 2, SEQ])
        V = sb("vectors", list(ins["vectors"].shape))
        eps = sb("eps", [P, 1])
        mods = [(sb(f"mod{n}", [P, 6 * KT, 2]), sb(f"gains{n}", [P, 2, KT, 2])) for n in range(2)]
        for n, name in enumerate(CONSTS):
            K[name] = C[:, n]
        K["masks"] = C[:, 8:10]
        K["rope_cos"], K["rope_sin"] = R[:, 0], R[:, 1]
        K["eps"] = eps[:]

        def c(name, layer=None):
            a, w = places[name if layer is None else f"{name}{layer}"]
            return V[:, a:a + w]

        with stage(nc, "arrived") as (block, arrived):
            @block.sync
            def _(sp):
                sp.dma_start(X[:, :, LAT], ins["x"]).then_inc(arrived, 16)
                sp.dma_start(X[:, :, 0:CTX], ins["ctx"]).then_inc(arrived, 16)
                sp.dma_start(C[:], ins["consts"]).then_inc(arrived, 16)
                sp.dma_start(R[:], ins["rope"]).then_inc(arrived, 16)
                sp.dma_start(V[:], ins["vectors"]).then_inc(arrived, 16)
                sp.wait_ge(arrived, 80)

            @block.vector
            def _(dve):
                dve.memset(eps[:], EPS)
        result = X
        dram = dict(ins)
        first_block(nc, K, c, X, dram)
        if stop is None or stop not in ("mix0", "ffn0", "mix1", "ffn1", "first"):
            dram["mod0"], dram["mod1"] = mods
            kept = second_block(nc, K, c, X, dram)
            if kept is not None:
                result = kept
        if stop is None:
            with nc.sbuf_tensor(unique("normed"), [P, KT, TOK], F32) as H:
                rms_norm(nc, K, token_tiles(X, SEGS[1:]), token_tiles(H, SEGS[1:]), SEGS[1:], KT, D,
                         lambda k, n: c("final_norm2")[:, k:k + 1])
                store(nc, out, H[:, :, LAT])
        else:
            store(nc, out, result[:])


def store(nc, out, x):
    with stage(nc, "stored") as (block, stored):
        @block.sync
        def _(sp):
            sp.dma_start(out, x).then_inc(stored, 16)
            sp.wait_ge(stored, 16)



def tiled(w):
    k, n = w.shape
    return np.ascontiguousarray(w.reshape(k // P, P, n // P, P).transpose(2, 1, 0, 3)).reshape(n // P, P, -1)


def on_partitions(v):
    v = v.reshape(-1, v.shape[-1])
    return v.T.reshape(-1, P, v.shape[0]).transpose(1, 0, 2).reshape(P, -1)


def padded(v):
    out = np.zeros((P,) + v.shape[1:], np.float32)
    out[:v.shape[0]] = v
    return out


def constants():
    i = np.arange(P)
    l, s = i[:, None], i[None, :]
    swap = np.zeros((P, P), np.float32)
    for m in range(P):
        if m % 32 < 16:
            swap[m + 16, m] = -1.0
        else:
            swap[m - 16, m] = 1.0
    tables = {"ident": l == s, "ones": l >= 0, "ones64": l // 64 == s // 64, "swap": swap,
              "le": l <= s, "ge": l >= s, "gt": l > s, "lt": l < s,
              "mask_f": np.where(l <= s, 0.0, NEG), "mask_b": np.where(l >= s, 0.0, NEG)}
    tables["ones"] = np.ones((P, P))
    consts = np.stack([np.asarray(tables[n], np.float32) for n in CONSTS], axis=1)
    inv = 10000.0 ** (-np.arange(0, 32, 2) / 32.0)
    t = np.arange(SEQ)
    ang = np.concatenate([np.tile(inv[:, None] * (t // 64)[None], (2, 1)),
                          np.tile(inv[:, None] * (t % 64)[None], (2, 1))])
    ang = np.tile(ang.astype(np.float32).astype(np.float64), (2, 1))
    rope = np.stack([np.cos(ang), np.sin(ang)], axis=1).astype(np.float32)
    out = {"consts": consts, "rope": rope}
    zs = []
    for seg, (_, L) in enumerate(SEGS):
        pos = np.arange(L)
        tt = (pos / (L - 1))[:, None]
        f = np.linspace(1e-4, 15, 16)
        ang = (2.0 * np.pi / L) * pos[:, None] * f[None]
        zs.append(np.concatenate([tt, np.cos(ang), -np.sin(ang)], axis=-1).T)
        deltas = np.linspace(np.log(1e-2) / 0.3, np.log(1e-2) / 1.5, 512)
        decay = np.exp(-tt * np.abs(deltas)[None]) + 0.05
        out[f"decay{seg}"] = np.ascontiguousarray(
            decay.reshape(L // P, P, 512).transpose(1, 0, 2)).astype(np.float32)
        w = np.pi * (2 * np.arange(L) + 1) / (2 * L)
        fwd = np.stack([np.cos(np.outer(pos, w)), np.sin(np.outer(pos, w))])
        inv_ = fwd.transpose(0, 2, 1) / L
        for name, m in (("dft", fwd), ("idft", inv_)):
            out[f"{name}{seg}"] = np.ascontiguousarray(
                m.reshape(2, L // P, P, L).transpose(0, 2, 1, 3)).astype(np.float32)
    out["positions"] = np.concatenate(zs, axis=1).astype(np.float32)
    return out


def lay_out(i):
    a = constants()
    vec = {}
    on = on_partitions
    feat = lambda x: np.ascontiguousarray(x.reshape(-1, KT, P).transpose(2, 1, 0))
    a["x"], a["ctx"] = feat(i["x"]), feat(i["ctx_2"])
    heads = [0, 4, 1, 5, 2, 6, 3, 7]
    for n in range(2):
        w = i["w_in"][n]
        q = w[:, :512].reshape(D, 8, 64)[:, heads].reshape(D, 512)
        order = np.concatenate([q, w[:, 512:640], w[:, 640:768], w[:, 768:1280], w[:, 1280:2304]], axis=1)
        a[f"w_in{n}"] = tiled(order)
        a[f"w_dt{n}"] = np.ascontiguousarray(w[:, 2304:].reshape(KT, P, 16).transpose(1, 0, 2)).reshape(P, -1)
        o = i["w_out"][n]
        a[f"w_out{n}"] = tiled(np.concatenate([o[:512].reshape(8, 64, D)[heads].reshape(512, D), o[512:]]))
        a[f"w_up{n}"] = np.concatenate([tiled(i["w_gate"][n]), tiled(i["w_up"][n])], axis=2)
        a[f"w_down{n}"] = tiled(i["w_down"][n])
        for name in ("norm_mix_w", "norm_ffn_w", "conv_w", "conv_b", "ssd_norm_w"):
            vec[f"{name}{n}"] = on(i[name][n])
        for name in ("q_norm_w", "k_norm_w"):
            vec[f"{name}{n}"] = on(np.tile(i[name][n], 2))
        vec[f"dt_bias{n}"] = padded(i["dt_bias"][n].reshape(16, 1))
        vec[f"a_log{n}"] = padded(i["a_log"][n].reshape(16, 1))
        vec[f"d_skip{n}"] = on(np.repeat(i["d_skip"][n], 64))
        up = i[f"ffn_up_{n}_2"]
        a[f"w_up2{n}"] = np.concatenate([tiled(up[:, :FF]), tiled(up[:, FF:])], axis=2)
        a[f"w_down2{n}"] = tiled(i[f"ffn_down_{n}_2"])
        ada = tiled(i[f"ada_w_{n}_2"])
        a[f"ada{n}"] = np.ascontiguousarray(ada.reshape(-1, 4, P, D).transpose(0, 2, 1, 3)).reshape(-1, P, 4 * D)
        vec[f"ada_b{n}"] = on(i[f"ada_b_{n}_2"])
        vec[f"norm_mix2{n}"] = on(i[f"norm_mix_{n}_2"])
        vec[f"norm_ffn2{n}"] = on(i[f"norm_ffn_{n}_2"])
        vec[f"ffn_conv_w{n}"] = on(i[f"ffn_conv_w_{n}_2"])
        vec[f"ffn_conv_b{n}"] = on(i[f"ffn_conv_b_{n}_2"])
    vec["final_norm_w"] = on(i["final_norm_w"])
    vec["final_norm2"] = on(i["final_norm_2"])
    vec["conditions"] = on(np.stack([i["c_2"][0], i["c_ctx_2"]]))
    w = i["w_in_0_2"]
    a["w_in2"] = tiled(np.concatenate([w[:, :1536], w[:, 3072:3584], w[:, 1536:3072]], axis=1))
    g = np.zeros((D, P), np.float32)
    gb = np.zeros((P, 1), np.float32)
    for kind, row in enumerate((0, 64, 32, 96)):
        g[:, row:row + 4] = w[:, 3584 + 4 * kind:3588 + 4 * kind]
        gb[row:row + 4, 0] = i["ml_gate_b_2"][4 * kind:4 * kind + 4]
    a["w_gates"] = tiled(g)
    vec["gate_b"] = gb
    no_bias = np.zeros(1024, np.float32)
    vec["conv2_w"] = np.concatenate([on(i["hy_conv_w_2"]), on(i["ml_conv_w_2"])], axis=1)
    vec["conv2_b"] = np.concatenate([on(i["hy_conv_b_2"]), on(no_bias)], axis=1)
    vec["filter_b"] = padded(np.stack([i["hy_fb1_2"], i["hy_fb2_2"]], axis=1))
    vec["filter_freq"] = padded(i["hy_freq_2"].reshape(64, 1))
    vec["hy_bias"] = on(i["hy_bias_2"])
    vec["ml_norm"] = on(i["ml_norm_g_2"])
    fw1 = np.zeros((64, 64), np.float32)
    fw1[:33] = i["hy_fw1_2"]
    a["filter_w"] = np.concatenate([fw1, i["hy_fw2_2"], i["hy_fw3_2"]], axis=1)
    a["w_out20"] = tiled(i["w_out_0_2"])
    a["w_out21"] = tiled(i["mla_w_o_2"])
    w = i["mla_w_down_2"]
    a["mla_down"] = tiled(np.concatenate([w, w[:, 640:704]], axis=1))
    u = i["mla_w_uq_2"].reshape(384, 8, 192)
    a["mla_uq"] = tiled(np.concatenate([u[:, :, :128].reshape(384, -1), u[:, :, 128:].reshape(384, -1)], axis=1))
    u = i["mla_w_ukv_2"].reshape(256, 8, 256)
    a["mla_uk"] = tiled(np.ascontiguousarray(u[:, :, :128]).reshape(256, -1))
    a["mla_uv"] = np.ascontiguousarray(u[:, :, 128:].reshape(2, P, D).transpose(1, 0, 2))
    vec["mla_q_norm"] = on(i["mla_q_norm_2"])
    vec["mla_kv_norm"] = on(i["mla_kv_norm_2"])
    places, at = {}, 0
    for name, v in vec.items():
        places[name] = (at, v.shape[1])
        at += v.shape[1]
    a["vectors"] = np.concatenate(list(vec.values()), axis=1)
    return {k: np.ascontiguousarray(v) for k, v in a.items()}, places


def kernel(**inputs):
    import concourse.bacc as bacc
    from concourse.bass_utils import run_bass_kernel_spmd

    arrays, places = lay_out({k: np.asarray(v) for k, v in inputs.items()})
    nc = bacc.Bacc("TRN2", target_bir_lowering=False, num_devices=1)
    ins = {name: nc.dram_tensor(f"in_{name}", a.shape, F32, kind="ExternalInput").ap()
           for name, a in arrays.items()}
    out = nc.dram_tensor("out", (P, KT, TOK if STOP else SEQ), F32, kind="ExternalOutput").ap()
    build(nc, ins, places, out, STOP)
    r = run_bass_kernel_spmd(nc, [{f"in_{name}": a for name, a in arrays.items()}], core_ids=[0])
    y = r.results[0]["out"]
    return np.ascontiguousarray(y.transpose(2, 1, 0)).reshape(1, -1, D)


STOP = None
```

```python
from contextlib import ExitStack, contextmanager
from itertools import count

import numpy as np

import concourse.bass as bass
from concourse import mybir

F32 = mybir.dt.float32
F32R = mybir.dt.float32r
ALU = mybir.AluOpType
ACT = mybir.ActivationFunctionType
AX = mybir.AxisListType

P = 128
D = 1024
KT = D // P
CTX, SEQ = 256, 512
TOK = CTX + SEQ
LAT = slice(CTX, TOK)
LT = SEQ // P
FF = 2816
FT = FF // P
HALF = FT // 2
UNIT = HALF * P
EPS = 1e-6
NEG = -1e30
FIRST_SEMAPHORE = 120
SEGS = [(0, CTX), (CTX, SEQ)]
PADDED = 1 + CTX + 1 + SEQ + 1
PSEG = [(1, CTX), (2 + CTX, SEQ)]



NAMES = count()


def unique(name):
    return f"{name}_{next(NAMES)}"


@contextmanager
def stage(nc, *names):
    first = FIRST_SEMAPHORE
    with ExitStack() as ctx:
        sems = [ctx.enter_context(nc.semaphore(n, num=first + k)) for k, n in enumerate(names)]
        with nc.Block() as block:
            yield (block, *sems)
        nc.multi_engine_barrier(mybir.ALL_ENGINES, sems_to_clear=range(first, first + len(names)))


class Chain:

    def __init__(self, eng, sem):
        self.eng, self.sem, self.n = eng, sem, 0

    def step(self, ins):
        self.n += 1
        ins.then_inc(self.sem, 1)
        self.eng.wait_ge(self.sem, self.n)


def later(i):
    return not isinstance(i, int) or i > 0


def in_pairs(eng, tiles, step):
    for j in range(min(2, tiles)):
        step(j, 0, j + 2 < tiles)
    end = max(1, (tiles - 4) // 2 + 1)
    if end > 1:
        with eng.Fori(1, end) as i:
            step(0, i, True)
            step(1, i, True)
    for n in range(2 * end, tiles):
        step(n % 2, n // 2, n + 2 < tiles)


class Weights:

    def __init__(self, nc, ctx, tiles, order):
        self.raw = ctx.enter_context(nc.sbuf_tensor("weights_raw", [P, 2, UNIT], F32))
        self.hi = ctx.enter_context(nc.sbuf_tensor("weights_hi", [P, 2, UNIT], F32R))
        self.lo = ctx.enter_context(nc.sbuf_tensor("weights_lo", [P, 2, UNIT], F32R))
        self.arrived = [ctx.enter_context(nc.semaphore("weights_arrived_even", num=FIRST_SEMAPHORE - 2)),
                        ctx.enter_context(nc.semaphore("weights_arrived_odd", num=FIRST_SEMAPHORE - 1))]
        self.tiles, self.order = tiles, order
        self.base, self.loaded, self.at, self.n, self.first = [0, 0], [0, 0], 0, 0, 0

    def begin(self, key):
        assert self.order[self.at] == key, (self.order[self.at], key)
        self.base = list(self.loaded)
        self.ahead = self.at > 0
        self.first = self.slot(self.n)
        self.w = self.tiles[key]
        self.n, self.cols = self.w.shape[0], self.w.shape[2]
        self.at += 1
        self.loaded[self.slot(0)] += (self.n + 1) // 2
        self.loaded[self.slot(1)] += self.n // 2
        return self.n

    def slot(self, n):
        return (self.first + n) % 2

    def load_first(self, sp, w, n):
        for m in range(2):
            s = self.slot(n + m)
            sp.dma_start(self.raw[:, s, 0:w.shape[2]], w[m]).then_inc(self.arrived[s], 16)

    def load(self, sp, split, beside=None):
        if self.at == 1:
            self.load_first(sp, self.w, 0)

        def tile(j, i, more):
            if later(i):
                sp.wait_ge(split, 2 * i + j - 1)
                s = self.slot(j)
                sp.dma_start(self.raw[:, s, 0:self.cols], self.w[2 * i + j]).then_inc(self.arrived[s], 16)
                if beside:
                    beside(j, i - 1)
        in_pairs(sp, self.n, tile)
        if beside:
            for n in range(max(0, self.n - 2), self.n):
                beside(n % 2, n // 2)
        if self.at < len(self.order):
            sp.wait_ge(split, self.n)
            self.load_first(sp, self.tiles[self.order[self.at]], self.n)

    def high(self, act, j, i, hi_ready, product_ready):
        if not later(i) and j == 0 and self.ahead:
            act.nop().then_inc(hi_ready, 1)
            return
        s = self.slot(j)
        act.wait_ge(self.arrived[s], 16 * (self.base[s] + i + 1))
        if later(i):
            act.wait_ge(product_ready, 2 * i + j - 1)
        act.activation(self.hi[:, s, 0:self.cols], self.raw[:, s, 0:self.cols], ACT.Copy).then_inc(hi_ready, 1)

    def rest(self, dve, j, i, hi_ready, split):
        if not later(i) and j == 0 and self.ahead:
            dve.nop().then_inc(split, 1)
            return
        s = self.slot(j)
        dve.wait_ge(hi_ready, 2 * i + j + 1)
        dve.tensor_tensor(self.lo[:, s, 0:self.cols], self.raw[:, s, 0:self.cols],
                          self.hi[:, s, 0:self.cols].bitcast(F32), ALU.subtract).then_inc(split, 1)

    def next_high(self, act, next_hi, product_ready):
        if self.at < len(self.order):
            cols, s = self.tiles[self.order[self.at]].shape[2], self.slot(self.n)
            act.wait_ge(self.arrived[s], 16 * (self.loaded[s] + 1))
            act.wait_ge(product_ready, self.n - 1)
            act.activation(self.hi[:, s, 0:cols], self.raw[:, s, 0:cols], ACT.Copy).then_inc(next_hi, 1)

    def next_rest(self, dve, next_hi):
        if self.at < len(self.order):
            cols, s = self.tiles[self.order[self.at]].shape[2], self.slot(self.n)
            dve.wait_ge(next_hi, 1)
            dve.tensor_tensor(self.lo[:, s, 0:cols], self.raw[:, s, 0:cols],
                              self.hi[:, s, 0:cols].bitcast(F32), ALU.subtract)

    def last(self, j, i, more):
        return not more and 2 * i + j == self.n - 1

    def products(self, pe, j, outs, rhs):
        kt, s = self.cols // P, self.slot(j)
        for k in range(kt):
            m = slice(k * P, (k + 1) * P)
            for out, (xh, xl) in zip(outs, rhs(k)):
                pe.matmul(out, self.hi[:, s, m], xh, start=k == 0, stop=False)
                pe.matmul(out, self.hi[:, s, m], xl, start=False, stop=False)
            for out, (xh, xl) in zip(outs, rhs(k)):
                mm = pe.matmul(out, self.lo[:, s, m], xh, start=False, stop=k == kt - 1)
        return mm


class Modulation:

    def __init__(self, nc, ctx, weights, raw):
        self.w, self.out, self.at = weights, raw, 0
        self.tile = ctx.enter_context(nc.sbuf_tensor("ada_tiles", [P, 2, D], F32))
        self.cond = ctx.enter_context(nc.sbuf_tensor("conditions", [P, 2, D], F32))
        self.prod = ctx.enter_context(nc.sbuf_tensor("ada_products", [P, D], F32))
        self.sums = ctx.enter_context(nc.sbuf_tensor("ada_sums", [P, 2, 2], F32))

    def load(self, sp, j, i, arrived, slots_free):
        sp.wait_ge(slots_free, 2 * i + j + 1)
        sp.dma_start(self.tile[:, j], self.w[self.at + 2 * i + j]).then_inc(arrived[j], 16)

    def free_slots(self, dve, slots_free):
        for _ in range(2):
            dve.nop().then_inc(slots_free, 1)

    def compute(self, dve, j, i, arrived, summed, slots_free):
        dve.wait_ge(arrived[j], 16 * (i + 1))
        for v in range(2):
            dve.tensor_tensor_reduce(out=self.tile[:, j] if v else self.prod[:], in0=self.tile[:, j], in1=self.cond[:, v], scale=1.0,
                                     scalar=0.0, op0=ALU.mult, op1=ALU.add,
                                     accum_out=self.sums[:, j, v:v + 1]).then_inc(summed, 1)
        dve.wait_ge(summed, 4 * i + 2 * j + 2)
        dve.tensor_copy(self.out[:, self.at + 2 * i + j], self.sums[:, j]).then_inc(slots_free, 1)


def operand(pair, segs, k0=0):
    return lambda k: [tuple(b[:, k0 + k, a:a + w] for b in pair) for a, w in segs]


@contextmanager
def split_pair(nc, name, tiles, tokens=TOK):
    with nc.sbuf_tensor(unique(name + "_hi"), [P, tiles, tokens], F32R) as hi, \
            nc.sbuf_tensor(unique(name + "_lo"), [P, tiles, tokens], F32R) as lo:
        yield hi, lo



class Rms:

    def __init__(self, nc, ctx, K, segs, size):
        self.K, self.segs, self.size = K, segs, size
        self.cols = ctx.enter_context(nc.sbuf_tensor(unique("rstd_cols"), [P, 8], F32))
        self.sums = ctx.enter_context(nc.psum_tensor(unique("sum_cols"), [P, 512], F32))
        self.spread = ctx.enter_context(nc.psum_tensor(unique("rstd_ps"), [P, 2, 512], F32))
        self.n = sum(w for _, w in segs) // P

    def column_sums(self, pe, squares):
        for t in range(self.n):
            mm = pe.matmul(self.sums[:, t:t + 1], squares[:, t * P:(t + 1) * P], self.K["ones"][:, 0:1],
                           start=True, stop=True)
        return mm

    def root(self, act):
        return act.activation(self.cols[:, 0:self.n], self.sums[:, 0:self.n], ACT.Sqrt, scale=1.0 / self.size,
                              bias=self.K["eps"])

    def invert(self, dve):
        return dve.reciprocal(self.cols[:, 0:self.n], self.cols[:, 0:self.n])

    def bring_back(self, pe):
        t = 0
        for n, (_, w) in enumerate(self.segs):
            for m in range(w // P):
                mm = pe.matmul(self.spread[:, n, m * P:(m + 1) * P], self.cols[:, t:t + 1].broadcast_to([P, P]),
                               self.K["ident"], start=True, stop=True)
                t += 1
        return mm

    def at(self, n):
        return self.spread[:, n, 0:self.segs[n][1]]


def rms_norm(nc, K, x, segs, tiles, size, gain, sums, out=None):
    with ExitStack() as ctx:
        rms = Rms(nc, ctx, K, segs, size)
        with stage(nc, "sums_ready", "root_ready", "rstd_ready", "spread", "normed", "stored") as (
                block, sums_ready, root_ready, rstd_ready, spread, normed, stored):
            if out is not None:
                @block.sync
                def _(sp):
                    for k in range(tiles):
                        sp.wait_ge(normed, k + 1)
                        sp.dma_start(out[:, k], x(k)).then_inc(stored, 16)
                    sp.wait_ge(stored, 16 * tiles)

            @block.scalar
            def _(act):
                act.wait_ge(sums_ready, 1)
                rms.root(act).then_inc(root_ready, 1)

            @block.tensor
            def _(pe):
                rms.column_sums(pe, sums).then_inc(sums_ready, 1)
                pe.wait_ge(rstd_ready, 1)
                rms.bring_back(pe).then_inc(spread, 1)

            @block.vector
            def _(dve):
                dve.wait_ge(root_ready, 1)
                rms.invert(dve).then_inc(rstd_ready, 1)
                dve.wait_ge(spread, 1)
                for k in range(tiles):
                    for n in range(len(segs)):
                        last = dve.scalar_tensor_tensor(x(k, n), x(k, n), gain(k, n), rms.at(n),
                                                        ALU.mult, ALU.mult)
                    last.then_inc(normed, 1)


def norm_split(nc, K, src, pair, k0, segs, tiles, size, gain, shift=None, keep=None, sums=None):
    hi, lo = pair
    a0, total = segs[0][0], sum(w for _, w in segs)
    span = slice(a0, a0 + total)
    with ExitStack() as ctx:
        rms = Rms(nc, ctx, K, segs, size)
        h = ctx.enter_context(nc.sbuf_tensor(unique("tile"), [P, 3, TOK], F32))
        with stage(nc, "squares_ready", "added", "sums_ready", "root_ready", "rstd_ready", "spread", "tile_ready",
                   "hi_ready", "even_split", "odd_split", "kept") as (
                block, squares_ready, added, sums_ready, root_ready, rstd_ready, spread, tile_ready,
                hi_ready, even_split, odd_split, kept):
            if keep is not None:
                @block.sync
                def _(sp):
                    sp.dma_start(*keep).then_inc(kept, 16)
                    sp.wait_ge(kept, 16)

            pooled = shift is None
            slot = lambda k: 2 - k % 2 if k else 0

            @block.scalar
            def _(act):
                for k in range(tiles if sums is None else 0):
                    if k >= 3:
                        act.wait_ge(added, k - 2)
                    act.activation(h[:, slot(k), span], src(k), ACT.Square).then_inc(squares_ready, 1)
                act.wait_ge(sums_ready, 1)
                rms.root(act).then_inc(root_ready, 1)
                for k in range(tiles):
                    act.wait_ge(tile_ready, k + 1)
                    if shift is None:
                        act.activation(hi[:, k0 + k, span], h[:, k % 3, span], ACT.Copy).then_inc(hi_ready, 1)
                    else:
                        for n, (a, w) in enumerate(segs):
                            last = act.activation(hi[:, k0 + k, a:a + w], h[:, k % 3, a:a + w], ACT.Identity,
                                                  bias=shift(k, n))
                        last.then_inc(hi_ready, 1)

            @block.tensor
            def _(pe):
                if sums is None:
                    pe.wait_ge(added, tiles - 1)
                rms.column_sums(pe, h[:, 0, span] if sums is None else sums[:, span]).then_inc(sums_ready, 1)
                pe.wait_ge(rstd_ready, 1)
                rms.bring_back(pe).then_inc(spread, 1)

            def rest(eng, k, done):
                eng.wait_ge(hi_ready, k + 1)
                if shift is None:
                    eng.tensor_tensor(lo[:, k0 + k, span], h[:, k % 3, span], hi[:, k0 + k, span].bitcast(F32),
                                      ALU.subtract).then_inc(done, 1)
                else:
                    for n, (a, w) in enumerate(segs):
                        last = eng.scalar_tensor_tensor(lo[:, k0 + k, a:a + w], h[:, k % 3, a:a + w], shift(k, n),
                                                        hi[:, k0 + k, a:a + w].bitcast(F32), ALU.add, ALU.subtract)
                    last.then_inc(done, 1)

            @block.vector
            def _(dve):
                for k in range(1, tiles if sums is None else 0):
                    dve.wait_ge(squares_ready, k + 1)
                    dve.tensor_tensor(h[:, 0, span], h[:, 0, span], h[:, slot(k), span], ALU.add).then_inc(added, 1)
                    dve.wait_ge(added, k)
                dve.wait_ge(root_ready, 1)
                rms.invert(dve).then_inc(rstd_ready, 1)
                dve.wait_ge(spread, 1)
                for k in range(tiles):
                    if k >= 3:
                        odd = pooled and (k - 3) % 2 == 1
                        dve.wait_ge(odd_split if odd else even_split, (k - 3) // 2 + 1 if pooled else k - 2)
                    for n in range(len(segs)):
                        a, w = segs[n]
                        last = dve.scalar_tensor_tensor(h[:, k % 3, a:a + w], src(k, n), gain(k, n), rms.at(n),
                                                        ALU.mult, ALU.mult)
                    last.then_inc(tile_ready, 1)
                    if k and (not pooled or k % 2):
                        rest(dve, k - 1, even_split)
                if not pooled or tiles % 2:
                    rest(dve, tiles - 1, even_split)

            if pooled:
                @block.gpsimd
                def _(pool):
                    for k in range(1, tiles, 2):
                        rest(pool, k, odd_split)


def split_tiles(nc, pairs):
    with stage(nc, "hi_ready", "even_split", "odd_split") as (block, hi_ready, even_split, odd_split):
        @block.scalar
        def _(act):
            for x, hi, lo in pairs:
                act.activation(hi, x, ACT.Copy).then_inc(hi_ready, 1)

        @block.vector
        def _(dve):
            for n, (x, hi, lo) in list(enumerate(pairs))[::2]:
                dve.wait_ge(hi_ready, n + 1)
                dve.tensor_tensor(lo, x, hi.bitcast(F32), ALU.subtract)

        @block.gpsimd
        def _(pool):
            for n, (x, hi, lo) in list(enumerate(pairs))[1::2]:
                pool.wait_ge(hi_ready, n + 1)
                pool.tensor_tensor(lo, x, hi.bitcast(F32), ALU.subtract)


def token_tiles(buf, segs):
    a0, total = segs[0][0], sum(w for _, w in segs)

    def at(k, n=None):
        if n is None:
            return buf[:, k, a0:a0 + total]
        return buf[:, k, segs[n][0]:segs[n][0] + segs[n][1]]
    return at


def project_residual(nc, R, key, rhs, x, segs, gate=None, M=None, kept=None,
                     sums=None):
    a0, total = segs[0][0], sum(w for _, w in segs)
    with ExitStack() as ctx:
        ps = ctx.enter_context(nc.psum_tensor(unique("sum"), [P, 2, 2, 512], F32))
        tiles = R.begin(key)
        sq = ctx.enter_context(nc.sbuf_tensor(unique("squares"), [P, 2, TOK], F32)) if sums is not None else None
        span = slice(a0, a0 + total)
        with stage(nc, "next_hi", "hi_ready", "split", "product_ready", "added",
                   "x_back", "squares_ready", "summed", "ada_even", "ada_odd", "ada_summed", "ada_free") as (
                block, next_hi, hi_ready, split, product_ready, added, x_back, squares_ready, summed, ada_even, ada_odd, ada_summed, ada_free):
            ada = (ada_even, ada_odd)

            @block.sync
            def _(sp):
                if kept is not None:
                    sp.dma_start(x[:, :, a0:a0 + total], kept[:, :, a0:a0 + total]).then_inc(x_back, 16)
                R.load(sp, split, M and (lambda j, i: M.load(sp, j, i, ada, ada_free)))

            @block.tensor
            def _(pe):
                def tile(j, i, more):
                    pe.wait_ge(split, 2 * i + j + 1)
                    if later(i):
                        pe.wait_ge(added, 2 * i + j - 1)
                    R.products(pe, j, [ps[:, j, n, 0:w] for n, (_, w) in enumerate(segs)],
                               rhs).then_inc(product_ready, 1)
                in_pairs(pe, tiles, tile)

            @block.scalar
            def _(act):
                def square(j, i):
                    act.wait_ge(added, 2 * i + j + 1)
                    act.wait_ge(summed, 2 * i + j + 1)
                    act.activation(sq[:, j, span], x[:, 2 * i + j, span], ACT.Square).then_inc(squares_ready, 1)

                def tile(j, i, more):
                    R.high(act, j, i, hi_ready, product_ready)
                    if later(i) and sums is not None:
                        square(j, i - 1)
                in_pairs(act, tiles, tile)
                R.next_high(act, next_hi, product_ready)
                if sums is not None:
                    for n in range(tiles - 2, tiles):
                        square(n % 2, n // 2)

            @block.vector
            def _(dve):
                def add_square(j, i):
                    dve.wait_ge(squares_ready, 2 * i + j + 1)
                    dve.wait_ge(summed, 2 * i + j + 2)
                    dve.tensor_tensor(sums[:, span], sums[:, span], sq[:, j, span], ALU.add).then_inc(summed, 1)

                def tile(j, i, more):
                    if R.last(j, i, more):
                        R.next_rest(dve, next_hi)
                    if later(i) and sums is not None:
                        add_square(j, i - 1)
                    dve.wait_ge(product_ready, 2 * i + j + 1)
                    if more:
                        R.rest(dve, j, i + 1, hi_ready, split)
                    for n, (a, w) in enumerate(segs):
                        t = x[:, 2 * i + j, a:a + w]
                        if gate is None:
                            last = dve.tensor_tensor(t, ps[:, j, n, 0:w], t, ALU.add)
                        else:
                            last = dve.scalar_tensor_tensor(t, ps[:, j, n, 0:w], gate(2 * i + j, n), t,
                                                            ALU.mult, ALU.add)
                    last.then_inc(added, 1)
                    if M:
                        M.compute(dve, j, i, ada, ada_summed, ada_free)
                if M:
                    M.free_slots(dve, ada_free)
                for j in range(2):
                    R.rest(dve, j, 0, hi_ready, split)
                if kept is not None:
                    dve.wait_ge(x_back, 16)
                if sums is not None:
                    dve.memset(sums[:, span], 0.0).then_inc(summed, 1)
                    dve.wait_ge(summed, 1)
                    dve.nop().then_inc(summed, 1)
                in_pairs(dve, tiles, tile)
                if sums is not None:
                    for n in range(tiles - 2, tiles):
                        add_square(n % 2, n // 2)
        if M:
            M.at += tiles


def project_plain(nc, R, key, rhs, out, segs, func=ACT.Copy, after=None):
    with ExitStack() as ctx:
        ps = ctx.enter_context(nc.psum_tensor(unique("product"), [P, 2, 2, 512], F32))
        tiles = R.begin(key)
        with stage(nc, "next_hi", "hi_ready", "split", "product_ready", "stored") as (
                block, next_hi, hi_ready, split, product_ready, stored):
            @block.sync
            def _(sp):
                R.load(sp, split)

            @block.tensor
            def _(pe):
                def tile(j, i, more):
                    pe.wait_ge(split, 2 * i + j + 1)
                    if later(i):
                        pe.wait_ge(stored, 2 * i + j - 1)
                    R.products(pe, j, [ps[:, j, n, 0:w] for n, (_, w) in enumerate(segs)],
                               rhs).then_inc(product_ready, 1)
                in_pairs(pe, tiles, tile)

            @block.scalar
            def _(act):
                def tile(j, i, more):
                    if R.last(j, i, more):
                        R.next_high(act, next_hi, product_ready)
                    act.wait_ge(product_ready, 2 * i + j + 1)
                    if more:
                        R.high(act, j, i + 1, hi_ready, product_ready)
                    for n, (a, w) in enumerate(segs):
                        last = act.activation(out[:, 2 * i + j, a:a + w], ps[:, j, n, 0:w], func)
                    last.then_inc(stored, 1)
                for j in range(2):
                    R.high(act, j, 0, hi_ready, product_ready)
                in_pairs(act, tiles, tile)
                if after:
                    act.wait_ge(stored, tiles)
                    after(act)

            @block.vector
            def _(dve):
                in_pairs(dve, tiles, lambda j, i, more: R.rest(dve, j, i, hi_ready, split))
                R.next_rest(dve, next_hi)


def project_conv(nc, R, key, rhs, out, segs, pseg, length, taps, bias, func):
    width = taps.shape[2]
    half = width // 2
    lo_, hi_ = pseg[0][0], pseg[-1][0] + pseg[-1][1]
    span = hi_ - lo_
    with ExitStack() as ctx:
        raw = ctx.enter_context(nc.sbuf_tensor(unique("conv_raw"), [P, 2, length], F32))
        acc = ctx.enter_context(nc.sbuf_tensor(unique("conv_acc"), [P, 2, length], F32))
        ps = ctx.enter_context(nc.psum_tensor(unique("product"), [P, 2, 2, 512], F32))
        tiles = R.begin(key)
        with stage(nc, "next_hi", "hi_ready", "split", "product_ready", "raw_ready", "conv_step", "conv_ready",
                   "stored", "pads_zero") as (
                block, next_hi, hi_ready, split, product_ready, raw_ready, conv_step, conv_ready, stored, pads_zero):
            @block.sync
            def _(sp):
                R.load(sp, split)

            @block.tensor
            def _(pe):
                def tile(j, i, more):
                    pe.wait_ge(split, 2 * i + j + 1)
                    if later(i):
                        pe.wait_ge(raw_ready, 2 * i + j - 1)
                    R.products(pe, j, [ps[:, j, n, 0:w] for n, (_, w) in enumerate(segs)],
                               rhs).then_inc(product_ready, 1)
                in_pairs(pe, tiles, tile)

            @block.scalar
            def _(act):
                for j in range(2):
                    R.high(act, j, 0, hi_ready, product_ready)
                act.wait_ge(pads_zero, 1)

                def tile(j, i, more):
                    if R.last(j, i, more):
                        R.next_high(act, next_hi, product_ready)
                    act.wait_ge(product_ready, 2 * i + j + 1)
                    if later(i):
                        act.wait_ge(conv_ready, 2 * i + j - 1)
                    for n, (p0, w) in enumerate(pseg):
                        last = act.activation(raw[:, j, p0:p0 + w], ps[:, j, n, 0:w], ACT.Copy)
                    last.then_inc(raw_ready, 1)
                    if more:
                        R.high(act, j, i + 1, hi_ready, product_ready)
                    act.wait_ge(conv_ready, 2 * i + j + 1)
                    for n, (p0, w) in enumerate(pseg):
                        a = segs[n][0] if len(segs) > 1 else 0
                        last = act.activation(out[:, 2 * i + j, a:a + w], acc[:, j, p0:p0 + w], func)
                    last.then_inc(stored, 1)
                in_pairs(act, tiles, tile)

            @block.vector
            def _(dve):
                dve.memset(raw[:], 0.0).then_inc(pads_zero, 1)
                for j in range(2):
                    R.rest(dve, j, 0, hi_ready, split)

                def tile(j, i, more):
                    n = 2 * i + j
                    if R.last(j, i, more):
                        R.next_rest(dve, next_hi)
                    dve.wait_ge(raw_ready, n + 1)
                    if later(i):
                        dve.wait_ge(stored, n - 1)
                    o = acc[:, j, lo_:hi_]
                    dve.tensor_scalar(o, raw[:, j, lo_ - half:lo_ - half + span], taps[:, n, 0:1], bias[:, n, 0:1],
                                      ALU.mult, ALU.add).then_inc(conv_step, 1)
                    for t in range(1, width):
                        dve.wait_ge(conv_step, (width - 1) * n + t)
                        dve.scalar_tensor_tensor(o, raw[:, j, lo_ - half + t:lo_ - half + t + span],
                                                 taps[:, n, t:t + 1], o, ALU.mult, ALU.add
                                                 ).then_inc(conv_step if t < width - 1 else conv_ready, 1)
                    if more:
                        R.rest(dve, j, i + 1, hi_ready, split)
                in_pairs(dve, tiles, tile)



Q_T, K_T, V_T, Z_T, DT_T = 0, 4, 5, 6, 10
PAD5 = SEQ + 4


def mix_projection(nc, K, R, c, layer, rhs, proj, conv, dt_rows):
    def after(act):
        act.activation(dt_rows, proj[0:16, DT_T], ACT.Identity, bias=c("dt_bias", layer)[0:16])
        act.activation(proj[:, Z_T:Z_T + 4], proj[:, Z_T:Z_T + 4], ACT.Silu)
    project_plain(nc, R, f"in{layer}a", rhs, proj, [(0, SEQ)], after=after)
    project_conv(nc, R, f"in{layer}b", rhs, conv, [(0, SEQ)], [(2, SEQ)], PAD5,
                 c("conv_w", layer).rearrange("p (n w) -> p n w", w=5),
                 c("conv_b", layer).rearrange("p (n w) -> p n w", w=1), ACT.Silu)


def head_norm_rope(nc, K, tiles):
    N = len(tiles)
    with_norm = tiles[0][1] is not None
    with ExitStack() as ctx:
        t2 = ctx.enter_context(nc.sbuf_tensor(unique("turned"), [P, 2, SEQ], F32))
        pr = ctx.enter_context(nc.psum_tensor(unique("rope_ps"), [P, 2, 512], F32))
        if with_norm:
            sq = ctx.enter_context(nc.sbuf_tensor(unique("squares"), [P, 2, SEQ], F32))
            rc = ctx.enter_context(nc.sbuf_tensor(unique("rstd_cols"), [P, N * LT, 2], F32))
            pn = ctx.enter_context(nc.psum_tensor(unique("norm_ps"), [P, 256, 2], F32))
            pb = ctx.enter_context(nc.psum_tensor(unique("rstd_ps"), [P, 2, 512], F32))
        with stage(nc, "squares_ready", "sums_ready", "root_ready", "inverted", "spread", "normed", "swapped", "dve_step",
                   "done") as (
                block, squares_ready, sums_ready, root_ready, inverted, spread, normed, swapped, dve_step, done):
            @block.scalar
            def _(act):
                if with_norm:
                    for n, (x, _) in enumerate(tiles):
                        if n >= 2:
                            act.wait_ge(sums_ready, n - 1)
                        act.activation(sq[:, n % 2], x, ACT.Square).then_inc(squares_ready, 1)
                    act.wait_ge(sums_ready, N)
                    act.activation(rc[:], pn[:, 0:N * LT], ACT.Sqrt, scale=1.0 / 64, bias=K["eps"]).then_inc(root_ready, 1)

            @block.tensor
            def _(pe):
                def swap(n):
                    if with_norm:
                        pe.wait_ge(normed, n + 1)
                    if n >= 2:
                        pe.wait_ge(done, n - 1)
                    pe.matmul(pr[:, n % 2], K["swap"], tiles[n][0], start=True, stop=True).then_inc(swapped, 1)

                def bring_back(n):
                    if n >= 2:
                        pe.wait_ge(normed, n - 1)
                    for t in range(LT):
                        for m in range(2):
                            mm = pe.matmul(pb[64 * m:64 * m + 64, n % 2, t * P:(t + 1) * P],
                                           rc[:, n * LT + t, m:m + 1].broadcast_to([P, 64]), K["ident"],
                                           start=True, stop=True)
                    mm.then_inc(spread, 1)
                if with_norm:
                    heads = K["ones64"].rearrange("p (h c) -> p h c", h=2)[:, :, 0]
                    for n in range(N):
                        pe.wait_ge(squares_ready, n + 1)
                        for t in range(LT):
                            mm = pe.matmul(pn[:, n * LT + t], sq[:, n % 2, t * P:(t + 1) * P], heads,
                                           start=True, stop=True)
                        mm.then_inc(sums_ready, 1)
                    pe.wait_ge(inverted, 1)
                    bring_back(0)
                for n in range(N):
                    if with_norm and n + 1 < N:
                        bring_back(n + 1)
                    swap(n)

            @block.vector
            def _(dve):
                chain = Chain(dve, dve_step)

                def norm(n):
                    x, g = tiles[n]
                    dve.wait_ge(spread, n + 1)
                    dve.scalar_tensor_tensor(x, x, g, pb[:, n % 2], ALU.mult, ALU.mult).then_inc(normed, 1)
                    dve.wait_ge(normed, n + 1)

                def rotate(n):
                    x = tiles[n][0]
                    dve.wait_ge(swapped, n + 1)
                    dve.tensor_tensor(t2[:, n % 2], pr[:, n % 2], K["rope_sin"], ALU.mult)
                    chain.step(dve.tensor_tensor(x, x, K["rope_cos"], ALU.mult))
                    dve.tensor_tensor(x, x, t2[:, n % 2], ALU.add).then_inc(done, 1)
                if with_norm:
                    dve.wait_ge(root_ready, 1)
                    dve.reciprocal(rc[:], rc[:]).then_inc(inverted, 1)
                    norm(0)
                for n in range(N):
                    if with_norm and n + 1 < N:
                        norm(n + 1)
                    rotate(n)
                dve.wait_ge(done, N)


def attention(nc, K, heads, keys, scale, score_parts, values, vrows, out):
    kt = keys // P
    cuts = [(0, 512)] if keys == 512 else [(0, 384), (384, 384)]
    nb = len(cuts)
    with ExitStack() as ctx:
        pr = ctx.enter_context(nc.sbuf_tensor(unique("probs"), [P, 2, keys], F32))
        pt = ctx.enter_context(nc.sbuf_tensor(unique("probs_t"), [P, 2, kt, SEQ], F32))
        sm = ctx.enter_context(nc.sbuf_tensor(unique("rows"), [P, 2, 4], F32))
        ps = ctx.enter_context(nc.psum_tensor(unique("scores"), [P, 2, nb, 512], F32))
        pT = ctx.enter_context(nc.psum_tensor(unique("turned"), [P, nb, 4, P], F32))
        po = ctx.enter_context(nc.psum_tensor(unique("mixed"), [P, 2, 512], F32))
        NQ = 4 * heads
        with stage(nc, "scores_ready", "max_ready", "exp_done", "probs_ready", "turned", "turned_copied",
                   "mixed_ready", "mixed_hi", "mixed_copied", "dve_step") as (
                block, scores_ready, max_ready, exp_done, probs_ready, turned, turned_copied,
                mixed_ready, mixed_hi, mixed_copied, dve_step):

            @block.tensor
            def _(pe):
                def scores(n):
                    if n >= 2:
                        pe.wait_ge(exp_done, n - 1)
                    for b, (a, w) in enumerate(cuts):
                        parts = score_parts(n // 4, (n % 4) * P)
                        for m, (q, k) in enumerate(parts):
                            mm = pe.matmul(ps[:, n % 2, b, 0:w], q, k(a, w), start=m == 0,
                                           stop=m == len(parts) - 1)
                    mm.then_inc(scores_ready, 1)

                def turn(n):
                    pe.wait_ge(probs_ready, n + 1)
                    if n:
                        pe.wait_ge(turned_copied, n)
                    for t in range(kt):
                        mm = pe.transpose(pT[:, t // 4, t % 4], pr[:, n % 2, t * P:(t + 1) * P], K["ident"])
                    mm.then_inc(turned, 1)

                def mix(h):
                    pe.wait_ge(turned_copied, 4 * h + 4)
                    if h >= 2:
                        pe.wait_ge(mixed_copied, h - 1)
                    row = 64 * (h % 2) if vrows == 64 else 0
                    for t in range(kt):
                        mm = pe.matmul(po[row:row + vrows, h % 2], values(h, t), pt[:, h % 2, t],
                                       start=t == 0, stop=t == kt - 1)
                    mm.then_inc(mixed_ready, 1)
                scores(0)
                for n in range(NQ):
                    if n + 1 < NQ:
                        scores(n + 1)
                    turn(n)
                    if n % 4 == 0 and n:
                        mix(n // 4 - 1)
                mix(heads - 1)

            def evac(dve, h):
                row = 64 * (h % 2) if vrows == 64 else 0
                dve.wait_ge(mixed_hi, h + 1)
                hi, lo = out(h)
                dve.tensor_tensor(lo, po[row:row + vrows, h % 2], hi.bitcast(F32),
                                  ALU.subtract).then_inc(mixed_copied, 1)

            @block.vector
            def _(dve):
                chain = Chain(dve, dve_step)
                for n in range(NQ):
                    dve.wait_ge(scores_ready, n + 1)
                    if n >= 2:
                        dve.wait_ge(exp_done, n - 1)
                    s = sm[:, n % 2]
                    src = ps[:, n % 2, 0, 0:512] if nb == 1 else ps[:, n % 2, :, 0:384]
                    chain.step(dve.tensor_reduce(s[:, 0:1], src, AX.X if nb == 1 else AX.XY, ALU.max))
                    dve.tensor_scalar(s[:, 1:2], s[:, 0:1], -scale, None, ALU.mult).then_inc(max_ready, 1)
                    dve.wait_ge(exp_done, n + 1)
                    chain.step(dve.reciprocal(s[:, 3:4], s[:, 2:3]))
                    dve.tensor_scalar(pr[:, n % 2], pr[:, n % 2], s[:, 3:4], None,
                                      ALU.mult).then_inc(probs_ready, 1)
                    if n % 4 == 1 and n > 4:
                        evac(dve, n // 4 - 1)
                evac(dve, heads - 1)

            @block.scalar
            def _(act):
                def copy(n):
                    act.wait_ge(turned, n + 1)
                    h = n // 4
                    if h >= 2:
                        act.wait_ge(mixed_ready, h - 1)
                    q0 = (n % 4) * P
                    for b in range(nb):
                        c0, c1 = 4 * b, min(4 * b + 4, kt)
                        last = act.activation(pt[:, h % 2, c0:c1, q0:q0 + P], pT[:, b, 0:c1 - c0], ACT.Copy)
                    last.then_inc(turned_copied, 1)

                def high(h):
                    row = 64 * (h % 2) if vrows == 64 else 0
                    act.wait_ge(mixed_ready, h + 1)
                    act.activation(out(h)[0], po[row:row + vrows, h % 2], ACT.Copy).then_inc(mixed_hi, 1)
                for n in range(NQ):
                    act.wait_ge(max_ready, n + 1)
                    if n >= 2:
                        act.wait_ge(turned, n - 1)
                    src = ps[:, n % 2, 0, 0:512] if nb == 1 else ps[:, n % 2, :, 0:384]
                    dst = pr[:, n % 2] if nb == 1 else pr[:, n % 2].rearrange("p (b w) -> p b w", b=nb)
                    act.activation(dst, src, ACT.Exp, bias=sm[:, n % 2, 1:2], scale=scale,
                                   accum_out=sm[:, n % 2, 2:3]).then_inc(exp_done, 1)
                    if n:
                        copy(n - 1)
                    if n % 4 == 1 and n > 4:
                        high(n // 4 - 1)
                copy(NQ - 1)
                high(heads - 1)


def turn_tiles(nc, K, pairs):
    with ExitStack() as ctx:
        ps = ctx.enter_context(nc.psum_tensor(unique("turn_ps"), [P, 2, 4, P], F32))
        with stage(nc, "turned", "copied") as (block, turned, copied):
            @block.tensor
            def _(pe):
                for n, (ins, _) in enumerate(pairs):
                    if n >= 2:
                        pe.wait_ge(copied, n - 1)
                    for m, x in enumerate(ins):
                        mm = pe.transpose(ps[:, n % 2, m], x, K["ident"])
                    mm.then_inc(turned, 1)

            @block.vector
            def _(dve):
                for n, (ins, out) in enumerate(pairs):
                    dve.wait_ge(turned, n + 1)
                    dve.tensor_copy(out, ps[:, n % 2, 0:len(ins)]).then_inc(copied, 1)


def ssd(nc, K, c, layer, proj, conv, dt_rows, mixed):
    with ExitStack() as ctx:
        def sb(name, shape):
            return ctx.enter_context(nc.sbuf_tensor(unique(name), shape, F32))

        rows = sb("dt_rows", [64, SEQ])
        tmp = sb("softplus", [48, SEQ])
        acol = sb("a_log", [P, 2])
        cols = sb("dt_cols", [P, LT, 2, 16])
        csl = sb("minus_local_sums", [P, LT, 16])
        gap = sb("between", [P, 2, LT, LT, 8])
        xt = sb("x_tokens", [P, LT, 4 * P])
        sc = sb("scores", [P, 2, LT, SEQ])
        PAIRS = [(0, j, i) for j in range(LT) for i in range(j + 1, LT)] + \
                [(1, j, i) for j in range(LT) for i in range(j)]
        with ExitStack() as c2:
            pt = c2.enter_context(nc.psum_tensor(unique("turn_ps"), [P, 2, 4, P], F32))
            pc = c2.enter_context(nc.psum_tensor(unique("col_ps"), [P, 4, P], F32))
            pb = c2.enter_context(nc.psum_tensor(unique("sum_ps"), [P, 512], F32))
            psc = c2.enter_context(nc.psum_tensor(unique("score_ps"), [P, 2, 512], F32))
            with stage(nc, "act_step", "dve_step", "abs_ready", "log_ready", "rows_ready", "cols_turned", "cols_copied",
                       "sums_ready", "sums_copied", "turned", "x_copied", "scores_ready", "scores_copied") as (
                    block, act_step, dve_step, abs_ready, log_ready, rows_ready, cols_turned, cols_copied,
                    sums_ready, sums_copied, turned, x_copied, scores_ready, scores_copied):
                @block.vector
                def _(dve):
                    chain = Chain(dve, dve_step)
                    chain.step(dve.memset(rows[:], 0.0))
                    chain.step(dve.scalar_tensor_tensor(tmp[0:16], dt_rows, -1.0, dt_rows, ALU.mult, ALU.max))
                    dve.nop().then_inc(abs_ready, 1)
                    for n in range(LT):
                        dve.wait_ge(turned, n + 1)
                        dve.tensor_copy(xt[:, n].rearrange("p (m c) -> p m c", m=4),
                                        pt[:, n % 2]).then_inc(x_copied, 1)
                    dve.wait_ge(log_ready, 2)
                    chain.step(dve.scalar_tensor_tensor(rows[0:16], dt_rows, 0.0, tmp[0:16], ALU.max, ALU.add))
                    chain.step(dve.tensor_scalar(rows[32:48], rows[0:16], acol[0:16, 0:1], -1.0,
                                                 ALU.mult, ALU.mult))
                    dve.nop().then_inc(rows_ready, 1)
                    dve.wait_ge(cols_turned, 1)
                    chain.step(dve.tensor_copy(cols[:, :, 0], pc[:, 0:LT, 0:16]))
                    dve.tensor_copy(cols[:, :, 1], pc[:, 0:LT, 32:48]).then_inc(cols_copied, 1)
                    dve.wait_ge(sums_copied, 1)
                    for n, (d, j, i) in enumerate(PAIRS):
                        dve.tensor_tensor(gap[:, d, j, i], gap[:, d, j, i], cols[:, j, 0, 8 * d:8 * d + 8],
                                          ALU.mult)

                @block.scalar
                def _(act):
                    chain = Chain(act, act_step)
                    act.activation(acol[0:16, 0:1], c("a_log", layer)[0:16], ACT.Exp).then_inc(log_ready, 1)
                    act.wait_ge(abs_ready, 1)
                    chain.step(act.activation(tmp[0:16], tmp[0:16], ACT.Exp, scale=-1.0))
                    act.activation(tmp[0:16], tmp[0:16], ACT.Ln, bias=1.0).then_inc(log_ready, 1)
                    for n in range(2 * LT):
                        act.wait_ge(scores_ready, n + 1)
                        act.activation(sc[:, n // LT, n % LT], psc[:, n % 2], ACT.Copy).then_inc(scores_copied, 1)
                    act.wait_ge(sums_ready, 1)
                    act.activation(csl[:].rearrange("p a b -> p (a b)"), pb[:, 0:64], ACT.Copy, scale=-1.0)
                    for n, (d, j, i) in enumerate(PAIRS):
                        last = act.activation(gap[:, d, j, i], pb[:, 64 + 8 * n:72 + 8 * n], ACT.Exp)
                    last.then_inc(sums_copied, 1)

                @block.tensor
                def _(pe):
                    for n in range(LT):
                        if n >= 2:
                            pe.wait_ge(x_copied, n - 1)
                        for m in range(4):
                            mm = pe.transpose(pt[:, n % 2, m], conv[:, m, n * P:(n + 1) * P], K["ident"])
                        mm.then_inc(turned, 1)
                    for n in range(2 * LT):
                        if n >= 2:
                            pe.wait_ge(scores_copied, n - 1)
                        g, j = n // LT, n % LT
                        pe.matmul(psc[:, n % 2], conv[:, 4 + g, j * P:(j + 1) * P], conv[:, 6 + g],
                                  start=True, stop=True).then_inc(scores_ready, 1)
                    pe.wait_ge(rows_ready, 1)
                    for n in range(LT):
                        mm = pe.transpose(pc[:, n, 0:64], rows[:, n * P:(n + 1) * P], K["ident"][0:64, 0:64])
                    mm.then_inc(cols_turned, 1)
                    pe.wait_ge(cols_copied, 1)
                    for j in range(LT):
                        pe.matmul(pb[:, 16 * j:16 * j + 8], K["le"], cols[:, j, 1, 0:8], start=True, stop=True)
                        pe.matmul(pb[:, 16 * j + 8:16 * j + 16], K["ge"], cols[:, j, 1, 8:16], start=True, stop=True)
                    for n, (d, j, i) in enumerate(PAIRS):
                        between = list(range(j + 1, i)) if d == 0 else list(range(i + 1, j))
                        o = pb[:, 64 + 8 * n:72 + 8 * n]
                        mm = pe.matmul(o, K["gt"] if d == 0 else K["lt"], cols[:, j, 1, 8 * d:8 * d + 8],
                                       start=True, stop=not between)
                        for m in between:
                            mm = pe.matmul(o, K["ones"], cols[:, m, 1, 8 * d:8 * d + 8], start=False,
                                           stop=m == between[-1])
                    mm.then_inc(sums_ready, 1)

        W = sb("weights_st", [P, 2, LT, SEQ])
        E = sb("decay_t", [P, 2, 2, SEQ])
        Dg = sb("decay_diag", [P, 2, 2, LT, P])
        pe_ps = ctx.enter_context(nc.psum_tensor(unique("decay_ps"), [P, 2, 2, 512], F32))
        py = ctx.enter_context(nc.psum_tensor(unique("y_ps"), [P, 2, 512], F32))
        with stage(nc, "sums_ready", "decays_ready", "diag_ready", "exp_done", "diag_exp", "weights_ready", "y_ready", "y_copied", "dve_step") as (
                block, sums_ready, decays_ready, diag_ready, exp_done, diag_exp, weights_ready, y_ready, y_copied, dve_step):
            @block.tensor
            def _(pe):
                def decays(h):
                    if h >= 2:
                        pe.wait_ge(diag_ready, h - 1)
                        pe.wait_ge(decays_ready, h - 1)
                    for d in range(2):
                        for i in range(LT):
                            a = cols[:, i, 1, 8 * d + h:8 * d + h + 1].broadcast_to([P, P])
                            mm = pe.matmul(pe_ps[:, h % 2, d, i * P:(i + 1) * P], a,
                                           K["le"] if d == 0 else K["ge"], start=True, stop=True)
                    mm.then_inc(sums_ready, 1)
                decays(0)
                decays(1)
                for h in range(8):
                    if h + 2 < 8:
                        decays(h + 2)
                    pe.wait_ge(weights_ready, h + 1)
                    if h >= 2:
                        pe.wait_ge(y_copied, h - 1)
                    r = 64 * (h % 2)
                    for j in range(LT):
                        mm = pe.matmul(py[r:r + 64, h % 2], xt[:, j, 64 * h:64 * h + 64], W[:, h % 2, j],
                                       start=j == 0, stop=j == LT - 1)
                    mm.then_inc(y_ready, 1)

            @block.scalar
            def _(act):
                def exps(h):
                    act.wait_ge(sums_ready, h + 1)
                    if h >= 2:
                        act.wait_ge(weights_ready, h - 1)
                    act.activation(E[:, h % 2], pe_ps[:, h % 2], ACT.Exp).then_inc(decays_ready, 1)
                exps(0)
                for h in range(8):
                    act.wait_ge(diag_ready, h + 1)
                    for d in range(2):
                        for j in range(LT):
                            act.activation(Dg[:, h % 2, d, j], Dg[:, h % 2, d, j], ACT.Exp,
                                           bias=csl[:, j, 8 * d + h:8 * d + h + 1]).then_inc(exp_done, 1)
                    for d in range(2):
                        for j in range(LT):
                            act.wait_ge(exp_done, 2 * LT * h + LT * d + j + 1)
                            last = act.activation(Dg[:, h % 2, d, j], Dg[:, h % 2, d, j], ACT.Copy,
                                                  scale=cols[:, j, 0, 8 * d + h:8 * d + h + 1])
                    last.then_inc(diag_exp, 1)
                    if h + 1 < 8:
                        exps(h + 1)

            def skip(dve, h):
                r, n = 64 * (h % 2), h // 2
                dve.wait_ge(y_ready, h + 1)
                dve.scalar_tensor_tensor(mixed[r:r + 64, n], conv[r:r + 64, n],
                                         c("d_skip", layer)[r:r + 64, n:n + 1], py[r:r + 64, h % 2],
                                         ALU.mult, ALU.add).then_inc(y_copied, 1)

            @block.vector
            def _(dve):
                chain = Chain(dve, dve_step)

                def diag(h):
                    dve.wait_ge(decays_ready, h + 1)
                    mask = K["masks"].unsqueeze(2).broadcast_to([P, 2, LT, P])
                    dve.tensor_tensor(Dg[:, h % 2], pe_ps[:, h % 2].rearrange("p d (j t) -> p d j t", j=LT), mask,
                                      ALU.add).then_inc(diag_ready, 1)
                diag(0)
                for h in range(8):
                    g = h // 4
                    w = W[:, h % 2]
                    dg = Dg[:, h % 2]
                    if h >= 2:
                        dve.wait_ge(y_ready, h - 1)
                    for d, j, i in PAIRS:
                        dve.scalar_tensor_tensor(w[:, j, i * P:(i + 1) * P], E[:, h % 2, d, i * P:(i + 1) * P],
                                                 gap[:, d, j, i, h:h + 1], sc[:, g, j, i * P:(i + 1) * P],
                                                 ALU.mult, ALU.mult)
                    if h + 1 < 8:
                        diag(h + 1)
                    dve.wait_ge(diag_exp, h + 1)
                    chain.step(dve.tensor_tensor(dg[:, 0], dg[:, 0], dg[:, 1], ALU.add))
                    for j in range(LT):
                        last = dve.tensor_tensor(w[:, j, j * P:(j + 1) * P], dg[:, 0, j],
                                                 sc[:, g, j, j * P:(j + 1) * P], ALU.mult)
                    last.then_inc(weights_ready, 1)
                    if h:
                        skip(dve, h - 1)
                skip(dve, 7)
                dve.wait_ge(y_copied, 8)
                for n in range(4):
                    dve.tensor_tensor(mixed[:, n], mixed[:, n], proj[:, Z_T + n], ALU.mult)


def gated_up(nc, K, R, key, f0, rhs, hid, segs, conv=None, M=None):
    hid_hi, hid_lo = hid
    a0, total = segs[0][0], sum(w for _, w in segs)
    whole = slice(0, total)
    with ExitStack() as ctx:
        gs = ctx.enter_context(nc.sbuf_tensor(unique("gate"), [P, total], F32))
        ht = ctx.enter_context(nc.sbuf_tensor(unique("hidden"), [P, total], F32))
        raw = acc = None
        if conv:
            raw = ctx.enter_context(nc.sbuf_tensor(unique("gate_raw"), [P, PADDED], F32))
            acc = ctx.enter_context(nc.sbuf_tensor(unique("gate_conv"), [P, PADDED], F32))
        ps = ctx.enter_context(nc.psum_tensor(unique("gate_up"), [P, 2, 2, 512], F32))
        R.begin(key)
        with stage(nc, "next_hi", "hi_ready", "split", "product_ready", "raw_ready", "conv_step", "conv_ready",
                   "gate_ready", "hidden_ready", "hidden_hi", "hidden_split", "pads_zero",
                   "ada_even", "ada_odd", "ada_summed", "ada_free") as (
                block, next_hi, hi_ready, split, product_ready, raw_ready, conv_step, conv_ready,
                gate_ready, hidden_ready, hidden_hi, hidden_split, pads_zero,
                ada_even, ada_odd, ada_summed, ada_free):
            gate_read = raw_ready if conv else gate_ready
            ada = (ada_even, ada_odd)

            @block.sync
            def _(sp):
                R.load(sp, split, M and (lambda j, i: M.load(sp, j, i, ada, ada_free)))

            @block.tensor
            def _(pe):
                def tile(j, i, more):
                    pe.wait_ge(split, 2 * i + j + 1)
                    if later(i):
                        pe.wait_ge(hidden_ready if j else gate_read, i)
                    R.products(pe, j, [ps[:, j, n, 0:w] for n, (_, w) in enumerate(segs)],
                               rhs).then_inc(product_ready, 1)
                in_pairs(pe, 2 * HALF, tile)

            pseg = PSEG if len(segs) == 2 else PSEG[1:]
            lo = pseg[0][0]
            span = pseg[-1][0] + pseg[-1][1] - lo

            @block.scalar
            def _(act):
                for j in range(2):
                    R.high(act, j, 0, hi_ready, product_ready)
                if conv:
                    act.wait_ge(pads_zero, 1)

                def silu(i):
                    if later(i):
                        act.wait_ge(hidden_ready, i)
                    for n, (a, w) in enumerate(segs):
                        p0 = pseg[n][0]
                        src = acc[:, p0:p0 + w] if conv else ps[:, 0, n, 0:w]
                        last = act.activation(gs[:, a - a0:a - a0 + w], src, ACT.Silu)
                    last.then_inc(gate_ready, 1)

                def tile(j, i, more):
                    if R.last(j, i, more):
                        R.next_high(act, next_hi, product_ready)
                    if j == 0:
                        act.wait_ge(product_ready, 2 * i + 1)
                        if conv:
                            if later(i):
                                act.wait_ge(conv_ready, i)
                            for n, (_, w) in enumerate(segs):
                                p0 = pseg[n][0]
                                last = act.activation(raw[:, p0:p0 + w], ps[:, 0, n, 0:w], ACT.Copy)
                            last.then_inc(raw_ready, 1)
                        else:
                            silu(i)
                        if more:
                            R.high(act, 0, i + 1, hi_ready, product_ready)
                        if conv:
                            act.wait_ge(conv_ready, i + 1)
                            silu(i)
                    else:
                        if more:
                            R.high(act, 1, i + 1, hi_ready, product_ready)
                        act.wait_ge(hidden_ready, i + 1)
                        act.activation(hid_hi[:, i, whole], ht[:, whole], ACT.Copy).then_inc(hidden_hi, 1)
                in_pairs(act, 2 * HALF, tile)

            @block.vector
            def _(dve):
                if M:
                    M.free_slots(dve, ada_free)
                if conv:
                    taps = conv[0].rearrange("p (n w) -> p n w", w=3)
                    bias = conv[1].rearrange("p (n w) -> p n w", w=1)
                    dve.memset(raw[:], 0.0).then_inc(pads_zero, 1)
                for j in range(2):
                    R.rest(dve, j, 0, hi_ready, split)

                def tile(j, i, more):
                    if R.last(j, i, more):
                        R.next_rest(dve, next_hi)
                    if j == 0:
                        if conv:
                            dve.wait_ge(raw_ready, i + 1)
                            if later(i):
                                dve.wait_ge(gate_ready, i)
                            f = f0 + i
                            o = acc[:, lo:lo + span]
                            dve.tensor_scalar(o, raw[:, lo:lo + span], taps[:, f, 1:2], bias[:, f, 0:1],
                                              ALU.mult, ALU.add).then_inc(conv_step, 1)
                            dve.wait_ge(conv_step, 2 * i + 1)
                            dve.scalar_tensor_tensor(o, raw[:, lo - 1:lo - 1 + span], taps[:, f, 0:1], o,
                                                     ALU.mult, ALU.add).then_inc(conv_step, 1)
                            dve.wait_ge(conv_step, 2 * i + 2)
                            dve.scalar_tensor_tensor(o, raw[:, lo + 1:lo + 1 + span], taps[:, f, 2:3], o,
                                                     ALU.mult, ALU.add).then_inc(conv_ready, 1)
                        if more:
                            R.rest(dve, 0, i + 1, hi_ready, split)
                    else:
                        dve.wait_ge(gate_ready, i + 1)
                        dve.wait_ge(product_ready, 2 * i + 2)
                        if later(i):
                            dve.wait_ge(hidden_split, i)
                        for n, (a, w) in enumerate(segs):
                            last = dve.tensor_tensor(ht[:, a - a0:a - a0 + w], gs[:, a - a0:a - a0 + w], ps[:, 1, n, 0:w], ALU.mult)
                        last.then_inc(hidden_ready, 1)
                        if more:
                            R.rest(dve, 1, i + 1, hi_ready, split)
                        dve.wait_ge(hidden_hi, i + 1)
                        dve.tensor_tensor(hid_lo[:, i, whole], ht[:, whole], hid_hi[:, i, whole].bitcast(F32),
                                          ALU.subtract).then_inc(hidden_split, 1)
                    if M:
                        M.compute(dve, j, i, ada, ada_summed, ada_free)
                in_pairs(dve, 2 * HALF, tile)
        if M:
            M.at += 2 * HALF


def feed_forward(nc, K, R, name, X, H, segs, conv=None, gate=None, M=None):
    a0, total = segs[0][0], sum(w for _, w in segs)
    own = [(a - a0, w) for a, w in segs]
    for half in range(2):
        with split_pair(nc, "hidden", HALF, total) as hid:
            gated_up(nc, K, R, f"up{name}{half}", half * HALF, operand(H, segs), hid, segs, conv, M)
            project_residual(nc, R, f"down{name}{half}", operand(hid, own), X, segs, gate,
                             M if M and M.w.shape[0] - M.at == 4 * 2 * HALF - 2 * HALF + 8 else None,
                             sums=K["squares"] if half else None)


def first_block(nc, K, R, M, c, X):
    segs = SEGS[1:]
    for layer in range(2):
        with ExitStack() as mx:
            def sb(name, shape):
                return mx.enter_context(nc.sbuf_tensor(unique(name), shape, F32))

            proj = sb("proj", [P, DT_T + 1, SEQ])
            conv = sb("conv", [P, 8, SEQ])
            dt_rows = sb("dt_raw", [16, SEQ])
            with split_pair(nc, "normed", KT) as H:
                norm_split(nc, K, token_tiles(X, segs), H, 0, segs, KT, D,
                           lambda k, n: c("norm_mix_w", layer)[:, k:k + 1],
                           sums=K["squares"] if layer else None)
                mix_projection(nc, K, R, c, layer, operand(H, segs), proj, conv, dt_rows[:])
            mixed = sb("ssd_out", [P, 4, SEQ])
            own = [(0, SEQ)]
            ssd(nc, K, c, layer, proj, conv, dt_rows[:], mixed)
            H = mx.enter_context(split_pair(nc, "mixed", KT, SEQ))
            for g in range(2):
                norm_split(nc, K, lambda k, n=None: mixed[:, 2 * g + k], H, 4 + 2 * g, own, 2, 2 * P,
                           lambda k, n: c("ssd_norm_w", layer)[:, 2 * g + k:2 * g + k + 1])
            tiles = [(proj[:, Q_T + n], c("q_norm_w", layer)) for n in range(4)]
            head_norm_rope(nc, K, tiles + [(proj[:, K_T], c("k_norm_w", layer))])
            vt = sb("v_tokens", [P, LT, P])
            turn_tiles(nc, K, [([proj[:, V_T, t * P:(t + 1) * P] for t in range(LT)], vt[:])])

            def parts(h, q0):
                r = 64 * (h % 2)
                return [(proj[r:r + 64, Q_T + h // 2, q0:q0 + P],
                         lambda a, w: proj[r:r + 64, K_T, a:a + w])]
            attention(nc, K, 8, SEQ, 64 ** -0.5, parts,
                      lambda h, t: vt[:, t, 64 * (h % 2):64 * (h % 2) + 64], 64,
                      lambda h: [x[64 * (h % 2):64 * (h % 2) + 64, h // 2] for x in H])
            project_residual(nc, R, f"out{layer}", operand(H, own), X, segs, sums=K["squares"])
        with split_pair(nc, "normed", KT) as H:
            norm_split(nc, K, token_tiles(X, segs), H, 0, segs, KT, D,
                       lambda k, n: c("norm_ffn_w", layer)[:, k:k + 1], sums=K["squares"])
            feed_forward(nc, K, R, f"{layer}", X, H, segs, M=M)
    rms_norm(nc, K, token_tiles(X, segs), segs, KT, D, lambda k, n: c("final_norm_w")[:, k:k + 1],
             K["squares"][:, LAT])


def copy_tiles(nc, pairs):
    with stage(nc, "copied") as (block, copied):
        @block.vector
        def _(dve):
            for dst, src in pairs:
                dve.tensor_copy(dst, src)



HY_T, OG_T, MQ_T, MK_T, MV_T = 0, 12, 16, 20, 24


def finish_modulation(nc, c, raw, gains):
    with stage(nc, "step") as (block, step):
        @block.vector
        def _(dve):
            chain = Chain(dve, step)
            for layer in range(2):
                mod = raw[:, layer * 6 * KT:(layer + 1) * 6 * KT]
                for v in range(2):
                    chain.step(dve.tensor_tensor(mod[:, :, v], mod[:, :, v], c("ada_b", layer), ALU.add))
                for s, name in ((1, "norm_mix2"), (4, "norm_ffn2")):
                    for v in range(2):
                        o = gains[layer][:, s // 4, :, v]
                        chain.step(dve.tensor_scalar(o, mod[:, s * KT:s * KT + KT, v], 1.0, None, ALU.add))
                        chain.step(dve.tensor_tensor(o, o, c(name, layer), ALU.mult))


def in2_projection(nc, K, R, c, rhs, og, hy, qk, vg):
    taps = c("conv2_w").rearrange("p (n w) -> p n w", w=3)
    bias = c("conv2_b").rearrange("p (n w) -> p n w", w=1)
    project_conv(nc, R, "hy", rhs, hy, SEGS, PSEG, PADDED, taps[:, 0:12], bias[:, 0:12], ACT.Copy)
    project_plain(nc, R, "og", rhs, og, SEGS, ACT.Sigmoid)
    project_conv(nc, R, "qk", rhs, qk, SEGS, PSEG, PADDED, taps[:, 12:20], bias[:, 12:20], ACT.Silu)

    def after(act):
        act.activation(vg[:, 4], vg[:, 4], ACT.Identity, bias=c("gate_b"))
    project_plain(nc, R, "vg", rhs, vg, SEGS, after=after)


def gate_sums(nc, K, G, rows, acol, emcol, t, one):
    with ExitStack() as ctx:
        ps = ctx.enter_context(nc.psum_tensor(unique("col_ps"), [P, 2, 8, 64], F32))
        with stage(nc, "dve_step", "abs_ready", "log_ready", "cols_turned", "rows_ready", "act_step") as (
                block, dve_step, abs_ready, log_ready, cols_turned, rows_ready, act_step):
            b, a, M, em = (rows[:, n] for n in range(4))

            @block.vector
            def _(dve):
                chain = Chain(dve, dve_step)
                chain.step(dve.memset(one, 1.0))
                chain.step(dve.tensor_copy(t[:, 0], G[64:128]))
                chain.step(dve.scalar_tensor_tensor(t[:, 1], t[:, 0], -1.0, t[:, 0], ALU.mult, ALU.max))
                dve.nop().then_inc(abs_ready, 1)
                dve.wait_ge(log_ready, 1)
                chain.step(dve.scalar_tensor_tensor(t[:, 0], t[:, 0], 0.0, t[:, 1], ALU.min, ALU.subtract))

                def scans(out, d0, d1, op0, op1):
                    chain.step(dve.tensor_tensor_scan(out[0:32], d0[0:32], d1[0:32], 0.0, op0, op1))
                    chain.step(dve.tensor_tensor_scan(out[32:64, CTX - 1::-1], d0[32:64, CTX - 1::-1],
                                                      d1[32:64, CTX - 1::-1], 0.0, op0, op1))
                    chain.step(dve.tensor_tensor_scan(out[32:64, TOK - 1:CTX - 1:-1],
                                                      d0[32:64, TOK - 1:CTX - 1:-1],
                                                      d1[32:64, TOK - 1:CTX - 1:-1], out[32:64, 0:1], op0, op1))
                scans(b, one, t[:, 0], ALU.mult, ALU.add)
                chain.step(dve.tensor_tensor(a, G[0:64], b, ALU.subtract))
                scans(M, a, a, ALU.max, ALU.max)
                chain.step(dve.tensor_tensor(em, M, b, ALU.add))
                chain.step(dve.tensor_scalar(M, M, -1.0, None, ALU.mult))
                dve.nop().then_inc(rows_ready, 1)
                dve.wait_ge(cols_turned, 1)
                dve.tensor_copy(acol[:], ps[:, 0, 0:6])

            @block.scalar
            def _(act):
                chain = Chain(act, act_step)
                act.wait_ge(abs_ready, 1)
                chain.step(act.activation(t[:, 1], t[:, 1], ACT.Exp, scale=-1.0))
                act.activation(t[:, 1], t[:, 1], ACT.Ln, bias=1.0).then_inc(log_ready, 1)
                act.wait_ge(cols_turned, 1)
                act.activation(emcol[:], ps[:, 1, 0:6], ACT.Exp, scale=-1.0)

            @block.tensor
            def _(pe):
                pe.wait_ge(rows_ready, 1)
                for m, x in enumerate((a, em)):
                    for n in range(6):
                        mm = pe.transpose(ps[:, m, n], x[:, n * P:(n + 1) * P], K["ident"][0:64, 0:64])
                mm.then_inc(cols_turned, 1)


def mlstm(nc, K, c, qk, og, mixed):
    with ExitStack() as ctx:
        def sb(name, shape):
            return ctx.enter_context(nc.sbuf_tensor(unique(name), shape, F32))
        rows = sb("gate_rows", [64, 4, TOK])
        acol = sb("a_cols", [P, 6, 64])
        emcol = sb("bound_cols", [P, 6, 64])
        Pw = sb("weights_st", [P, 2, TOK])
        Dc = sb("decays", [P, 2, TOK])
        gate_sums(nc, K, mixed[:, 4], rows, acol, emcol, Pw[0:64], Dc[0:64, 0])
        S = sb("scores", [P, 6, TOK])
        vt = sb("v_tokens", [P, 6, 4, P + 1])
        exponents = sb("diagonal_exponents", [P, 2, P])
        part = sb("backward_part", [P, 2, 3, P])
        dn = sb("denominators", [P, 2, 3, 1])
        turn_tiles(nc, K, [([mixed[:, h, t * P:(t + 1) * P] for h in range(4)], vt[:, t, :, 0:P]) for t in range(6)])
        Mb = mixed[:, 0:2]
        tokens = lambda h: mixed[:, 4 + h].rearrange("p (b i c) -> p b i c", b=2, i=3)

        def tiles(d, j):
            if d == 0:
                return list(range(j, 6))
            return list(range(0, j + 1)) + list(range(2, 6)) if j < 2 else list(range(2, j + 1))

        def spans(d, j, diagonal=True):
            out = []
            for i in tiles(d, j):
                if i == j and not diagonal:
                    continue
                if out and out[-1][0] + out[-1][1] == i * P:
                    out[-1] = (out[-1][0], out[-1][1] + P)
                else:
                    out.append((i * P, P))
            return out
        ORDER = ((0, 1, 2, 3, 4, 5), (1, 0, 5, 4, 3, 2))
        RUNS = [(h, d) for h in range(4) for d in range(2)]
        STEPS = [(h, d, j) for h, d in RUNS for j in ORDER[d]]
        SCORES = [(h, j, seg) for h in range(4) for j in ORDER[1] for seg in ((0, 1) if j < 2 else (1,))]
        PER_HEAD = len(SCORES) // 4
        with ExitStack() as c2:
            psb = c2.enter_context(nc.psum_tensor(unique("row_ps"), [P, 2, 512], F32))
            pss = c2.enter_context(nc.psum_tensor(unique("score_ps"), [P, 2, 512], F32))
            po = c2.enter_context(nc.psum_tensor(unique("sum_ps"), [P, 2, 2, 512], F32))
            sums = lambda n: po[:, n % 2, :, 0:3 * (P + 1)].rearrange("p b (i c) -> p b i c", i=3)
            with stage(nc, "rows_spread", "rows_copied", "scores_ready", "scores_copied", "masked", "decays_ready",
                       "weights_ready", "weights_used", "out_done", "dve_step") as (
                    block, rows_spread, rows_copied, scores_ready, scores_copied, masked, decays_ready,
                    weights_ready, weights_used, out_done, dve_step):

                @block.tensor
                def _(pe):
                    def spread(n):
                        h, d = RUNS[n]
                        if n:
                            pe.wait_ge(rows_copied, n)
                        sel = K["ident"][0:64, 32 * d + h:32 * d + h + 1].broadcast_to([64, P])
                        for seg, (a, w) in enumerate(SEGS):
                            mm = pe.matmul(psb[:, seg, 0:w], sel, rows[:, 2, a:a + w], start=True, stop=True)
                        mm.then_inc(rows_spread, 1)

                    def scores(h, tile):
                        for n in range(PER_HEAD * h, PER_HEAD * (h + 1)):
                            _, j, seg = SCORES[n]
                            if j != tile:
                                continue
                            if n >= 2:
                                pe.wait_ge(scores_copied, n - 1)
                            a, w = SEGS[seg]
                            pe.matmul(pss[:, n % 2, 0:w], qk[:, 4 + h, j * P:(j + 1) * P], qk[:, h, a:a + w],
                                      start=True, stop=True).then_inc(scores_ready, 1)
                    spread(0)
                    for j in ORDER[1]:
                        scores(0, j)
                    for n, (h, d) in enumerate(RUNS):
                        if n >= 2:
                            pe.wait_ge(out_done, n - 1)
                        touches = [[(m, i) for m, j in enumerate(ORDER[d]) for i in tiles(d, j) if i // 3 == b]
                                   for b in range(2)]
                        for m, j in enumerate(ORDER[d]):
                            if d == 1 and h < 3:
                                scores(h + 1, j)
                            if m == 2 and n + 1 < 8:
                                spread(n + 1)
                            pe.wait_ge(weights_ready, 6 * n + m + 1)
                            for i in tiles(d, j):
                                mm = pe.matmul(sums(n)[:, i // 3, i % 3], Pw[:, m % 2, i * P:(i + 1) * P],
                                               vt[:, j, h], start=(m, i) == touches[i // 3][0],
                                               stop=(m, i) == touches[i // 3][-1])
                            mm.then_inc(weights_used, 1)

                @block.scalar
                def _(act):
                    def copy_rows(n):
                        act.wait_ge(rows_spread, n + 1)
                        if n >= 2:
                            act.wait_ge(weights_ready, 6 * (n - 1))
                        for seg, (a, w) in enumerate(SEGS):
                            last = act.activation(Mb[:, n % 2, a:a + w], psb[:, seg, 0:w], ACT.Copy)
                        last.then_inc(rows_copied, 1)
                        act.wait_ge(rows_copied, n + 1)

                    def copy_scores(h, tile):
                        for n in range(PER_HEAD * h, PER_HEAD * (h + 1)):
                            _, j, seg = SCORES[n]
                            if j != tile:
                                continue
                            act.wait_ge(scores_ready, n + 1)
                            if h:
                                act.wait_ge(weights_ready, 6 * (2 * h - 1) + ORDER[1].index(j) + 1)
                            a, w = SEGS[seg]
                            act.activation(S[:, j, a:a + w], pss[:, n % 2, 0:w], ACT.Copy,
                                           scale=P ** -0.5).then_inc(scores_copied, 1)
                    copy_rows(0)
                    for j in ORDER[1]:
                        copy_scores(0, j)
                    for n, (h, d) in enumerate(RUNS):
                        for m, j in enumerate(ORDER[d]):
                            q = 6 * n + m
                            if q >= 2:
                                act.wait_ge(weights_ready, q - 1)
                            r = 32 * d + h
                            for a, w in spans(d, j, diagonal=False):
                                act.activation(Dc[:, m % 2, a:a + w], Mb[:, n % 2, a:a + w], ACT.Exp,
                                               bias=acol[:, j, r:r + 1])
                            act.wait_ge(masked, q + 1)
                            act.activation(Dc[:, m % 2, j * P:(j + 1) * P], exponents[:, q % 2],
                                           ACT.Exp).then_inc(decays_ready, 1)
                            if m == 3 and n + 1 < 8:
                                copy_rows(n + 1)
                            if d == 1 and h < 3 and m:
                                copy_scores(h + 1, ORDER[1][m - 1])
                        if d == 1 and h < 3:
                            copy_scores(h + 1, ORDER[1][5])

                @block.vector
                def _(dve):
                    chain = Chain(dve, dve_step)
                    chain.step(dve.memset(vt[:, :, :, P:P + 1], 1.0))

                    def mask(q):
                        h, d, j = STEPS[q]
                        n = q // 6
                        r = 32 * d + h
                        dve.wait_ge(rows_copied, n + 1)
                        if q >= 2:
                            dve.wait_ge(decays_ready, q - 1)
                        dve.scalar_tensor_tensor(exponents[:, q % 2], Mb[:, n % 2, j * P:(j + 1) * P],
                                                 acol[:, j, r:r + 1], K["mask_f"] if d == 0 else K["mask_b"],
                                                 ALU.add, ALU.add).then_inc(masked, 1)

                    def quotient(n):
                        h, d = RUNS[n]
                        dve.wait_ge(weights_used, 6 * n + 6)
                        r = 32 * d + h
                        num, den = sums(n)[:, :, :, 0:P], sums(n)[:, :, :, P:P + 1]
                        bound = emcol[:, :, r:r + 1].rearrange("p (b i) c -> p b i c", b=2)
                        chain.step(dve.tensor_copy(dn[:], den))
                        chain.step(dve.scalar_tensor_tensor(dn[:], dn[:], -1.0, dn[:], ALU.mult, ALU.max))
                        chain.step(dve.tensor_tensor(dn[:], dn[:], bound, ALU.max))
                        chain.step(dve.reciprocal(dn[:], dn[:]))
                        dve.tensor_tensor(part[:] if d else tokens(h), num, dn[:].broadcast_to([P, 2, 3, P]),
                                          ALU.mult).then_inc(out_done, 1)
                        if d:
                            dve.wait_ge(out_done, n + 1)
                            chain.step(dve.tensor_tensor(tokens(h), tokens(h), part[:], ALU.add))
                    mask(0)
                    for n, (h, d) in enumerate(RUNS):
                        if d == 0:
                            dve.wait_ge(scores_copied, PER_HEAD * (h + 1))
                        for m, j in enumerate(ORDER[d]):
                            q = 6 * n + m
                            if q + 1 < 48:
                                mask(q + 1)
                            dve.wait_ge(decays_ready, q + 1)
                            if q >= 2:
                                dve.wait_ge(weights_used, q - 1)
                            for a, w in spans(d, j):
                                last = dve.tensor_tensor(Pw[:, m % 2, a:a + w], Dc[:, m % 2, a:a + w],
                                                         S[:, j, a:a + w], ALU.mult)
                            last.then_inc(weights_ready, 1)
                            if m == 1 and n:
                                quotient(n - 1)
                    quotient(7)

        sq = sb("mean_squares", [P, 4, 6])
        with ExitStack() as c2:
            pt = c2.enter_context(nc.psum_tensor(unique("turn_ps"), [P, 2, 2, 512], F32))
            with stage(nc, "squared", "summed", "root_ready", "inverted", "normed", "turned", "gated") as (
                    block, squared, summed, root_ready, inverted, normed, turned, gated):
                @block.scalar
                def _(act):
                    for h in range(4):
                        act.activation(mixed[:, h], mixed[:, 4 + h], ACT.Square).then_inc(squared, 1)
                    act.wait_ge(summed, 4)
                    act.activation(sq[:], sq[:], ACT.Sqrt, scale=1.0 / P, bias=K["eps"]).then_inc(root_ready, 1)

                @block.vector
                def _(dve):
                    for h in range(4):
                        dve.wait_ge(squared, h + 1)
                        dve.tensor_reduce(sq[:, h], mixed[:, h].rearrange("p (i c) -> p i c", i=6), AX.X,
                                          ALU.add).then_inc(summed, 1)
                    dve.wait_ge(root_ready, 1)
                    dve.reciprocal(sq[:], sq[:]).then_inc(inverted, 1)
                    dve.wait_ge(inverted, 1)
                    for h in range(4):
                        x = mixed[:, 4 + h].rearrange("p (i c) -> p i c", i=6)
                        dve.tensor_tensor(x, x, sq[:, h].unsqueeze(2).broadcast_to([P, 6, P]),
                                          ALU.mult).then_inc(normed, 1)
                    for h in range(4):
                        dve.wait_ge(turned, h + 1)
                        dve.scalar_tensor_tensor(mixed[:, 4 + h].rearrange("p (b t) -> p b t", b=2),
                                                 pt[:, h % 2, :, 0:3 * P], c("ml_norm")[:, h:h + 1],
                                                 og[:, h].rearrange("p (b t) -> p b t", b=2),
                                                 ALU.mult, ALU.mult).then_inc(gated, 1)

                @block.tensor
                def _(pe):
                    for h in range(4):
                        pe.wait_ge(normed, h + 1)
                        if h >= 2:
                            pe.wait_ge(gated, h - 1)
                        for i in range(6):
                            mm = pe.transpose(pt[:, h % 2, i // 3, (i % 3) * P:(i % 3 + 1) * P],
                                              mixed[:, 4 + h, i * P:(i + 1) * P], K["ident"])
                        mm.then_inc(turned, 1)


def hyena(nc, K, c, hy, dram, mixed):
    with ExitStack() as ctx:
        def sb(name, shape):
            return ctx.enter_context(nc.sbuf_tensor(unique(name), shape, F32))
        fw = sb("filter_w", [64, 2 * SEQ + 64 + 64])
        z = sb("positions", [33, TOK])
        hid = sb("filter_hidden", [64, 2, TOK])
        with ExitStack() as c2:
            t = c2.enter_context(nc.sbuf_tensor(unique("turns"), [64, 2, TOK], F32))
            ps = c2.enter_context(nc.psum_tensor(unique("hid_ps"), [64, 2, 2, 512], F32))
            with stage(nc, "arrived", "product_ready", "angle_ready", "sine_ready", "dve_step", "g_done") as (
                    block, arrived, product_ready, angle_ready, sine_ready, dve_step, g_done):
                @block.sync
                def _(sp):
                    sp.dma_start(fw[:], dram["filter_w"]).then_inc(arrived, 16)
                    sp.dma_start(z[:], dram["positions"]).then_inc(arrived, 16)

                @block.tensor
                def _(pe):
                    pe.wait_ge(arrived, 32)
                    for n in range(2):
                        if n:
                            pe.wait_ge(sine_ready, 1)
                        for seg, (a, w) in enumerate(SEGS):
                            if n == 0:
                                mm = pe.matmul(ps[:, n, seg, 0:w], fw[0:33, 0:64], z[:, a:a + w],
                                               start=True, stop=True)
                            else:
                                mm = pe.matmul(ps[:, n, seg, 0:w], fw[:, 64:128], hid[:, 0, a:a + w],
                                               start=True, stop=True)
                        mm.then_inc(product_ready, 1)

                @block.vector
                def _(dve):
                    chain = Chain(dve, dve_step)
                    for m in range(4):
                        dve.tensor_tensor(hy[:, 8 + m], hy[:, 8 + m], hy[:, 4 + m], ALU.mult)
                    MAGIC, INV = 12582912.0, float(np.float32(1 / (2 * np.pi)))
                    HI = 6.28125
                    MID = float(np.float32(2 * np.pi - HI))
                    LO = float(2 * np.pi - HI - MID)
                    for n in range(2):
                        dve.wait_ge(product_ready, n + 1)
                        u, r = t[:, 0], t[:, 1]
                        for seg, (a, w) in enumerate(SEGS):
                            chain.step(dve.tensor_scalar(u[:, a:a + w], ps[:, n, seg, 0:w],
                                                         c("filter_b")[0:64, n:n + 1],
                                                         c("filter_freq")[0:64, 0:1], ALU.add, ALU.mult))
                        chain.step(dve.tensor_scalar(r, u, INV, MAGIC, ALU.mult, ALU.add))
                        chain.step(dve.tensor_scalar(r, r, MAGIC, None, ALU.subtract))
                        for part in (HI, MID, LO):
                            chain.step(dve.scalar_tensor_tensor(u, r, -part, u, ALU.mult, ALU.add))
                        chain.step(dve.tensor_scalar(u, u, 3.1415925, -3.1415925, ALU.min, ALU.max))
                        dve.nop().then_inc(angle_ready, 1)
                        if n == 0:
                            dve.wait_ge(sine_ready, 1)

                @block.scalar
                def _(act):
                    for n in range(2):
                        act.wait_ge(angle_ready, n + 1)
                        act.activation(hid[:, n], t[:, 0], ACT.Sin).then_inc(sine_ready, 1)

        gt = sb("g_tokens", [P, LT, SEQ])
        fl = sb("filters", [P, 2, LT, SEQ])
        dc = sb("filter_decay", [P, LT, SEQ])
        F = sb("dft", [P, 2, LT, SEQ])
        Y = sb("spectrum", [P, LT, 2, SEQ])
        gs = sb("g_spectrum", [P, 2, SEQ])
        t = sb("products", [P, 4, SEQ])
        for seg, (a0, L) in enumerate(SEGS):
            lt = L // P
            turn_tiles(nc, K, [([hy[:, 8 + m, a0 + s * P:a0 + (s + 1) * P] for m in range(4)],
                                gt[:, s].rearrange("p (m q) -> p m q", m=4)) for s in range(lt)])
            with ExitStack() as c3:
                ph = c3.enter_context(nc.psum_tensor(unique("filter_ps"), [P, 2, 2, 512], F32))
                with stage(nc, "arrived", "product_ready", "shaped", "zeroed", "summed", "dve_step") as (
                        block, arrived, product_ready, shaped, zeroed, summed, dve_step):
                    @block.sync
                    def _(sp):
                        sp.dma_start(dc[:, 0:lt], dram[f"decay{seg}"]).then_inc(arrived, 16)
                        for m in range(2):
                            sp.dma_start(F[:, m, 0:lt, 0:L], dram[f"dft{seg}"][m]).then_inc(arrived, 16)
                        sp.wait_ge(arrived, 48)

                    @block.tensor
                    def _(pe):
                        for s in range(lt):
                            if s >= 2:
                                pe.wait_ge(shaped, s - 1)
                            for m in range(2):
                                mm = pe.matmul(ph[:, s % 2, m], hid[:, 1, a0 + s * P:a0 + (s + 1) * P],
                                               fw[:, 128 + m * SEQ:128 + (m + 1) * SEQ], start=True, stop=True)
                            mm.then_inc(product_ready, 1)

                    @block.vector
                    def _(dve):
                        chain = Chain(dve, dve_step)
                        dve.wait_ge(arrived, 48)
                        for s in range(lt):
                            dve.wait_ge(product_ready, s + 1)
                            chain.step(dve.tensor_tensor(t[:, 0], ph[:, s % 2, 0], dc[:, s], ALU.mult))
                            dve.tensor_tensor(t[:, 1], ph[:, s % 2, 1], dc[:, s], ALU.mult).then_inc(shaped, 1)
                            dve.wait_ge(shaped, s + 1)
                            if s == 0:
                                chain.step(dve.memset(t[0:1, 1], 0.0))
                            chain.step(dve.tensor_tensor(fl[:, 0, s], t[:, 0], t[:, 1], ALU.add))
                            chain.step(dve.tensor_tensor(fl[:, 1, s], t[:, 1], t[:, 0], ALU.subtract))
            with ExitStack() as c3:
                pf = c3.enter_context(nc.psum_tensor(unique("spec_ps"), [P, 2, 4, 512], F32))
                with stage(nc, "spectra_ready", "g_copied", "product_step", "spectrum_done") as (
                        block, spectra_ready, g_copied, product_step, spectrum_done):
                    @block.tensor
                    def _(pe):
                        for k in range(lt):
                            if k >= 2:
                                pe.wait_ge(spectrum_done, k - 1)
                            for q, (table, x) in enumerate(((0, gt), (1, gt), (0, fl[:, 0]), (1, fl[:, 1]))):
                                for s in range(lt):
                                    mm = pe.matmul(pf[:, k % 2, q], F[:, table, s, k * P:(k + 1) * P], x[:, s],
                                                   start=s == 0, stop=s == lt - 1)
                            mm.then_inc(spectra_ready, 1)

                    @block.scalar
                    def _(act):
                        for k in range(lt):
                            act.wait_ge(spectra_ready, k + 1)
                            if k:
                                act.wait_ge(spectrum_done, k)
                            act.activation(gs[:], pf[:, k % 2, 0:2], ACT.Copy).then_inc(g_copied, 1)

                    @block.vector
                    def _(dve):
                        for k in range(lt):
                            dve.wait_ge(g_copied, k + 1)
                            if k:
                                dve.wait_ge(spectrum_done, k)
                            for n, (g, f) in enumerate(((0, 2), (1, 3), (1, 2), (0, 3))):
                                dve.tensor_tensor(t[:, n], gs[:, g], pf[:, k % 2, f], ALU.mult).then_inc(product_step, 1)
                            dve.wait_ge(product_step, 4 * k + 4)
                            dve.tensor_tensor(Y[:, k, 0], t[:, 0], t[:, 1], ALU.add)
                            dve.tensor_tensor(Y[:, k, 1], t[:, 2], t[:, 3], ALU.subtract).then_inc(spectrum_done, 1)
                with stage(nc, "even_arrived", "y_ready", "y_done", "dve_step") as (block, arrived, y_ready, y_done, dve_step):
                    @block.sync
                    def _(sp):
                        for m in range(2):
                            sp.dma_start(F[:, m, 0:lt, 0:L], dram[f"idft{seg}"][m]).then_inc(arrived, 16)

                    @block.tensor
                    def _(pe):
                        pe.wait_ge(arrived, 32)
                        for m in range(4):
                            for k in range(lt):
                                for q in range(2):
                                    mm = pe.matmul(pf[:, 0, m, 0:L], Y[:, k, q, m * P:(m + 1) * P], F[:, q, k, 0:L],
                                                   start=k == 0 and q == 0, stop=k == lt - 1 and q == 1)
                            mm.then_inc(y_ready, 1)

                    @block.vector
                    def _(dve):
                        chain = Chain(dve, dve_step)
                        for m in range(4):
                            dve.wait_ge(y_ready, m + 1)
                            o = t[:, m, 0:L]
                            chain.step(dve.scalar_tensor_tensor(o, hy[:, 8 + m, a0:a0 + L], c("hy_bias")[:, m:m + 1],
                                                                pf[:, 0, m, 0:L], ALU.mult, ALU.add))
                            dve.tensor_tensor(mixed[:, m, a0:a0 + L], o, hy[:, m, a0:a0 + L], ALU.mult)


def mla(nc, K, R, c, H, X, dram):
    with ExitStack() as ctx:
        def sb(name, shape):
            return ctx.enter_context(nc.sbuf_tensor(unique(name), shape, F32))
        q = sb("queries", [P, 12, SEQ])
        vt = sb("v_tokens", [P, 6, D])
        kr = sb("rope_keys", [P, TOK])
        kn = X
        lseg = SEGS[1:]
        with nc.sbuf_tensor(unique("latent"), [P, 6, TOK], F32) as down:
            project_plain(nc, R, "kv_a", operand(H, SEGS), down, SEGS)
            copy_tiles(nc, [(kr[:], down[:, 5])])
            part = lambda n0, segs: (lambda k, n=None: token_tiles(down, segs)(n0 + k, n))
            norm_split(nc, K, part(0, lseg), H, 0, lseg, 3, 3 * P, lambda k, n: c("mla_q_norm")[:, k:k + 1])
            norm_split(nc, K, part(3, SEGS), H, 3, SEGS, 2, 2 * P, lambda k, n: c("mla_kv_norm")[:, k:k + 1])
        project_plain_at(nc, R, "uq", operand(H, lseg), q)
        head_norm_rope(nc, K, [(q[:, 8 + n], None) for n in range(4)] + [(kr[:, LAT], None)])
        project_plain(nc, R, "uk", operand(H, SEGS, 3), kn, SEGS)
        with ExitStack() as c2:
            W = c2.enter_context(nc.sbuf_tensor(unique("w_v"), [P, 2, D], F32))
            Wh = c2.enter_context(nc.sbuf_tensor(unique("w_v_hi"), [P, 2, D], F32R))
            Wl = c2.enter_context(nc.sbuf_tensor(unique("w_v_lo"), [P, 2, D], F32R))
            ps = c2.enter_context(nc.psum_tensor(unique("v_ps"), [P, 2, 2, 512], F32))
            with stage(nc, "arrived", "hi_ready", "split", "v_ready", "v_copied") as (
                    block, arrived, hi_ready, split, v_ready, v_copied):
                @block.sync
                def _(sp):
                    sp.dma_start(W[:], dram["mla_uv"]).then_inc(arrived, 16)

                @block.vector
                def _(dve):
                    dve.wait_ge(hi_ready, 1)
                    dve.tensor_tensor(Wl[:], W[:], Wh[:].bitcast(F32), ALU.subtract).then_inc(split, 1)

                @block.tensor
                def _(pe):
                    pe.wait_ge(split, 1)
                    for t in range(6):
                        if t >= 2:
                            pe.wait_ge(v_copied, t - 1)
                        for n in range(2):
                            o = ps[:, t % 2, n]
                            for k in range(2):
                                for m, (h, w) in enumerate(((0, Wh), (0, Wl), (1, Wh))):
                                    mm = pe.matmul(o, H[h][:, 3 + k, t * P:(t + 1) * P],
                                                   w[:, k, n * 512:(n + 1) * 512], start=k == 0 and m == 0,
                                                   stop=k == 1 and m == 2)
                        mm.then_inc(v_ready, 1)

                @block.scalar
                def _(act):
                    act.wait_ge(arrived, 16)
                    act.activation(Wh[:], W[:], ACT.Copy).then_inc(hi_ready, 1)
                    for t in range(6):
                        act.wait_ge(v_ready, t + 1)
                        act.activation(vt[:, t].rearrange("p (n w) -> p n w", n=2), ps[:, t % 2],
                                       ACT.Copy).then_inc(v_copied, 1)

        def parts(h, q0):
            r = 64 * (h % 2)
            return [(q[:, h, q0:q0 + P], lambda a, w: kn[:, h, a:a + w]),
                    (q[r:r + 64, 8 + h // 2, q0:q0 + P], lambda a, w: kr[r:r + 64, a:a + w])]
        attention(nc, K, 8, TOK, 192 ** -0.5, parts, lambda h, t: vt[:, t, h * P:(h + 1) * P], P,
                  lambda h: [x[:, h, LAT] for x in H])


def project_plain_at(nc, R, key, rhs, out):
    project_plain(nc, R, key, rhs, out, [(0, SEQ)])


def second_block(nc, K, R, c, X, dram):
    raw, all_gains = dram["mod"], dram["gains"]
    finish_modulation(nc, c, raw, all_gains)
    for layer in range(2):
        segs = SEGS if layer == 0 else SEGS[1:]
        n0 = len(SEGS) - len(segs)
        m, gains = raw[:, layer * 6 * KT:(layer + 1) * 6 * KT], all_gains[layer]
        gain = lambda which, seg0=0: (lambda k, n: gains[:, which, k, 1 - n - seg0:2 - n - seg0])
        vec = lambda which, seg0=0: (lambda k, n: m[:, which * KT:which * KT + KT][:, k, 1 - n - seg0:2 - n - seg0])
        with ExitStack() as ctx:
            if layer == 0:
                with ExitStack() as hx:
                    hy = hx.enter_context(nc.sbuf_tensor(unique("hyena_in"), [P, 12, TOK], F32))
                    with ExitStack() as mx:
                        og = mx.enter_context(nc.sbuf_tensor(unique("out_gate"), [P, 4, TOK], F32))
                        qk = mx.enter_context(nc.sbuf_tensor(unique("qk"), [P, 8, TOK], F32))
                        with split_pair(nc, "normed", KT) as H:
                            norm_split(nc, K, token_tiles(X, SEGS), H, 0, SEGS, KT, D, gain(0), vec(0),
                                       keep=(dram["x_kept"], X[:]))
                            in2_projection(nc, K, R, c, operand(H, SEGS), og, hy, qk, X)
                        mlstm(nc, K, c, qk, og, X)
                    hyena(nc, K, c, hy, dram, X)
            H = ctx.enter_context(split_pair(nc, "normed", KT))
            if layer == 0:
                split_tiles(nc, [(X[:, k], H[0][:, k], H[1][:, k]) for k in range(KT)])
            else:
                norm_split(nc, K, token_tiles(X, SEGS), H, 0, SEGS, KT, D, gain(0), vec(0),
                           keep=(dram["x_kept"], X[:]), sums=K["squares"])
                mla(nc, K, R, c, H, X, dram)
            project_residual(nc, R, f"out2{layer}", operand(H, segs), X, segs, vec(2, n0), kept=dram["x_kept"],
                             sums=K["squares"])
            norm_split(nc, K, token_tiles(X, segs), H, 0, segs, KT, D, gain(1, n0), vec(3, n0),
                       sums=K["squares"])
            feed_forward(nc, K, R, f"2{layer}", X, H, segs,
                         (c("ffn_conv_w", layer), c("ffn_conv_b", layer)), vec(5, n0))



CONSTS = ["ident", "ones", "ones64", "swap", "le", "ge", "gt", "lt", "mask_f", "mask_b"]


WEIGHT_ORDER = [k for n in "01" for k in (f"in{n}a", f"in{n}b", f"out{n}", f"up{n}0", f"down{n}0", f"up{n}1", f"down{n}1")] + \
    ["hy", "og", "qk", "vg", "out20", "up200", "down200", "up201", "down201"] + \
    ["kv_a", "uq", "uk", "out21", "up210", "down210", "up211", "down211"]


def weight_tiles(ins):
    w = {"hy": ins["w_in2"][0:12], "og": ins["w_in2"][12:16], "qk": ins["w_in2"][16:24],
         "vg": ins["w_in2"][24:29], "kv_a": ins["mla_down"], "uq": ins["mla_uq"], "uk": ins["mla_uk"]}
    for n in "01":
        w[f"in{n}a"], w[f"in{n}b"] = ins[f"w_in{n}"][0:DT_T + 1], ins[f"w_in{n}"][DT_T + 1:]
        for block in ("", "2"):
            w[f"out{block}{n}"] = ins[f"w_out{block}{n}"]
            for half in range(2):
                up, down = ins[f"w_up{block}{n}"], ins[f"w_down{block}{n}"]
                w[f"up{block}{n}{half}"] = up[half * 2 * HALF:(half + 1) * 2 * HALF]
                w[f"down{block}{n}{half}"] = down[:, :, half * UNIT:(half + 1) * UNIT]
    return w


def build(nc, ins, places, out):
    K = {}
    with ExitStack() as ctx:
        def sb(name, shape):
            return ctx.enter_context(nc.sbuf_tensor(name, shape, F32))
        X = sb("x", [P, KT, TOK])
        C = sb("consts", [P, len(CONSTS), P])
        rope = sb("rope", [P, 2, SEQ])
        V = sb("vectors", list(ins["vectors"].shape))
        eps = sb("eps", [P, 1])
        K["squares"] = sb("residual_squares", [P, TOK])
        mod = sb("modulation", [P, 2 * 6 * KT, 2])
        gains = [sb(f"gains{n}", [P, 2, KT, 2]) for n in range(2)]
        for n, name in enumerate(CONSTS):
            K[name] = C[:, n]
        K["masks"] = C[:, 8:10]
        K["rope_cos"], K["rope_sin"] = rope[:, 0], rope[:, 1]
        K["eps"] = eps[:]

        def c(name, layer=None):
            a, w = places[name if layer is None else f"{name}{layer}"]
            return V[:, a:a + w]

        dram = dict(ins)
        dram["x_kept"] = nc.dram_tensor("x_kept", (P, KT, TOK), F32).ap()
        R = Weights(nc, ctx, weight_tiles(ins), WEIGHT_ORDER)
        with ExitStack() as mc:
            M = Modulation(nc, mc, ins["ada"], mod)
            with stage(nc, "arrived", "conditions_arrived") as (block, arrived, conditions_arrived):
                @block.sync
                def _(sp):
                    sp.dma_start(M.cond[:], ins["conditions"].partition_broadcast(P)).then_inc(conditions_arrived, 16)
                    sp.dma_start(X[:, :, LAT], ins["x"]).then_inc(arrived, 16)
                    sp.dma_start(X[:, :, 0:CTX], ins["ctx"]).then_inc(arrived, 16)
                    sp.dma_start(C[:], ins["consts"]).then_inc(arrived, 16)
                    sp.dma_start(rope[:], ins["rope"]).then_inc(arrived, 16)
                    sp.dma_start(V[:], ins["vectors"]).then_inc(arrived, 16)
                    sp.wait_ge(arrived, 80)

                @block.vector
                def _(dve):
                    dve.memset(eps[:], EPS)

                @block.scalar
                def _(act):
                    act.wait_ge(conditions_arrived, 16)
                    act.activation(M.cond[:], M.cond[:], ACT.Silu)
            first_block(nc, K, R, M, c, X)
        dram["mod"], dram["gains"] = mod, gains
        second_block(nc, K, R, c, X, dram)
        rms_norm(nc, K, token_tiles(X, SEGS[1:]), SEGS[1:], KT, D, lambda k, n: c("final_norm2")[:, k:k + 1],
                 K["squares"][:, LAT], out)



def tiled(w):
    k, n = w.shape
    return np.ascontiguousarray(w.reshape(k // P, P, n // P, P).transpose(2, 1, 0, 3)).reshape(n // P, P, -1)


def alternating(gate, up):
    return np.stack([tiled(gate), tiled(up)], axis=1).reshape(2 * FT, P, -1)


def on_partitions(v):
    v = v.reshape(-1, v.shape[-1])
    return v.T.reshape(-1, P, v.shape[0]).transpose(1, 0, 2).reshape(P, -1)


def padded(v):
    out = np.zeros((P,) + v.shape[1:], np.float32)
    out[:v.shape[0]] = v
    return out


def constants():
    i = np.arange(P)
    l, s = i[:, None], i[None, :]
    swap = np.zeros((P, P), np.float32)
    for m in range(P):
        if m % 32 < 16:
            swap[m + 16, m] = -1.0
        else:
            swap[m - 16, m] = 1.0
    tables = {"ident": l == s, "ones": l >= 0, "ones64": l // 64 == s // 64, "swap": swap,
              "le": l <= s, "ge": l >= s, "gt": l > s, "lt": l < s,
              "mask_f": np.where(l <= s, 0.0, NEG), "mask_b": np.where(l >= s, 0.0, NEG)}
    tables["ones"] = np.ones((P, P))
    consts = np.stack([np.asarray(tables[n], np.float32) for n in CONSTS], axis=1)
    inv = 10000.0 ** (-np.arange(0, 32, 2) / 32.0)
    t = np.arange(SEQ)
    ang = np.concatenate([np.tile(inv[:, None] * (t // 64)[None], (2, 1)),
                          np.tile(inv[:, None] * (t % 64)[None], (2, 1))])
    ang = np.tile(ang.astype(np.float32).astype(np.float64), (2, 1))
    rope = np.stack([np.cos(ang), np.sin(ang)], axis=1).astype(np.float32)
    out = {"consts": consts, "rope": rope}
    zs = []
    for seg, (_, L) in enumerate(SEGS):
        pos = np.arange(L)
        tt = (pos / (L - 1))[:, None]
        f = np.linspace(1e-4, 15, 16)
        ang = (2.0 * np.pi / L) * pos[:, None] * f[None]
        zs.append(np.concatenate([tt, np.cos(ang), -np.sin(ang)], axis=-1).T)
        deltas = np.linspace(np.log(1e-2) / 0.3, np.log(1e-2) / 1.5, 512)
        decay = np.exp(-tt * np.abs(deltas)[None]) + 0.05
        out[f"decay{seg}"] = np.ascontiguousarray(
            decay.reshape(L // P, P, 512).transpose(1, 0, 2)).astype(np.float32)
        w = np.pi * (2 * np.arange(L) + 1) / (2 * L)
        fwd = np.stack([np.cos(np.outer(pos, w)), np.sin(np.outer(pos, w))])
        inv_ = fwd.transpose(0, 2, 1) / L
        for name, m in (("dft", fwd), ("idft", inv_)):
            out[f"{name}{seg}"] = np.ascontiguousarray(
                m.reshape(2, L // P, P, L).transpose(0, 2, 1, 3)).astype(np.float32)
    out["positions"] = np.concatenate(zs, axis=1).astype(np.float32)
    return out


def lay_out(i):
    a = constants()
    vec = {}
    on = on_partitions
    feat = lambda x: np.ascontiguousarray(x.reshape(-1, KT, P).transpose(2, 1, 0))
    a["x"], a["ctx"] = feat(i["x"]), feat(i["ctx_2"])
    heads = [0, 4, 1, 5, 2, 6, 3, 7]
    for n in range(2):
        w = i["w_in"][n]
        q = w[:, :512].reshape(D, 8, 64)[:, heads].reshape(D, 512)
        steps = np.concatenate([w[:, 2304:], np.zeros((D, P - 16), np.float32)], axis=1)
        a[f"w_in{n}"] = tiled(np.concatenate([q, w[:, 512:1280], steps, w[:, 1280:2304]], axis=1))
        o = i["w_out"][n]
        a[f"w_out{n}"] = tiled(np.concatenate([o[:512].reshape(8, 64, D)[heads].reshape(512, D), o[512:]]))
        a[f"w_up{n}"] = alternating(i["w_gate"][n], i["w_up"][n])
        a[f"w_down{n}"] = tiled(i["w_down"][n])
        for name in ("norm_mix_w", "norm_ffn_w", "conv_w", "conv_b", "ssd_norm_w"):
            vec[f"{name}{n}"] = on(i[name][n])
        for name in ("q_norm_w", "k_norm_w"):
            vec[f"{name}{n}"] = on(np.tile(i[name][n], 2))
        vec[f"dt_bias{n}"] = padded(i["dt_bias"][n].reshape(16, 1))
        vec[f"a_log{n}"] = padded(i["a_log"][n].reshape(16, 1))
        vec[f"d_skip{n}"] = on(np.repeat(i["d_skip"][n], 64))
        up = i[f"ffn_up_{n}_2"]
        a[f"w_up2{n}"] = alternating(up[:, :FF], up[:, FF:])
        a[f"w_down2{n}"] = tiled(i[f"ffn_down_{n}_2"])
        vec[f"ada_b{n}"] = on(i[f"ada_b_{n}_2"])
        vec[f"norm_mix2{n}"] = on(i[f"norm_mix_{n}_2"])
        vec[f"norm_ffn2{n}"] = on(i[f"norm_ffn_{n}_2"])
        vec[f"ffn_conv_w{n}"] = on(i[f"ffn_conv_w_{n}_2"])
        vec[f"ffn_conv_b{n}"] = on(i[f"ffn_conv_b_{n}_2"])
    vec["final_norm_w"] = on(i["final_norm_w"])
    vec["final_norm2"] = on(i["final_norm_2"])
    a["conditions"] = np.stack([i["c_2"][0], i["c_ctx_2"]])
    a["ada"] = np.concatenate([i["ada_w_0_2"].T, i["ada_w_1_2"].T]).reshape(-1, P, D)
    w = i["w_in_0_2"]
    g = np.zeros((D, P), np.float32)
    gb = np.zeros((P, 1), np.float32)
    for kind, row in enumerate((0, 64, 32, 96)):
        g[:, row:row + 4] = w[:, 3584 + 4 * kind:3588 + 4 * kind]
        gb[row:row + 4, 0] = i["ml_gate_b_2"][4 * kind:4 * kind + 4]
    a["w_in2"] = tiled(np.concatenate([w[:, :1536], w[:, 3072:3584], w[:, 1536:3072], g], axis=1))
    vec["gate_b"] = gb
    no_bias = np.zeros(1024, np.float32)
    vec["conv2_w"] = np.concatenate([on(i["hy_conv_w_2"]), on(i["ml_conv_w_2"])], axis=1)
    vec["conv2_b"] = np.concatenate([on(i["hy_conv_b_2"]), on(no_bias)], axis=1)
    vec["filter_b"] = padded(np.stack([i["hy_fb1_2"], i["hy_fb2_2"]], axis=1))
    vec["filter_freq"] = padded(i["hy_freq_2"].reshape(64, 1))
    vec["hy_bias"] = on(i["hy_bias_2"])
    vec["ml_norm"] = on(i["ml_norm_g_2"])
    fw1 = np.zeros((64, 64), np.float32)
    fw1[:33] = i["hy_fw1_2"]
    a["filter_w"] = np.concatenate([fw1, i["hy_fw2_2"], i["hy_fw3_2"]], axis=1)
    a["w_out20"] = tiled(i["w_out_0_2"])
    a["w_out21"] = tiled(i["mla_w_o_2"])
    w = i["mla_w_down_2"]
    a["mla_down"] = tiled(np.concatenate([w, w[:, 640:704]], axis=1))
    u = i["mla_w_uq_2"].reshape(384, 8, 192)
    a["mla_uq"] = tiled(np.concatenate([u[:, :, :128].reshape(384, -1), u[:, :, 128:].reshape(384, -1)], axis=1))
    u = i["mla_w_ukv_2"].reshape(256, 8, 256)
    a["mla_uk"] = tiled(np.ascontiguousarray(u[:, :, :128]).reshape(256, -1))
    a["mla_uv"] = np.ascontiguousarray(u[:, :, 128:].reshape(2, P, D).transpose(1, 0, 2))
    vec["mla_q_norm"] = on(i["mla_q_norm_2"])
    vec["mla_kv_norm"] = on(i["mla_kv_norm_2"])
    places, at = {}, 0
    for name, v in vec.items():
        places[name] = (at, v.shape[1])
        at += v.shape[1]
    a["vectors"] = np.concatenate(list(vec.values()), axis=1)
    return {k: np.ascontiguousarray(v) for k, v in a.items()}, places


def kernel(**inputs):
    import concourse.bacc as bacc
    from concourse.bass_utils import run_bass_kernel_spmd

    arrays, places = lay_out({k: np.asarray(v) for k, v in inputs.items()})
    nc = bacc.Bacc("TRN2", target_bir_lowering=False, num_devices=1)
    ins = {name: nc.dram_tensor(f"in_{name}", a.shape, F32, kind="ExternalInput").ap()
           for name, a in arrays.items()}
    out = nc.dram_tensor("out", (P, KT, SEQ), F32, kind="ExternalOutput").ap()
    build(nc, ins, places, out)
    r = run_bass_kernel_spmd(nc, [{f"in_{name}": a for name, a in arrays.items()}], core_ids=[0])
    y = r.results[0]["out"]
    return np.ascontiguousarray(y.transpose(2, 1, 0)).reshape(1, -1, D)
```
